# Optimizing a Trainium2 kernel written in Bass

```python
import jax, jax.numpy as jnp
from jax import lax
import numpy as np

D_MODEL = 1024
BATCH = 1
SEQ = 2048
DEPTH = 2

GRID_W = 64
CTX_LEN = 256
N_EVEN = (DEPTH + 1) // 2
N_ODD = DEPTH // 2
EPS = 1e-6

GLA_HEADS = 4
GLA_DK = 64
GLA_DV = 128
GLA_GATE_RANK = 16
GLA_TAU = 16.0
GLA_CHUNK = 64

MLA_HEADS = 4
MLA_Q_RANK = 256
MLA_KV_RANK = 128
MLA_NOPE = 128
MLA_ROPE = 64
MLA_V = 128
ROPE_BASE = 10000.0
Q_BLOCK = 128

FOURIER_GROUPS = 4
FOURIER_GW = D_MODEL // FOURIER_GROUPS

D_FF = 2816
N_EXPERTS = 8
TOP_K = 2
D_FF_EXPERT = 3584

IN_SPLITS = (GLA_HEADS * GLA_DK, GLA_HEADS * GLA_DK, GLA_HEADS * GLA_DV, GLA_GATE_RANK, GLA_GATE_RANK,
             GLA_HEADS * GLA_DV, MLA_Q_RANK, MLA_KV_RANK, MLA_ROPE)
D_IN = (2 * GLA_HEADS * GLA_DK + 2 * GLA_HEADS * GLA_DV + 2 * GLA_GATE_RANK
        + MLA_Q_RANK + MLA_KV_RANK + MLA_ROPE)
MIX_WIDTH = GLA_HEADS * GLA_DV + MLA_HEADS * MLA_V

kernel_name = "hybrid_gla_mla_fnet_moe_dit"

def rmsnorm(x, g):
    xf = x.astype(jnp.float32)
    y = xf * lax.rsqrt(jnp.mean(xf * xf, axis=-1, keepdims=True) + EPS)
    return (y * g.astype(jnp.float32)).astype(x.dtype)

def adaln(cond, w, b):
    m = jax.nn.silu(cond) @ w + b
    return jnp.split(m, 6, axis=-1)

def modulate(h, shift, scale):
    return h * (1.0 + scale[:, None, :]) + shift[:, None, :]

def _flip(t):
    return jnp.flip(t, axis=1)

def axial_rope_tables(n_tok):
    rows = n_tok // GRID_W
    row = jnp.broadcast_to(jnp.arange(rows, dtype=jnp.float32)[:, None], (rows, GRID_W)).reshape(-1)
    col = jnp.broadcast_to(jnp.arange(GRID_W, dtype=jnp.float32)[None, :], (rows, GRID_W)).reshape(-1)
    half = MLA_ROPE // 2
    inv = 1.0 / (ROPE_BASE ** (jnp.arange(0, half, 2, dtype=jnp.float32) / half))
    ang = jnp.concatenate([row[:, None] * inv, col[:, None] * inv], axis=-1)
    return jnp.cos(ang), jnp.sin(ang)

def _rotate(u, cos, sin):
    u1, u2 = jnp.split(u, 2, axis=-1)
    return jnp.concatenate([u1 * cos - u2 * sin, u2 * cos + u1 * sin], axis=-1)

def apply_axial_rope(x, cos, sin):
    xf = x.astype(jnp.float32)
    c = cos[None, :, None, :]
    s = sin[None, :, None, :]
    nf = cos.shape[-1] // 2
    xr, xcol = jnp.split(xf, 2, axis=-1)
    out = jnp.concatenate([_rotate(xr, c[..., :nf], s[..., :nf]),
                           _rotate(xcol, c[..., nf:], s[..., nf:])], axis=-1)
    return out.astype(x.dtype)

def split_columns(p):
    out, start = [], 0
    for w in IN_SPLITS:
        out.append(p[..., start:start + w])
        start += w
    return out

def gla_inputs(q, k, v, zf, zb, w_gate_f, b_gate_f, w_gate_b, b_gate_b):
    B, L, _ = q.shape
    def heads(t, d):
        return t.astype(jnp.float32).reshape(B, L, GLA_HEADS, d)
    def log_alpha(z, w, b):
        return (jax.nn.log_sigmoid((z @ w + b).astype(jnp.float32)) / GLA_TAU).reshape(B, L, GLA_HEADS, GLA_DK)
    return (heads(q, GLA_DK) * GLA_DK ** -0.5, heads(k, GLA_DK), heads(v, GLA_DV),
            log_alpha(zf, w_gate_f, b_gate_f), log_alpha(zb, w_gate_b, b_gate_b))

def gla_states(k, v, log_a, s0):
    B, L, H, dk = k.shape
    n = L // GLA_CHUNK
    kc = k.reshape(B, n, GLA_CHUNK, H, dk)
    vc = v.reshape(B, n, GLA_CHUNK, H, -1)
    bcum = jnp.cumsum(log_a.reshape(B, n, GLA_CHUNK, H, dk), axis=2)
    b_last = bcum[:, :, -1]
    d_state = jnp.einsum('bnchk,bnchv->bnhkv', kc * jnp.exp(b_last[:, :, None] - bcum), vc)
    def step(S, inp):
        decay, ds = inp
        return decay[..., None] * S + ds, S
    s_fin, s_prev = lax.scan(step, s0, (jnp.moveaxis(jnp.exp(b_last), 1, 0), jnp.moveaxis(d_state, 1, 0)))
    return jnp.moveaxis(s_prev, 0, 1), s_fin, bcum

def gla_output(q, k, v, bcum, s_prev):
    B, L, H, dk = q.shape
    n = L // GLA_CHUNK
    qc = q.reshape(B, n, GLA_CHUNK, H, dk) * jnp.exp(bcum)
    kc = k.reshape(B, n, GLA_CHUNK, H, dk) * jnp.exp(-bcum)
    vc = v.reshape(B, n, GLA_CHUNK, H, -1)
    att = jnp.einsum('bnihk,bnjhk->bnhij', qc, kc)
    att = jnp.where(jnp.tril(jnp.ones((GLA_CHUNK, GLA_CHUNK), dtype=bool)), att, 0.0)
    o = jnp.einsum('bnhij,bnjhv->bnihv', att, vc) + jnp.einsum('bnihk,bnhkv->bnihv', qc, s_prev)
    return o.reshape(B, L, H, -1)

def gla_scan(q, k, v, log_a, s0):
    s_prev, _, bcum = gla_states(k, v, log_a, s0)
    return gla_output(q, k, v, bcum, s_prev)

def gla_finish(o, r, g):
    B, L = o.shape[:2]
    return rmsnorm(o, g).reshape(B, L, -1).astype(r.dtype) * jax.nn.silu(r)

def mla_q(cq, q_norm, w_uq):
    B, L, _ = cq.shape
    q = (rmsnorm(cq, q_norm) @ w_uq).reshape(B, L, MLA_HEADS, MLA_NOPE + MLA_ROPE)
    return q[..., :MLA_NOPE], q[..., MLA_NOPE:]

def mla_kv(ckv, kv_norm, w_ukv):
    B, L, _ = ckv.shape
    kv = (rmsnorm(ckv, kv_norm) @ w_ukv).reshape(B, L, MLA_HEADS, MLA_NOPE + MLA_V)
    return kv[..., :MLA_NOPE], kv[..., MLA_NOPE:]

def mla_attend(q_nope, q_rope, k_nope, k_rope, v):
    B, S, H, _ = q_nope.shape
    nb = S // Q_BLOCK
    scale = (MLA_NOPE + MLA_ROPE) ** -0.5
    def block(args):
        qn, qr = args
        s = jnp.einsum('bqhd,bkhd->bhqk', qn, k_nope) + jnp.einsum('bqhr,bkr->bhqk', qr, k_rope)
        p = jax.nn.softmax(s.astype(jnp.float32) * scale, axis=-1).astype(v.dtype)
        return jnp.einsum('bhqk,bkhd->bqhd', p, v)
    def to_blocks(t):
        return jnp.moveaxis(t.reshape(B, nb, Q_BLOCK, *t.shape[2:]), 1, 0)
    o = lax.map(block, (to_blocks(q_nope), to_blocks(q_rope)))
    return jnp.moveaxis(o, 0, 1).reshape(B, S, H * MLA_V)

def even_mixer(hx, hc, ctx_full, cos, sin, w_in, w_gate_f, b_gate_f, w_gate_b, b_gate_b,
               gla_norm, q_norm, w_uq, kv_norm, w_ukv, w_o):
    gq, gk, gv, gzf, gzb, gr, cq, ckv, kr = split_columns(hx @ w_in)
    cgq, cgk, cgv, cgzf, cgzb, cgr, ccq, cckv, ckr = split_columns(hc @ w_in)
    gate_w = (w_gate_f, b_gate_f, w_gate_b, b_gate_b)
    qx, kx, vx, lafx, labx = gla_inputs(gq, gk, gv, gzf, gzb, *gate_w)
    qc, kc, vc, lafc, labc = gla_inputs(cgq, cgk, cgv, cgzf, cgzb, *gate_w)
    s0 = jnp.zeros((hc.shape[0], GLA_HEADS, GLA_DK, GLA_DV), jnp.float32)
    spf, sff, bcf = gla_states(kc, vc, lafc, s0)
    spb, sfb, bcb = gla_states(_flip(kc), _flip(vc), _flip(labc), s0)
    o_x = gla_scan(qx, kx, vx, lafx, sff) + _flip(gla_scan(_flip(qx), _flip(kx), _flip(vx), _flip(labx), sfb))
    knc, vmc = mla_kv(cckv, kv_norm, w_ukv)
    knx, vmx = mla_kv(ckv, kv_norm, w_ukv)
    qnx, qrx = mla_q(cq, q_norm, w_uq)
    qrx = apply_axial_rope(qrx, cos, sin)
    krx = apply_axial_rope(kr[:, :, None, :], cos, sin)[:, :, 0, :]
    a_x = mla_attend(qnx, qrx, jnp.concatenate([knc, knx], axis=1),
                     jnp.concatenate([ckr, krx], axis=1), jnp.concatenate([vmc, vmx], axis=1))
    y_x = jnp.concatenate([gla_finish(o_x, gr, gla_norm), a_x], axis=-1) @ w_o
    if not ctx_full:
        return y_x, None
    o_c = gla_output(qc, kc, vc, bcf, spf) + _flip(gla_output(_flip(qc), _flip(kc), _flip(vc), bcb, spb))
    qnc, qrc = mla_q(ccq, q_norm, w_uq)
    a_c = mla_attend(qnc, qrc, knc, ckr, vmc)
    y_c = jnp.concatenate([gla_finish(o_c, cgr, gla_norm), a_c], axis=-1) @ w_o
    return y_x, y_c

def fourier_mix(h, w_o):
    B, L, D = h.shape
    hg = h.astype(jnp.float32).reshape(B, L, FOURIER_GROUPS, D // FOURIER_GROUPS)
    f = jnp.fft.fft2(hg, axes=(1, 3), norm="ortho").real
    return f.reshape(B, L, D).astype(h.dtype) @ w_o

def swiglu(h, w1, w3, w2):
    return (jax.nn.silu(h @ w1) * (h @ w3)) @ w2

def moe_swiglu(t, w_router, w1, w3, w2):
    logits = (t @ w_router).astype(jnp.float32)
    top_v, top_i = lax.top_k(logits, TOP_K)
    gates = jax.nn.softmax(top_v, axis=-1).astype(t.dtype)
    e_flat = top_i.reshape(-1)
    order = jnp.argsort(e_flat)
    tok = order // TOP_K
    xs = t[tok]
    sizes = jnp.bincount(e_flat, length=N_EXPERTS).astype(jnp.int32)
    h = jax.nn.silu(lax.ragged_dot(xs, w1, sizes)) * lax.ragged_dot(xs, w3, sizes)
    y = lax.ragged_dot(h, w2, sizes) * gates.reshape(-1)[order][:, None]
    return jnp.zeros_like(t).at[tok].add(y)

def setup_inputs(seed: int = 0) -> dict:
    key = jax.random.key(seed)
    ks = iter(jax.random.split(key, 40))
    f32 = jnp.float32
    D = D_MODEL
    def nrm(shape, fan_in, g=1.0):
        return (g * fan_in ** -0.5) * jax.random.normal(next(ks), shape, f32)
    def gain(shape):
        return 1.0 + 0.05 * jax.random.normal(next(ks), shape, f32)
    def bias(shape, s):
        return s * jax.random.normal(next(ks), shape, f32)
    return {
        "x": jax.random.normal(next(ks), (BATCH, SEQ, D), f32),
        "c": jax.random.normal(next(ks), (BATCH, D), f32),
        "ctx": jax.random.normal(next(ks), (BATCH, CTX_LEN, D), f32),
        "c_ctx": jax.random.normal(next(ks), (D,), f32),
        "w_mod": nrm((DEPTH, D, 6 * D), D, 0.5),
        "b_mod": bias((DEPTH, 6 * D), 0.02),
        "g_mix_pre": gain((DEPTH, D)),
        "g_mix_post": gain((DEPTH, D)),
        "g_ffn_pre": gain((DEPTH, D)),
        "g_ffn_post": gain((DEPTH, D)),
        "e_w_in": nrm((N_EVEN, D, D_IN), D),
        "e_w_gate_f": nrm((N_EVEN, GLA_GATE_RANK, GLA_HEADS * GLA_DK), GLA_GATE_RANK),
        "e_b_gate_f": bias((N_EVEN, GLA_HEADS * GLA_DK), 0.1),
        "e_w_gate_b": nrm((N_EVEN, GLA_GATE_RANK, GLA_HEADS * GLA_DK), GLA_GATE_RANK),
        "e_b_gate_b": bias((N_EVEN, GLA_HEADS * GLA_DK), 0.1),
        "e_gla_norm": gain((N_EVEN, GLA_DV)),
        "e_q_norm": gain((N_EVEN, MLA_Q_RANK)),
        "e_w_uq": nrm((N_EVEN, MLA_Q_RANK, MLA_HEADS * (MLA_NOPE + MLA_ROPE)), MLA_Q_RANK),
        "e_kv_norm": gain((N_EVEN, MLA_KV_RANK)),
        "e_w_ukv": nrm((N_EVEN, MLA_KV_RANK, MLA_HEADS * (MLA_NOPE + MLA_V)), MLA_KV_RANK),
        "e_w_o": nrm((N_EVEN, MIX_WIDTH, D), MIX_WIDTH),
        "e_w1": nrm((N_EVEN, D, D_FF), D),
        "e_w3": nrm((N_EVEN, D, D_FF), D),
        "e_w2": nrm((N_EVEN, D_FF, D), D_FF),
        "o_w_o": nrm((N_ODD, D, D), D),
        "o_w_router": nrm((N_ODD, D, N_EXPERTS), D),
        "o_w1": nrm((N_ODD, N_EXPERTS, D, D_FF_EXPERT), D),
        "o_w3": nrm((N_ODD, N_EXPERTS, D, D_FF_EXPERT), D),
        "o_w2": nrm((N_ODD, N_EXPERTS, D_FF_EXPERT, D), D_FF_EXPERT),
    }

def reference(x, c, ctx, c_ctx, w_mod, b_mod, g_mix_pre, g_mix_post, g_ffn_pre, g_ffn_post,
              e_w_in, e_w_gate_f, e_b_gate_f, e_w_gate_b, e_b_gate_b, e_gla_norm,
              e_q_norm, e_w_uq, e_kv_norm, e_w_ukv, e_w_o, e_w1, e_w3, e_w2,
              o_w_o, o_w_router, o_w1, o_w3, o_w2):
    cos, sin = axial_rope_tables(x.shape[1])
    last_read = 2 * ((DEPTH - 1) // 2)
    xc = ctx
    hc = None
    for i in range(DEPTH):
        j = i // 2
        even = (i % 2 == 0)
        ctx_live = i <= last_read
        ctx_full = i < last_read

        def channel_mixer(h):
            if even:
                return swiglu(h, e_w1[j], e_w3[j], e_w2[j])
            return lax.map(lambda t: moe_swiglu(t, o_w_router[j], o_w1[j], o_w3[j], o_w2[j]), h)

        sh_m, sc_m, ga_m, sh_f, sc_f, ga_f = adaln(c, w_mod[i], b_mod[i])
        hx = modulate(rmsnorm(x, g_mix_pre[i]), sh_m, sc_m)
        if ctx_live:
            csh_m, csc_m, cga_m, csh_f, csc_f, cga_f = adaln(c_ctx[None, :], w_mod[i], b_mod[i])
            hc = modulate(rmsnorm(xc, g_mix_pre[i]), csh_m, csc_m)
        if even:
            y, yc = even_mixer(hx, hc, ctx_full, cos, sin, e_w_in[j], e_w_gate_f[j], e_b_gate_f[j],
                               e_w_gate_b[j], e_b_gate_b[j], e_gla_norm[j], e_q_norm[j], e_w_uq[j],
                               e_kv_norm[j], e_w_ukv[j], e_w_o[j])
        else:
            y = fourier_mix(hx, o_w_o[j])
            yc = fourier_mix(hc, o_w_o[j]) if ctx_full else None
        x = x + ga_m[:, None, :] * rmsnorm(y, g_mix_post[i])
        hx = modulate(rmsnorm(x, g_ffn_pre[i]), sh_f, sc_f)
        x = x + ga_f[:, None, :] * rmsnorm(channel_mixer(hx), g_ffn_post[i])
        if ctx_full:
            xc = xc + cga_m[:, None, :] * rmsnorm(yc, g_mix_post[i])
            hcf = modulate(rmsnorm(xc, g_ffn_pre[i]), csh_f, csc_f)
            xc = xc + cga_f[:, None, :] * rmsnorm(channel_mixer(hcf), g_ffn_post[i])
    return x


_drawn_inputs = setup_inputs


def setup_inputs(seed=0):
    import zlib

    import numpy as np

    out = dict(_drawn_inputs(seed))
    spreads = {}
    factors = {'e_b_gate_f': 14.474,
     'e_b_gate_b': 12.239,
     'e_q_norm': 8.0,
     'e_kv_norm': 4.08,
     'e_w_gate_f': 4.674,
     'e_w_gate_b': 3.988,
     'e_gla_norm': 6.937}
    for name, (base, spread) in spreads.items():
        noise = np.random.default_rng([zlib.crc32(name.encode()), seed]).standard_normal(out[name].shape)
        drawn = base * np.exp(spread * noise) if base else spread * noise
        out[name] = __import__('jax').numpy.asarray(drawn.astype(out[name].dtype))
    for name, factor in factors.items():
        out[name] = (out[name] * factor).astype(out[name].dtype)
    return out
```

```python
from contextlib import ExitStack

import numpy as np

import concourse.bass as bass
from concourse import mybir

F32 = mybir.dt.float32
U32 = mybir.dt.uint32
I32 = mybir.dt.int32
ALU = mybir.AluOpType
ACT = mybir.ActivationFunctionType
AXX = mybir.AxisListType.X

P = 128
BANK = 512
D = 1024
KD = D // P
SEQ = 2048
CTX = 256
NT = SEQ // P
NC = CTX // P
NA = NT + NC
EPS = 1e-6

HEADS = 4
DK, DV = 64, 128
RANK = 16
QR, KVR, ROPE, NOPE = 256, 128, 64, 128
D_IN = 2016
COL_Q, COL_K, COL_V, COL_Z, COL_R, COL_CQ, COL_CKV, COL_KR = 0, 256, 512, 1024, 1056, 1568, 1824, 1952
GRID_W = 64


class Memory:

    def __init__(self, nc, ctx, name):
        self.nc, self.ctx, self.name = nc, ctx, name
        self.numbers = []
        ctx.callback(self.zero)

    def zero(self):
        while self.numbers:
            first = self.numbers.pop(0)
            end = first + 1
            while self.numbers and self.numbers[0] == end:
                end += 1
                self.numbers.pop(0)
            self.nc.all_engine_barrier(sems_to_clear=range(first, end))

    def sbuf(self, name, shape, dt=F32):
        return self.ctx.enter_context(self.nc.sbuf_tensor(f"{self.name}_{name}", shape, dt))

    def psum(self, name, shape, dt=F32):
        return self.ctx.enter_context(self.nc.psum_tensor(f"{self.name}_{name}", shape, dt))

    def sem(self, name):
        handle = self.ctx.enter_context(self.nc.semaphore(f"{self.name}_{name}"))
        self.numbers.append(handle.num)
        return handle


def rows(ap, t):
    return ap.rearrange("(t p) n -> t p n", p=P)[bass.ds(t, 1)].rearrange("a p n -> p (a n)")


def modulation(nc, cc, w_mod, b_mod, g_mix_pre, g_ffn_pre, g_mix_post, g_ffn_post, ident_d, cols_d, gate_d):
    NB = 12
    with ExitStack() as ctx:
        m = Memory(nc, ctx, "mod")
        W = m.sbuf("w", [P, 3, KD, BANK])
        ident = m.sbuf("ident", [P, P])
        vec = m.sbuf("vec", [P, P])
        vecT = m.sbuf("vecT", [P, P])
        cin = m.sbuf("cin", [2 * KD, P])
        cT = m.sbuf("cT", [P, 2 * KD])
        ce = m.sbuf("ce", [P, 2 * KD])
        sil = m.sbuf("sil", [P, KD, 2])
        brow = m.sbuf("brow", [1, 2, 2, D])
        grow = m.sbuf("grow", [1, 2, 2, D])
        orow = m.sbuf("orow", [1, 2, D])
        ocol = m.sbuf("ocol", [P, 2, 2, 2, KD])
        psc = m.psum("psc", [P, 2, BANK])
        psr = m.psum("psr", [P, 2, 2, BANK])
        pst = m.psum("pst", [P, BANK])
        small_in, t_done, t_copied, c_exp, c_one, c_rec, sil_done = (
            m.sem(n) for n in ("small_in", "t_done", "t_copied", "c_exp", "c_one", "c_rec", "sil_done"))
        w_in = [m.sem(f"w_in{s}") for s in range(3)]
        w_used, half_read, stored, step = (m.sem(n) for n in ("w_used", "half_read", "stored", "step"))
        wv = w_mod.rearrange("l (k p) (b n) -> l b p k n", p=P, n=BANK)
        block = ctx.enter_context(nc.Block())

        def put(sp, u):
            sp.wait_ge(half_read, u + 1)
            if u:
                sp.wait_ge(stored, 32 * u)
            sp.dma_start(cols_d[u // 2, u % 2], ocol[:, u % 2]).then_inc(stored, 16)
            sp.dma_start(gate_d[u // 2, u % 2:u % 2 + 1], orow[:, u % 2]).then_inc(stored, 16)

        @block.sync
        def _(sp):
            sp.dma_start(ident[:, :], ident_d).then_inc(small_in, 16)
            sp.dma_start(vec[0:96, :], b_mod.rearrange("l (n p) -> (l n) p", p=P)).then_inc(small_in, 16)
            sp.dma_start(vec[96:112, :], g_mix_pre.rearrange("l (n p) -> (l n) p", p=P)).then_inc(small_in, 16)
            sp.dma_start(vec[112:128, :], g_ffn_pre.rearrange("l (n p) -> (l n) p", p=P)).then_inc(small_in, 16)
            sp.dma_start(cin[:, :], cc.rearrange("c (n p) -> (c n) p", p=P)).then_inc(small_in, 16)
            bv = b_mod.rearrange("(a l) (h s n) -> a l h s n", a=1, h=2, s=3)
            for l in range(2):
                sp.dma_start(brow[:, l], bv[:, l, :, 2]).then_inc(small_in, 16)
                sp.dma_start(grow[:, l, 0], g_mix_post[l:l + 1]).then_inc(small_in, 16)
                sp.dma_start(grow[:, l, 1], g_ffn_post[l:l + 1]).then_inc(small_in, 16)
            for l in range(2):
                for b in range(NB):
                    n = l * NB + b
                    if n >= 3:
                        sp.wait_ge(w_used, n - 2)
                    sp.dma_start(W[:, n % 3], wv[l, b]).then_inc(w_in[n % 3], 16)
                    if b % 6 == 5 and n > 6:
                        put(sp, l * 2 + b // 6 - 1)
            put(sp, 3)
            sp.wait_ge(stored, 4 * 32)

        @block.tensor
        def _(pe):
            pe.wait_ge(small_in, 16 * 11)
            nc.tensor.transpose(pst[:, 0:P], vec[:, :], ident[:, :])
            nc.tensor.transpose(pst[:, P:P + 16], cin[:, :], ident[0:16, 0:16]).then_inc(t_done, 1)
            pe.wait_ge(sil_done, 1)
            for l in range(2):
                for b in range(NB):
                    n, h, seg = l * NB + b, b // 6, b % 6 // 2
                    if b % 6 == 0 and l:
                        pe.wait_ge(half_read, (l - 1) * 2 + h + 1)
                    pe.wait_ge(w_in[n % 3], 16 * (n // 3 + 1))
                    if seg < 2:
                        for q in range(4):
                            at = (seg * KD + b % 2 * 4 + q) * 2
                            for k in range(KD):
                                last = nc.tensor.matmul(psc[:, h, at:at + 2], W[:, n % 3, k, q * P:(q + 1) * P],
                                                        sil[:, k], start=k == 0, stop=k == KD - 1)
                    else:
                        for k in range(KD):
                            last = nc.tensor.matmul(psr[0:2, h, b % 2], sil[:, k], W[:, n % 3, k],
                                                    start=k == 0, stop=k == KD - 1)
                    last.then_inc(w_used, 1)

        @block.scalar
        def _(act):
            act.wait_ge(t_copied, 1)
            nc.scalar.activation(ce[:, :], cT[:, :], ACT.Exp, scale=-1.0).then_inc(c_exp, 1)

        @block.vector
        def _(dve):
            dve.wait_ge(t_done, 1)
            nc.vector.tensor_copy(vecT[:, :], pst[:, 0:P])
            nc.vector.tensor_copy(cT[:, :], pst[:, P:P + 16]).then_inc(t_copied, 1)
            dve.wait_ge(c_exp, 1)
            nc.vector.tensor_scalar(ce[:, :], ce[:, :], 1.0, None, ALU.add).then_inc(c_one, 1)
            dve.wait_ge(c_one, 1)
            nc.vector.reciprocal(ce[:, :], ce[:, :]).then_inc(c_rec, 1)
            dve.wait_ge(c_rec, 1)
            nc.vector.tensor_tensor(sil[:, :, :].rearrange("p k c -> p c k"), cT[:, :].rearrange("p (c k) -> p c k", c=2),
                                    ce[:, :].rearrange("p (c k) -> p c k", c=2), ALU.mult).then_inc(sil_done, 1)
            for u in range(4):
                l, h = u // 2, u % 2
                dve.wait_ge(w_used, 6 * u + 6)
                if u >= 2:
                    dve.wait_ge(stored, 32 * (u - 1))
                pv = psc[:, h, 0:4 * KD].rearrange("p (s k c) -> p s k c", s=2, c=2)
                for c in range(2):
                    sh = vecT[:, l * 48 + h * 24:l * 48 + h * 24 + 8]
                    sc = vecT[:, l * 48 + h * 24 + 8:l * 48 + h * 24 + 16]
                    g = vecT[:, 96 + h * 16 + l * 8:96 + h * 16 + l * 8 + 8]
                    nc.vector.tensor_tensor(ocol[:, h, c, 0], pv[:, 0, :, c], sh, ALU.add)
                    nc.vector.tensor_tensor(ocol[:, h, c, 1], pv[:, 1, :, c], sc, ALU.add).then_inc(step, 1)
                    dve.wait_ge(step, 2 * u + c + 1)
                    nc.vector.scalar_tensor_tensor(ocol[:, h, c, 1], ocol[:, h, c, 1], 1.0, g, ALU.add, ALU.mult).then_inc(c_one, 1)
                ov = orow[:, h].rearrange("a (b n) -> a b n", b=2)
                bv = brow[:, l, h].rearrange("a (b n) -> a b n", b=2)
                gv = grow[:, l, h].rearrange("a (b n) -> a b n", b=2)
                nc.vector.tensor_tensor(ov, psr[0:1, h], bv, ALU.add).then_inc(c_one, 1)
                dve.wait_ge(c_one, 3 * u + 4)
                nc.vector.tensor_tensor(ov, ov, gv, ALU.mult).then_inc(half_read, 1)


def nothing(i, s):
    pass


def staged(eng, pairs, early, front, back, apart=1):
    def step(i):
        front(i, 0)
        early(i, 1)
        if not (isinstance(i, int) and i == 0):
            back(i - 1, 1)
        front(i, 1)
        if not (isinstance(i, int) and i == pairs - 1):
            early(i + 1, 0)
        back(i, 0)

    early(0, 0)
    for i in range(apart):
        step(i)
    with eng.Fori(apart, pairs - 1) as i:
        step(i)
    step(pairs - 1)
    back(pairs - 1, 1)


def project(nc, name, src, ntiles, cols_x, cols_c, w, width, dst, ident_d):
    norm = cols_x is not None
    nb = (width + BANK - 1) // BANK
    blocks = [(b * BANK, min(width, (b + 1) * BANK)) for b in range(nb)]
    pairs = ntiles // 2
    with ExitStack() as ctx:
        m = Memory(nc, ctx, name)
        W = m.sbuf("w", [P, KD, width])
        X = m.sbuf("x", [P, 2, D])
        XN = m.sbuf("xn", [P, 2, D]) if norm else X
        HT = m.sbuf("ht", [P, 2, KD, P])
        O = m.sbuf("o", [P, 2, width])
        ident = m.sbuf("ident", [P, P])
        mod = m.sbuf("mod", [P, 2, 2, KD])
        stat = m.sbuf("stat", [P, 2, 4])
        eps = m.sbuf("eps", [P, 1])
        psT = m.psum("psT", [P, 2, BANK])
        psO = m.psum("psO", [P, nb, BANK])
        w_loaded = m.sem("w_loaded")
        squared = m.sem("squared")
        rooted = m.sem("rooted")
        inverted = m.sem("inverted")
        xn_done = m.sem("xn_done")
        tr_done = m.sem("tr_done")
        ht_a, ht_v = m.sem("ht_a"), m.sem("ht_v")
        banks_done = m.sem("banks_done")
        banks_a, banks_v = m.sem("banks_a"), m.sem("banks_v")
        eps_set = m.sem("eps_set")
        ident_in = m.sem("ident_in")
        x_in = [m.sem(f"x_in{s}") for s in range(2)]
        o_free = [m.sem(f"o_free{s}") for s in range(2)]
        block = ctx.enter_context(nc.Block())
        consts = 16 * (2 if norm else 0)
        mine_a, mine_v = list(range(0, nb, 2)), list(range(1, nb, 2))
        x_free = xn_done if norm else tr_done

        @block.sync
        def _(sp):
            sp.dma_start(ident[:, :], ident_d).then_inc(ident_in, 16)
            if norm:
                sp.dma_start(mod[:, 0], cols_x).then_inc(w_loaded, 16)
                sp.dma_start(mod[:, 1], cols_c).then_inc(w_loaded, 16)
            wv = w.rearrange("(k p) n -> p k n", p=P)
            for k in range(0, KD, 2):
                sp.dma_start(W[:, k:k + 2], wv[:, k:k + 2]).then_inc(w_loaded, 16)

            for s in range(2):
                sp.sem_inc(o_free[s], 16)

            def load(i, s):
                sp.wait_ge(x_free, i * 2 + s + 1)
                sp.wait_ge(ident_in, 16)
                sp.dma_start(X[:, s], rows(src, i * 2 + s)).then_inc(x_in[s], 16)

            def store(i, s):
                n = i * 2 + s
                sp.wait_ge(banks_a, (n + 2) * len(mine_a))
                sp.wait_ge(banks_v, (n + 2) * len(mine_v))
                sp.wait_ge(ident_in, 16)
                sp.dma_start(rows(dst, i * 2 + s), O[:, s]).then_inc(o_free[s], 16)
            staged(sp, pairs, load, nothing, store)
            for s in range(2):
                sp.wait_ge(o_free[s], 16 * (pairs + 1))

        def banks_out(eng, i, s, mine, copied, copy):
            eng.wait_ge(o_free[s], i * 16 + 16)
            for b in mine:
                eng.wait_ge(banks_done, (i * 2 + s + 2) * nb + b + 1)
                a, z = blocks[b]
                copy(O[:, s, a:z], psO[:, b, 0:z - a]).then_inc(copied, 1)

        @block.scalar
        def _(act):
            act.sem_inc(banks_a, len(mine_a))
            act.wait_ge(w_loaded, consts + 64)
            if norm:
                act.wait_ge(eps_set, 1)

            def early(i, s):
                n = i * 2 + s
                if norm:
                    act.wait_ge(x_in[s], i * 16 + 16)
                    act.wait_ge(tr_done, n + 1)
                    nc.scalar.activation(XN[:, s], X[:, s], ACT.Square, accum_out=stat[:, s, 0:1]).then_inc(squared, 1)
                    act.wait_ge(squared, n + 1)
                    nc.scalar.activation(stat[:, s, 1:2], stat[:, s, 0:1], ACT.Sqrt, bias=eps[:, 0:1],
                                         scale=1.0 / D).then_inc(rooted, 1)

            def front(i, s):
                n = i * 2 + s
                act.wait_ge(tr_done, n + 3)
                act.wait_ge(banks_done, (n + 1) * nb)
                if norm:
                    c = 1 if isinstance(i, int) and i == 0 else 0
                    for k in range(4, 8):
                        last = nc.scalar.activation(HT[:, s, k], psT[:, 1, (k - 4) * P:(k - 3) * P], ACT.Identity,
                                                    bias=mod[:, c, 0, k:k + 1], scale=mod[:, c, 1, k:k + 1])
                else:
                    last = nc.scalar.activation(HT[:, s, 4:8], psT[:, 1].rearrange("p (k n) -> p k n", k=4), ACT.Copy)
                last.then_inc(ht_a, 1)

            def back(i, s):
                banks_out(act, i, s, mine_a, banks_a,
                          lambda out, ps: nc.scalar.activation(out, ps, ACT.Copy))
            staged(act, pairs, early, front, back)

        @block.vector
        def _(dve):
            dve.sem_inc(banks_v, len(mine_v))
            dve.sem_inc(xn_done, 2)
            nc.vector.memset(eps[:, :], EPS).then_inc(eps_set, 1)
            dve.wait_ge(w_loaded, consts + 64)

            def early(i, s):
                n = i * 2 + s
                if norm:
                    dve.wait_ge(rooted, n + 1)
                    nc.vector.reciprocal(stat[:, s, 2:3], stat[:, s, 1:2]).then_inc(inverted, 1)
                    dve.wait_ge(inverted, n + 1)
                    nc.vector.tensor_scalar(XN[:, s], X[:, s], stat[:, s, 2:3], None, ALU.mult).then_inc(xn_done, 1)

            def front(i, s):
                n = i * 2 + s
                dve.wait_ge(tr_done, n + 3)
                dve.wait_ge(banks_done, (n + 1) * nb)
                if norm:
                    c = 1 if isinstance(i, int) and i == 0 else 0
                    for k in range(4):
                        last = nc.vector.tensor_scalar(HT[:, s, k], psT[:, 0, k * P:(k + 1) * P], mod[:, c, 1, k:k + 1],
                                                       mod[:, c, 0, k:k + 1], ALU.mult, ALU.add)
                else:
                    last = nc.vector.tensor_copy(HT[:, s, 0:4], psT[:, 0].rearrange("p (k n) -> p k n", k=4))
                last.then_inc(ht_v, 1)

            def back(i, s):
                banks_out(dve, i, s, mine_v, banks_v, nc.vector.tensor_copy)
            staged(dve, pairs, early, front, back)

        @block.tensor
        def _(pe):
            pe.sem_inc(banks_done, 2 * nb)
            pe.sem_inc(tr_done, 2)
            pe.wait_ge(w_loaded, consts + 64)
            pe.wait_ge(ident_in, 16)

            def front(i, s):
                n = i * 2 + s
                if norm:
                    pe.wait_ge(xn_done, n + 3)
                else:
                    pe.wait_ge(x_in[s], i * 16 + 16)
                if not isinstance(i, int) or n > 0:
                    pe.wait_ge(ht_a, n)
                    pe.wait_ge(ht_v, n)
                for k in range(KD):
                    last = nc.tensor.transpose(psT[:, k // 4, k % 4 * P:(k % 4 + 1) * P], XN[:, s, k * P:(k + 1) * P],
                                               ident[:, :])
                last.then_inc(tr_done, 1)

            def back(i, s):
                n = i * 2 + s
                pe.wait_ge(ht_a, n + 1)
                pe.wait_ge(ht_v, n + 1)
                for b, (a, z) in enumerate(blocks):
                    mine, copied = (mine_a, banks_a) if b in mine_a else (mine_v, banks_v)
                    pe.wait_ge(copied, n * len(mine) + mine.index(b) + 1)
                    for k in range(KD):
                        last = nc.tensor.matmul(psO[:, b, 0:z - a], HT[:, s, k], W[:, k, a:z], start=k == 0, stop=k == KD - 1)
                    last.then_inc(banks_done, 1)
            staged(pe, pairs, nothing, front, back)


def residual(nc, name, y, x, dst, gate, cols, hT_d, ident_d, stride4=False):
    pairs = NT // 2
    with ExitStack() as ctx:
        m = Memory(nc, ctx, name)
        Y = m.sbuf("y", [P, 2, D])
        X = m.sbuf("x", [P, 2, D])
        T = m.sbuf("t", [P, 2, D])
        XO = m.sbuf("xo", [P, 2, D])
        XN = m.sbuf("xn", [P, 2, D])
        junk = m.sbuf("junk", [P, D])
        HT = m.sbuf("ht", [P, 2, KD, P])
        G = m.sbuf("g", [P, D])
        ident = m.sbuf("ident", [P, P])
        mod = m.sbuf("mod", [P, 2, KD])
        stat = m.sbuf("stat", [P, 2, 8])
        eps = m.sbuf("eps", [P, 1])
        psT = m.psum("psT", [P, 2, 2, BANK])
        const_in = m.sem("const_in")
        ident_in = m.sem("ident_in")
        eps_set = m.sem("eps_set")
        yx_in = [m.sem(f"yx_in{s}") for s in range(2)]
        yroot = m.sem("yroot")
        xroot = m.sem("xroot")
        sq_y, sq_x = m.sem("sq_y"), m.sem("sq_x")
        inv, inv_x = m.sem("inv"), m.sem("inv_x")
        scaled = m.sem("scaled")
        summed = m.sem("summed")
        normed = m.sem("normed")
        tr_done = m.sem("tr_done")
        ht_a, ht_v = m.sem("ht_a"), m.sem("ht_v")
        x_out = [m.sem(f"x_out{s}") for s in range(2)]
        h_out = [m.sem(f"h_out{s}") for s in range(2)]
        block = ctx.enter_context(nc.Block())
        nconst = 16 * (2 if cols is not None else 1)

        @block.sync
        def _(sp):
            sp.dma_start(ident[:, :], ident_d).then_inc(ident_in, 16)
            sp.dma_start(G[:, :], gate.rearrange("(a n) -> a n", a=1).to_broadcast([P, D])).then_inc(const_in, 16)
            if cols is not None:
                sp.dma_start(mod[:, :], cols).then_inc(const_in, 16)
            for s in range(2):
                sp.sem_inc(x_out[s], 16)
                sp.sem_inc(h_out[s], 16)

            def load(i, s):
                n = i * 2 + s
                sp.wait_ge(summed, n + 1)
                sp.wait_ge(ident_in, 16)
                sp.dma_start(Y[:, s], rows(y, n)).then_inc(yx_in[s], 16)
                sp.dma_start(X[:, s], rows(x, n)).then_inc(yx_in[s], 16)

            def store_x(i, s):
                n = i * 2 + s
                sp.wait_ge(summed, n + 3)
                sp.wait_ge(ident_in, 16)
                sp.dma_start(rows(dst, n), XO[:, s]).then_inc(x_out[s], 16)

            def store_h(i, s):
                n = i * 2 + s
                if cols is None:
                    return
                sp.wait_ge(ht_a, n + 3)
                sp.wait_ge(ht_v, n + 3)
                sp.wait_ge(ident_in, 16)
                sp.dma_start(hT_d[:, :, bass.ds(n * P, P)], HT[:, s]).then_inc(h_out[s], 16)
            staged(sp, pairs, load, store_x, store_h)
            for s in range(2):
                sp.wait_ge(x_out[s], 16 * (pairs + 1))
                sp.wait_ge(h_out[s], 16 * (pairs + 1) if cols is not None else 16)

        @block.scalar
        def _(act):
            act.sem_inc(ht_a, 2)
            act.wait_ge(eps_set, 1)
            act.wait_ge(const_in, nconst)

            def early(i, s):
                n = i * 2 + s
                act.wait_ge(yx_in[s], i * 32 + 32)
                nc.scalar.activation(junk[:, :], Y[:, s], ACT.Square, accum_out=stat[:, s, 0:1]).then_inc(sq_y, 1)
                act.wait_ge(sq_y, n + 1)
                nc.scalar.activation(stat[:, s, 1:2], stat[:, s, 0:1], ACT.Sqrt, bias=eps[:, 0:1], scale=1.0 / D).then_inc(yroot, 1)

            def front(i, s):
                n = i * 2 + s
                if cols is None:
                    return
                act.wait_ge(summed, n + 3)
                nc.scalar.activation(junk[:, :], XO[:, s], ACT.Square, accum_out=stat[:, s, 4:5]).then_inc(sq_x, 1)
                act.wait_ge(sq_x, n + 1)
                nc.scalar.activation(stat[:, s, 5:6], stat[:, s, 4:5], ACT.Sqrt, bias=eps[:, 0:1], scale=1.0 / D).then_inc(xroot, 1)

            def back(i, s):
                n = i * 2 + s
                if cols is None:
                    return
                act.wait_ge(tr_done, n + 3)
                act.wait_ge(h_out[s], i * 16 + 16)
                for k in range(4, 8):
                    last = nc.scalar.activation(HT[:, s, k], psT[:, s, 1, (k - 4) * P:(k - 3) * P], ACT.Identity,
                                                bias=mod[:, 0, k:k + 1], scale=mod[:, 1, k:k + 1])
                last.then_inc(ht_a, 1)
            staged(act, pairs, early, front, back)

        @block.vector
        def _(dve):
            dve.sem_inc(summed, 2)
            dve.sem_inc(ht_v, 2)
            nc.vector.memset(eps[:, :], EPS).then_inc(eps_set, 1)
            dve.wait_ge(const_in, nconst)

            def early(i, s):
                n = i * 2 + s
                dve.wait_ge(yroot, n + 1)
                nc.vector.reciprocal(stat[:, s, 2:3], stat[:, s, 1:2]).then_inc(inv, 1)
                dve.wait_ge(inv, n + 1)
                nc.vector.scalar_tensor_tensor(T[:, s], Y[:, s], stat[:, s, 2:3], G[:, :], ALU.mult, ALU.mult).then_inc(scaled, 1)
                dve.wait_ge(scaled, n + 1)
                dve.wait_ge(x_out[s], i * 16 + 16)
                if cols is not None:
                    dve.wait_ge(tr_done, n + 1)
                nc.vector.tensor_tensor(XO[:, s], X[:, s], T[:, s], ALU.add).then_inc(summed, 1)

            def front(i, s):
                n = i * 2 + s
                if cols is None:
                    return
                dve.wait_ge(xroot, n + 1)
                nc.vector.reciprocal(stat[:, s, 6:7], stat[:, s, 5:6]).then_inc(inv_x, 1)
                dve.wait_ge(inv_x, n + 1)
                dve.wait_ge(tr_done, n + 1)
                nc.vector.tensor_scalar(XN[:, s], XO[:, s], stat[:, s, 6:7], None, ALU.mult).then_inc(normed, 1)

            def back(i, s):
                n = i * 2 + s
                if cols is None:
                    return
                dve.wait_ge(tr_done, n + 3)
                dve.wait_ge(h_out[s], i * 16 + 16)
                for k in range(4):
                    last = nc.vector.tensor_scalar(HT[:, s, k], psT[:, s, 0, k * P:(k + 1) * P], mod[:, 1, k:k + 1],
                                                   mod[:, 0, k:k + 1], ALU.mult, ALU.add)
                last.then_inc(ht_v, 1)
            staged(dve, pairs, early, front, back)

        @block.tensor
        def _(pe):
            pe.sem_inc(tr_done, 2)
            pe.wait_ge(ident_in, 16)

            def front(i, s):
                n = i * 2 + s
                if cols is None:
                    return
                pe.wait_ge(normed, n + 1)
                pe.wait_ge(ht_a, n + 1)
                pe.wait_ge(ht_v, n + 1)
                for k in range(KD):
                    last = nc.tensor.transpose(psT[:, s, k // 4, k % 4 * P:(k % 4 + 1) * P], XN[:, s, k * P:(k + 1) * P],
                                               ident[:, :])
                last.then_inc(tr_done, 1)
            staged(pe, pairs, nothing, front, nothing)


def swiglu(nc, name, hT_d, w1, w3, w2, gates_d, y_d, x_tiles=NT):
    E, _, F = w1.shape
    FC = F // P
    NB = SEQ // BANK
    TB = BANK // P
    with ExitStack() as ctx:
        m = Memory(nc, ctx, name)
        HT = m.sbuf("ht", [P, KD, SEQ])
        YA = m.sbuf("ya", [P, NT, D])
        W1 = m.sbuf("w1", [P, 2, KD, P])
        W3 = m.sbuf("w3", [P, 2, KD, P])
        W2 = m.sbuf("w2", [P, 2, D])
        S = m.sbuf("s", [P, 2, BANK])
        A = m.sbuf("a", [P, 2, BANK])
        GT = m.sbuf("gt", [P, NT, E])
        psU = m.psum("psU", [P, 2, BANK])
        psG = m.psum("psG", [P, 2, BANK])
        psY = m.psum("psY", [P, 4, BANK])
        h_in = m.sem("h_in")
        w_in = [m.sem(f"w_in{s}") for s in range(2)]
        h_ready = m.sem("h_ready")
        ug_done = m.sem("ug_done")
        silu_done = m.sem("silu_done")
        a_done = m.sem("a_done")
        y_done = m.sem("y_done")
        y_added = m.sem("y_added")
        zeroed = m.sem("zeroed")
        y_out = m.sem("y_out")
        block = ctx.enter_context(nc.Block())
        per = NB * TB * 2
        npairs = FC // 2

        @block.sync
        def _(sp):
            for k in range(KD):
                sp.dma_start(HT[:, k], hT_d[:, k]).then_inc(h_in, 16)
            if gates_d is not None:
                sp.dma_start(GT[:, :], gates_d).then_inc(h_in, 16)
            w1v = w1.rearrange("e (k p) (f n) -> e f p k n", p=P, n=P)
            w3v = w3.rearrange("e (k p) (f n) -> e f p k n", p=P, n=P)
            w2v = w2.rearrange("e (f p) n -> e f p n", p=P)
            with sp.Fori(0, E) as e:
                with sp.Fori(0, npairs) as i:
                    for s in range(2):
                        c = (e * npairs + i) * 2 + s
                        sp.wait_ge(y_done, c * per + per)
                        sp.wait_ge(a_done, 2)
                        f = i * 2 + s
                        sp.dma_start(W1[:, s], w1v[bass.ds(e, 1), bass.ds(f, 1)].rearrange("a b p k n -> p (a b k) n")).then_inc(w_in[s], 16)
                        sp.dma_start(W3[:, s], w3v[bass.ds(e, 1), bass.ds(f, 1)].rearrange("a b p k n -> p (a b k) n")).then_inc(w_in[s], 16)
                        sp.dma_start(W2[:, s], w2v[bass.ds(e, 1), bass.ds(f, 1)].rearrange("a b p n -> p (a b n)")).then_inc(w_in[s], 16)
            sp.wait_ge(y_added, 4 + E * FC * per)
            for t in range(0, NT, 4):
                sp.dma_start(y_d.rearrange("(t p) n -> p t n", p=P)[:, t:t + 4], YA[:, t:t + 4]).then_inc(y_out, 16)
            sp.wait_ge(y_out, 16 * (NT // 4))

        @block.tensor
        def _(pe):
            pe.sem_inc(y_done, 2 * per)
            pe.wait_ge(h_in, 16 * (KD + (1 if gates_d is not None else 0)))

            def up(c, ws, s, b):
                n = c * NB + b
                if b == 0:
                    pe.wait_ge(w_in[s], ws * 48 + 48)
                pe.wait_ge(a_done, n + 1)
                for ps, W in ((psU, W1), (psG, W3)):
                    for k in range(KD):
                        last = nc.tensor.matmul(ps[:, b % 2], W[:, s, k], HT[:, k, b * BANK:(b + 1) * BANK],
                                                start=k == 0, stop=k == KD - 1)
                last.then_inc(ug_done, 1)

            def down(c, s, b):
                n = c * NB + b
                pe.wait_ge(a_done, n + 3)
                for t in range(TB):
                    for h in range(2):
                        j = t * 2 + h
                        pe.wait_ge(y_added, c * per + b * TB * 2 + j + 1)
                        nc.tensor.matmul(psY[:, j % 4], A[:, b % 2, t * P:(t + 1) * P], W2[:, s, h * BANK:(h + 1) * BANK],
                                         start=True, stop=True).then_inc(y_done, 1)
            with pe.Fori(0, E) as e:
                with pe.Fori(0, npairs) as i:
                    for s in range(2):
                        ws = e * npairs + i
                        c = ws * 2 + s
                        for b in range(NB + 1):
                            if b < NB:
                                up(c, ws, s, b)
                            if b:
                                down(c, s, b - 1)

        @block.scalar
        def _(act):
            act.sem_inc(silu_done, 2)
            with act.Fori(0, E * npairs) as i:
                for s in range(2):
                    for b in range(NB):
                        n = (i * 2 + s) * NB + b
                        act.wait_ge(ug_done, n + 1)
                        act.wait_ge(a_done, n + 1)
                        nc.scalar.activation(S[:, b % 2], psU[:, b % 2], ACT.Silu).then_inc(silu_done, 1)

        @block.vector
        def _(dve):
            dve.sem_inc(a_done, 2)
            dve.sem_inc(y_added, 4)
            nc.vector.memset(YA[:, :], 0.0).then_inc(zeroed, 1)
            dve.wait_ge(h_in, 16 * (KD + (1 if gates_d is not None else 0)))
            dve.wait_ge(zeroed, 1)

            def hidden(c, b):
                n = c * NB + b
                dve.wait_ge(silu_done, n + 3)
                dve.wait_ge(y_done, c * per + (2 + 0) * per + (b - 1) * TB * 2)
                nc.vector.tensor_tensor(A[:, b % 2], S[:, b % 2], psG[:, b % 2], ALU.mult).then_inc(a_done, 1)

            def add(e, c, b):
                for t in range(TB):
                    for h in range(2):
                        j = t * 2 + h
                        dve.wait_ge(y_done, (c + 2) * per + b * TB * 2 + j + 1)
                        out = YA[:, b * TB + t, h * BANK:(h + 1) * BANK]
                        if gates_d is None:
                            nc.vector.tensor_tensor(out, psY[:, j % 4], out, ALU.add).then_inc(y_added, 1)
                        else:
                            nc.vector.scalar_tensor_tensor(out, psY[:, j % 4], GT[:, b * TB + t, bass.ds(e, 1)], out,
                                                           ALU.mult, ALU.add).then_inc(y_added, 1)
            with dve.Fori(0, E) as e:
                with dve.Fori(0, npairs) as i:
                    for s in range(2):
                        c = (e * npairs + i) * 2 + s
                        for b in range(NB + 1):
                            if b < NB:
                                hidden(c, b)
                            if b:
                                add(e, c, b - 1)


def mla_prepare(nc, proj_d, q_norm, kv_norm, rope_tok, ident_d, ckvT, krT, ckv, cqT):
    W = D_IN - COL_CQ
    KV, KR = COL_CKV - COL_CQ, COL_KR - COL_CQ
    pairs = NA // 2
    with ExitStack() as ctx:
        m = Memory(nc, ctx, "mp")
        X = m.sbuf("x", [P, 2, W])
        N = m.sbuf("n", [P, 2, QR])
        R = m.sbuf("r", [P, 2, 2, ROPE])
        RT = m.sbuf("rt", [P, 2, 2, ROPE])
        junk = m.sbuf("junk", [P, QR])
        junk2 = m.sbuf("junk2", [P, KVR])
        K = m.sbuf("k", [P, 2, KVR])
        G = m.sbuf("g", [P, KVR])
        qn = m.sbuf("qn", [P, 2])
        ident = m.sbuf("ident", [P, P])
        stat = m.sbuf("stat", [P, 2, 8])
        eps = m.sbuf("eps", [P, 1])
        psT = m.psum("psT", [P, 2, BANK])
        psK = m.psum("psK", [P, 2, BANK])
        const_in, eps_set = m.sem("const_in"), m.sem("eps_set")
        x_in = [m.sem(f"x_in{s}") for s in range(2)]
        squared, rooted, inverted = m.sem("squared"), m.sem("rooted"), m.sem("inverted")
        parts = m.sem("parts")
        ready = m.sem("ready")
        tr_done = m.sem("tr_done")
        out_a, out_v = m.sem("out_a"), m.sem("out_v")
        block = ctx.enter_context(nc.Block())

        @block.sync
        def _(sp):
            sp.dma_start(ident[:, :], ident_d).then_inc(const_in, 16)
            sp.dma_start(G[:, :], kv_norm.to_broadcast([P, KVR])).then_inc(const_in, 16)
            sp.dma_start(qn[:, :], q_norm).then_inc(const_in, 16)
            sp.wait_ge(const_in, 48)

            def load(i, s):
                n = i * 2 + s
                sp.wait_ge(ready, n + 1)
                sp.wait_ge(const_in, 48)
                sp.dma_start(X[:, s], rows(proj_d[:, COL_CQ:D_IN], n)).then_inc(x_in[s], 16)
                sp.dma_start(RT[:, s], rope_tok.rearrange("(t p) a n -> t p a n", p=P)[bass.ds(n, 1)].rearrange("t p a n -> p (t a) n")).then_inc(x_in[s], 16)
            staged(sp, pairs, load, nothing, nothing)

        @block.scalar
        def _(act):
            act.sem_inc(out_a, 2)
            act.wait_ge(const_in, 48)
            act.wait_ge(eps_set, 1)

            def early(i, s):
                n = i * 2 + s
                act.wait_ge(x_in[s], i * 32 + 32)
                nc.scalar.activation(junk[:, 0:QR], X[:, s, 0:QR], ACT.Square, accum_out=stat[:, s, 0:1]).then_inc(squared, 1)
                nc.scalar.activation(junk2[:, :], X[:, s, KV:KV + KVR], ACT.Square, accum_out=stat[:, s, 1:2]).then_inc(squared, 1)
                act.wait_ge(squared, n * 2 + 2)
                nc.scalar.activation(stat[:, s, 2:3], stat[:, s, 0:1], ACT.Sqrt, bias=eps[:, 0:1], scale=1.0 / QR)
                nc.scalar.activation(stat[:, s, 3:4], stat[:, s, 1:2], ACT.Sqrt, bias=eps[:, 0:1], scale=1.0 / KVR).then_inc(rooted, 1)

            def front(i, s):
                n = i * 2 + s
                act.wait_ge(tr_done, n + 3)
                for k in range(2):
                    last = nc.scalar.activation(cqT[:, k, bass.ds(n * P, P)], psT[:, s, k * P:(k + 1) * P], ACT.Copy,
                                                scale=qn[:, k:k + 1])
                last.then_inc(out_a, 1)
            staged(act, pairs, early, front, nothing)

        @block.vector
        def _(dve):
            dve.sem_inc(ready, 2)
            dve.sem_inc(out_v, 2)
            nc.vector.memset(eps[:, :], EPS).then_inc(eps_set, 1)
            dve.wait_ge(const_in, 48)

            def early(i, s):
                n = i * 2 + s
                dve.wait_ge(rooted, n + 1)
                nc.vector.reciprocal(stat[:, s, 4:6], stat[:, s, 2:4]).then_inc(inverted, 1)
                dve.wait_ge(inverted, n + 1)
                dve.wait_ge(tr_done, n + 1)
                nc.vector.tensor_scalar(N[:, s], X[:, s, 0:QR], stat[:, s, 4:5], None, ALU.mult)
                nc.vector.scalar_tensor_tensor(K[:, s], X[:, s, KV:KV + KVR], stat[:, s, 5:6], G[:, :],
                                               ALU.mult, ALU.mult)
                kr = X[:, s, KR:KR + ROPE].rearrange("p (a u n) -> p a u n", a=2, u=2)
                sn = RT[:, s, 1].rearrange("p (a u n) -> p a u n", a=2, u=2)
                r1 = R[:, s, 1].rearrange("p (a u n) -> p a u n", a=2, u=2)
                nc.vector.tensor_tensor(R[:, s, 0], X[:, s, KR:KR + ROPE], RT[:, s, 0], ALU.mult)
                nc.vector.tensor_tensor(r1[:, :, 0], kr[:, :, 1], sn[:, :, 0], ALU.mult).then_inc(parts, 1)
                nc.vector.tensor_tensor(r1[:, :, 1], kr[:, :, 0], sn[:, :, 1], ALU.mult).then_inc(parts, 1)
                dve.wait_ge(parts, n * 2 + 2)
                nc.vector.tensor_tensor(R[:, s, 0], R[:, s, 0], R[:, s, 1], ALU.add).then_inc(ready, 1)

            def front(i, s):
                n = i * 2 + s
                dve.wait_ge(tr_done, n + 3)
                nc.vector.tensor_copy(ckvT[:, bass.ds(n * P, P)], psK[:, s, 0:P])
                nc.vector.tensor_copy(ckv[:, bass.ds(n, 1)].rearrange("p a n -> p (a n)"), K[:, s])
                nc.vector.tensor_copy(krT[:, bass.ds(n * P, P)], psK[0:ROPE, s, P:2 * P]).then_inc(out_v, 1)
            staged(dve, pairs, early, front, nothing)

        @block.tensor
        def _(pe):
            pe.sem_inc(tr_done, 2)
            pe.wait_ge(const_in, 48)

            def front(i, s):
                n = i * 2 + s
                pe.wait_ge(ready, n + 3)
                pe.wait_ge(out_a, n + 1)
                pe.wait_ge(out_v, n + 1)
                for k in range(2):
                    nc.tensor.transpose(psT[:, s, k * P:(k + 1) * P], N[:, s, k * P:(k + 1) * P], ident[:, :])
                nc.tensor.transpose(psK[:, s, 0:P], K[:, s], ident[:, :])
                nc.tensor.transpose(psK[0:ROPE, s, P:2 * P], R[:, s, 0], ident[:, :]).then_inc(tr_done, 1)
            staged(pe, pairs, nothing, front, nothing)


def mla_attend(nc, w_uq, w_uq_swapped, w_ukT, w_ukv, rope_feat, ident_d, ckvT, krT, ckv, cqT, mix_d):
    KT = NA
    KEYS = KT * P
    chunks = [(c * BANK, min(KEYS, (c + 1) * BANK)) for c in range((KEYS + BANK - 1) // BANK)]
    groups = [(g, min(KT, g + 4)) for g in range(0, KT, 4)]
    NCH, NG = len(chunks), len(groups)
    SCALE = float(NOPE + ROPE) ** -0.5
    HW = NOPE + ROPE
    with ExitStack() as ctx:
        m = Memory(nc, ctx, "ma")
        WUQ = m.sbuf("wuq", [P, 2, HEADS * HW])
        WUS = m.sbuf("wus", [P, 2, HEADS * ROPE])
        WKT = m.sbuf("wkt", [P, HEADS, KVR])
        WV = m.sbuf("wv", [P, HEADS, DV])
        RF = m.sbuf("rf", [ROPE, 2, SEQ])
        ident = m.sbuf("ident", [P, P])
        QN = m.sbuf("qn", [P, HEADS, P])
        QP = m.sbuf("qp", [P, HEADS, P])
        QR_ = m.sbuf("qr", [ROPE, HEADS, P])
        QT = m.sbuf("qt", [ROPE, HEADS, P])
        PM = m.sbuf("pm", [P, 2, KEYS])
        PT = m.sbuf("pt", [P, KT, P])
        OL = m.sbuf("ol", [P, P])
        MX = m.sbuf("mx", [P, HEADS * DV])
        stat = m.sbuf("stat", [P, 2, 2, 8])
        top = m.sbuf("top", [P, 2, 4])
        psS = m.psum("psS", [P, NCH, BANK])
        psT = m.psum("psT", [P, 2, BANK])
        psO = m.psum("psO", [P, BANK])
        const_in = m.sem("const_in")
        q_done = m.sem("q_done")
        qn_out = m.sem("qn_out")
        qr_part = m.sem("qr_part")
        qr_out = m.sem("qr_out")
        qp_done = m.sem("qp_done")
        qp_out = m.sem("qp_out")
        s_done = m.sem("s_done")
        c_max = m.sem("c_max")
        h_max = m.sem("h_max")
        neg_max = m.sem("neg_max")
        exp_done = m.sem("exp_done")
        sums = m.sem("sums")
        inv_done = m.sem("inv_done")
        t_done = m.sem("t_done")
        t_out = m.sem("t_out")
        pv_done = m.sem("pv_done")
        ol_out = m.sem("ol_out")
        av_done = m.sem("av_done")
        av_out = m.sem("av_out")
        m_out = m.sem("m_out")
        block = ctx.enter_context(nc.Block())
        NCONST = 6 * 16

        def heads(eng, tile_start, score, weigh):
            def tile(t, before):
                tile_start(t)
                for h in range(HEADS):
                    score(t, h)
                    if h:
                        weigh(t, h - 1)
                    elif before is not None:
                        weigh(before, HEADS - 1)
            tile(0, None)
            with eng.Fori(1, NT) as t:
                tile(t, t - 1)
            weigh(NT - 1, HEADS - 1)

        @block.sync
        def _(sp):
            sp.dma_start(WUQ[:, :], w_uq.rearrange("(k p) n -> p k n", p=P)).then_inc(const_in, 16)
            sp.dma_start(WUS[:, :], w_uq_swapped.rearrange("(k p) n -> p k n", p=P)).then_inc(const_in, 16)
            sp.dma_start(WKT[:, :], w_ukT).then_inc(const_in, 16)
            sp.dma_start(WV[:, :], w_ukv.rearrange("c (h n) -> c h n", h=HEADS)[:, :, NOPE:NOPE + DV]).then_inc(const_in, 16)
            sp.dma_start(RF[:, :], rope_feat).then_inc(const_in, 16)
            sp.dma_start(ident[:, :], ident_d).then_inc(const_in, 16)
            sp.wait_ge(const_in, NCONST)
            with sp.Fori(0, NT) as t:
                sp.wait_ge(av_out, t * HEADS + HEADS)
                sp.wait_ge(const_in, NCONST)
                sp.dma_start(rows(mix_d[:, HEADS * DV:2 * HEADS * DV], t), MX[:, :]).then_inc(m_out, 16)
            sp.wait_ge(m_out, 16 * NT)

        @block.tensor
        def _(pe):
            pe.wait_ge(const_in, NCONST)

            def start(t):
                if not isinstance(t, int):
                    pe.wait_ge(exp_done, t * HEADS * NCH)
                tok = bass.ds((t + NC) * P, P)
                for h in range(HEADS):
                    for k in range(2):
                        nc.tensor.matmul(psS[:, 0, h * P:(h + 1) * P], WUQ[:, k, h * HW:h * HW + NOPE], cqT[:, k, tok],
                                         start=k == 0, stop=k == 1)
                for h in range(HEADS):
                    for k in range(2):
                        nc.tensor.matmul(psS[0:ROPE, 1, h * P:(h + 1) * P], WUQ[:, k, h * HW + NOPE:(h + 1) * HW], cqT[:, k, tok],
                                         start=k == 0, stop=k == 1)
                for h in range(HEADS):
                    for k in range(2):
                        last = nc.tensor.matmul(psS[0:ROPE, 2, h * P:(h + 1) * P], WUS[:, k, h * ROPE:(h + 1) * ROPE], cqT[:, k, tok],
                                                start=k == 0, stop=k == 1)
                last.then_inc(q_done, 1)
                pe.wait_ge(qn_out, t + 1)
                for h in range(HEADS):
                    last = nc.tensor.matmul(psS[:, 3, h * P:(h + 1) * P], WKT[:, h], QN[:, h], start=True, stop=True)
                last.then_inc(qp_done, 1)
                pe.wait_ge(qp_out, t + 1)
                pe.wait_ge(qr_out, t + 1)

            def score(t, h):
                g = t * HEADS + h
                for c, (a, z) in enumerate(chunks):
                    if h or not isinstance(t, int):
                        pe.wait_ge(exp_done, (g - 1) * NCH + c + 1)
                    nc.tensor.matmul(psS[:, c, 0:z - a], QP[:, h], ckvT[:, a:z], start=True, stop=False)
                    nc.tensor.matmul(psS[:, c, 0:z - a], QR_[:, h], krT[:, a:z], start=False, stop=True).then_inc(s_done, 1)

            def weigh(t, h):
                g = t * HEADS + h
                s = h % 2
                pe.wait_ge(exp_done, (g + 1) * NCH)
                for j in range(NG + 1):
                    if j < NG:
                        a, z = groups[j]
                        if j >= 2 or h or not isinstance(t, int):
                            pe.wait_ge(t_out, g * NG + j - 1)
                        for q in range(a, z):
                            last = nc.tensor.transpose(psT[:, (j + h) % 2, (q - a) * P:(q - a + 1) * P], PM[:, s, q * P:(q + 1) * P], ident[:, :])
                        last.then_inc(t_done, 1)
                    if j:
                        a, z = groups[j - 1]
                        pe.wait_ge(t_out, g * NG + j)
                        if j == 1 and (h or not isinstance(t, int)):
                            pe.wait_ge(av_out, g)
                        for q in range(a, z):
                            last = nc.tensor.matmul(psO[:, 0:P], ckv[:, q], PT[:, q], start=q == 0, stop=q == KT - 1)
                last.then_inc(pv_done, 1)
                pe.wait_ge(ol_out, g + 1)
                nc.tensor.matmul(psO[:, P:2 * P], OL[:, :], WV[:, h], start=True, stop=True).then_inc(av_done, 1)
            heads(pe, start, score, weigh)

        @block.scalar
        def _(act):
            act.wait_ge(const_in, NCONST)

            def start(t):
                act.wait_ge(q_done, t + 1)
                nc.scalar.activation(QN[:, :], psS[:, 0].rearrange("p (h n) -> p h n", h=HEADS), ACT.Copy).then_inc(qn_out, 1)
                act.wait_ge(qp_done, t + 1)
                nc.scalar.activation(QP[:, :], psS[:, 3].rearrange("p (h n) -> p h n", h=HEADS), ACT.Copy).then_inc(qp_out, 1)

            def score(t, h):
                g = t * HEADS + h
                s = h % 2
                act.wait_ge(neg_max, g + 1)
                for c, (a, z) in enumerate(chunks):
                    if c == 0 and (h >= 2 or not isinstance(t, int)):
                        act.wait_ge(pv_done, g - 1)
                    nc.scalar.activation(PM[:, s, a:z], psS[:, c, 0:z - a], ACT.Exp, bias=top[:, s, 1:2], scale=SCALE,
                                         accum_out=stat[:, s, 1, c:c + 1]).then_inc(exp_done, 1)

            def weigh(t, h):
                g = t * HEADS + h
                s = h % 2
                act.wait_ge(pv_done, g + 1)
                nc.scalar.activation(OL[:, :], psO[:, 0:P], ACT.Copy).then_inc(ol_out, 1)
                act.wait_ge(inv_done, g + 1)
                act.wait_ge(av_done, g + 1)
                if h == 0 and not isinstance(t, int):
                    act.wait_ge(m_out, t * 16)
                nc.scalar.activation(MX[:, h * DV:(h + 1) * DV], psO[:, P:2 * P], ACT.Copy, scale=top[:, s, 3:4]).then_inc(av_out, 1)
            heads(act, start, score, weigh)

        @block.vector
        def _(dve):
            dve.wait_ge(const_in, NCONST)

            def start(t):
                dve.wait_ge(q_done, t + 1)
                cos = RF[:, 0, bass.ds(t * P, P)]
                sin = RF[:, 1, bass.ds(t * P, P)]
                for h in range(HEADS):
                    nc.vector.tensor_tensor(QR_[:, h], psS[0:ROPE, 1, h * P:(h + 1) * P], cos, ALU.mult)
                    last = nc.vector.tensor_tensor(QT[:, h], psS[0:ROPE, 2, h * P:(h + 1) * P], sin, ALU.mult)
                last.then_inc(qr_part, 1)
                dve.wait_ge(qr_part, t + 1)
                nc.vector.tensor_tensor(QR_[:, :], QR_[:, :], QT[:, :], ALU.add).then_inc(qr_out, 1)

            def score(t, h):
                g = t * HEADS + h
                s = h % 2
                for c, (a, z) in enumerate(chunks):
                    dve.wait_ge(s_done, g * NCH + c + 1)
                    last = nc.vector.reduce_max(stat[:, s, 0, c:c + 1], psS[:, c, 0:z - a], AXX)
                last.then_inc(c_max, 1)
                dve.wait_ge(c_max, g + 1)
                nc.vector.reduce_max(top[:, s, 0:1], stat[:, s, 0, 0:NCH], AXX).then_inc(h_max, 1)
                dve.wait_ge(h_max, g + 1)
                nc.vector.tensor_scalar(top[:, s, 1:2], top[:, s, 0:1], -SCALE, None, ALU.mult).then_inc(neg_max, 1)

            def weigh(t, h):
                g = t * HEADS + h
                s = h % 2
                for j, (a, z) in enumerate(groups):
                    dve.wait_ge(t_done, g * NG + j + 1)
                    if j == 0 and (h or not isinstance(t, int)):
                        dve.wait_ge(pv_done, g)
                    nc.vector.tensor_copy(PT[:, a:z], psT[:, (j + h) % 2, 0:(z - a) * P].rearrange("p (k n) -> p k n", n=P)).then_inc(t_out, 1)
                    if j == 0:
                        dve.wait_ge(exp_done, (g + 1) * NCH)
                        nc.vector.reduce_sum(top[:, s, 2:3], stat[:, s, 1, 0:NCH], AXX).then_inc(sums, 1)
                        dve.wait_ge(sums, g + 1)
                        nc.vector.reciprocal(top[:, s, 3:4], top[:, s, 2:3]).then_inc(inv_done, 1)
            heads(dve, start, score, weigh)


def gla(nc, name, proj_d, w_gate, b_gate, cum_d, rest_d, mask_d, ident_d, o_d, backward):
    C = P // 2
    order = (1, 0) if backward else (0, 1)
    edge = [0, C] if backward else [C - 1, P - 1]
    QK = HEADS * DK
    pairs = NA // 2

    def place(n):
        if not backward:
            return n
        if isinstance(n, int):
            return NC - 1 - n if n < NC else NA - 1 - n + NC
        return (n * -1) + (NA - 1 + NC)

    def n_positive(i, s):
        return n_above(i, s, 0)

    def n_above(i, s, k):
        return not (isinstance(i, int) and i * 2 + s <= k)

    def static(i):
        return isinstance(i, int) and i == 0

    with ExitStack() as ctx:
        m = Memory(nc, ctx, name)
        X = m.sbuf("x", [P, 2, 2 * QK])
        Z = m.sbuf("z", [P, 2, 2 * RANK])
        V = m.sbuf("v", [P, 2, HEADS * DV])
        ZT = m.sbuf("zt", [2 * RANK + 1, 2, P])
        WG = m.sbuf("wg", [2 * RANK + 1, QK])
        NEG = m.sbuf("neg", [P, QK])
        AB = m.sbuf("ab", [P, QK])
        LA = m.sbuf("la", [P, 2, QK])
        EB = m.sbuf("eb", [P, 2, 2 * QK])
        EN = m.sbuf("en", [P, 2, QK])
        QT = m.sbuf("qt", [P, 2, QK])
        KT = m.sbuf("kt", [P, 2, QK])
        KH = m.sbuf("kh", [P, 2, QK])
        AT = m.sbuf("at", [P, HEADS, P])
        SA = m.sbuf("sa", [P, 2, DV])
        SB = m.sbuf("sb", [P, 2, DV])
        O = m.sbuf("o", [P, 2, HEADS * DV])
        CUM = m.sbuf("cum", [P, P])
        REST = m.sbuf("rest", [P, P])
        MASK = m.sbuf("mask", [P, 2, P], I32)
        ident = m.sbuf("ident", [P, P])
        one = m.sbuf("one", [P, 1])
        psU = m.psum("psU", [P, BANK])
        psB = m.psum("psB", [P, BANK])
        psQ = m.psum("psQ", [P, BANK])
        psAO = m.psum("psAO", [P, 2, BANK])
        psS = m.psum("psS", [P, 2, BANK])
        const_in, set_up, one_set = m.sem("const_in"), m.sem("set_up"), m.sem("one_set")
        x_in = [m.sem(f"x_in{s}") for s in range(2)]
        v_in = [m.sem(f"v_in{s}") for s in range(2)]
        passed = m.sem("passed")
        z_done = m.sem("z_done")
        z_out = m.sem("z_out")
        u_done = m.sem("u_done")
        neg = m.sem("neg")
        ab = m.sem("ab")
        ex = m.sem("ex")
        ln = m.sem("ln")
        la_done = m.sem("la_done")
        b_done = m.sem("b_done")
        qk_done = m.sem("qk_done")
        eb_done = m.sem("eb_done")
        scaled = m.sem("scaled")
        ds_done = m.sem("ds_done")
        at_done = m.sem("at_done")
        at_out = m.sem("at_out")
        o_first = m.sem("o_first")
        o_done = m.sem("o_done")
        sb_done = m.sem("sb_done")
        sa_done = m.sem("sa_done")
        o_out = m.sem("o_out")
        stored = [m.sem(f"stored{s}") for s in range(2)]
        block = ctx.enter_context(nc.Block())
        NCONST = 16 * 6

        @block.sync
        def _(sp):
            sp.dma_start(ident[:, :], ident_d).then_inc(const_in, 16)
            sp.dma_start(CUM[:, :], cum_d).then_inc(const_in, 16)
            sp.dma_start(REST[:, :], rest_d).then_inc(const_in, 16)
            sp.dma_start(MASK[:, :], mask_d).then_inc(const_in, 16)
            for s in range(2):
                sp.sem_inc(stored[s], 16)
            sp.wait_ge(set_up, 4)
            a = RANK if backward else 0
            sp.dma_start(WG[a:a + RANK, :], w_gate).then_inc(const_in, 16)
            sp.dma_start(WG[2 * RANK:2 * RANK + 1, :], b_gate).then_inc(const_in, 16)
            sp.wait_ge(const_in, NCONST)

            def load_x(i, s):
                n = i * 2 + s
                t = place(n)
                sp.wait_ge(scaled, n + 1)
                sp.wait_ge(const_in, NCONST)
                sp.dma_start(X[:, s], rows(proj_d[:, COL_Q:COL_V], t)).then_inc(x_in[s], 16)
                sp.dma_start(Z[:, s], rows(proj_d[:, COL_Z:COL_R], t)).then_inc(x_in[s], 16)

            def load_v(i, s):
                n = i * 2 + s
                t = place(n)
                if isinstance(i, int) and i == 1:
                    sp.wait_ge(ds_done, n - 1)
                sp.wait_ge(o_done, n + 1)
                sp.wait_ge(const_in, NCONST)
                sp.dma_start(V[:, s], rows(proj_d[:, COL_V:COL_Z], t)).then_inc(v_in[s], 16)

            def store(i, s):
                n = i * 2 + s
                if static(i):
                    return
                t = place(n)
                sp.wait_ge(o_out, n - NC + 1)
                sp.wait_ge(const_in, NCONST)
                sp.dma_start(rows(o_d, t + (-NC)), O[:, s]).then_inc(stored[s], 16)
            staged(sp, pairs, load_x, load_v, store, apart=2)
            for s in range(2):
                sp.wait_ge(stored[s], 16 * pairs)

        @block.gpsimd
        def _(pool):
            pool.memset(WG[:, :], 0.0).then_inc(set_up, 1)
            pool.wait_ge(set_up, 1)
            pool.memset(AT[:, :], 0.0).then_inc(set_up, 1)
            pool.wait_ge(set_up, 2)
            pool.memset(SA[:, :], 0.0).then_inc(set_up, 1)
            pool.wait_ge(set_up, 3)
            pool.memset(ZT[2 * RANK:2 * RANK + 1, :], 1.0).then_inc(set_up, 1)

        @block.tensor
        def _(pe):
            pe.sem_inc(b_done, 2)
            pe.sem_inc(o_done, 2 + NC)
            pe.wait_ge(const_in, NCONST)
            pe.wait_ge(set_up, 4)

            def early(i, s):
                n = i * 2 + s
                pe.wait_ge(x_in[s], i * 32 + 32)
                if n_positive(i, s):
                    pe.wait_ge(ab, n)
                    pe.wait_ge(neg, n)
                nc.tensor.transpose(psU[0:2 * RANK, QK:QK + P], Z[:, s], ident[:, :]).then_inc(z_done, 1)
                pe.wait_ge(z_out, n + 1)
                nc.tensor.matmul(psU[:, 0:QK], ZT[:, s], WG[:, :], start=True, stop=True).then_inc(u_done, 1)

            def front(i, s):
                n = i * 2 + s
                pe.wait_ge(la_done, n + 1)
                if n_positive(i, s):
                    pe.wait_ge(eb_done, n)
                for p in range(2):
                    nc.tensor.matmul(psB[:, p * P:(p + 1) * P], LA[:, s, p * P:(p + 1) * P], CUM[:, :], start=True, stop=True)
                nc.tensor.matmul(psB[:, QK:2 * QK], REST[:, :], LA[:, s], start=True, stop=True).then_inc(b_done, 1)
                if n_positive(i, s):
                    pe.wait_ge(scaled, n + 2)
                for p in range(4):
                    last = nc.tensor.transpose(psQ[:, p * P:(p + 1) * P], X[:, s, p * P:(p + 1) * P], ident[:, :])
                last.then_inc(qk_done, 1)

            def back(i, s):
                n = i * 2 + s
                pe.wait_ge(scaled, n + 3)
                pe.wait_ge(v_in[s], i * 16 + 16)
                if n_positive(i, s):
                    pe.wait_ge(sa_done, n + 2)
                for c in range(2):
                    for p in range(2):
                        last = nc.tensor.matmul(psS[:, c, p * 2 * DV:(p + 1) * 2 * DV], KH[c * C:(c + 1) * C, s, p * P:(p + 1) * P],
                                                V[c * C:(c + 1) * C, s, p * 2 * DV:(p + 1) * 2 * DV], start=True, stop=True)
                last.then_inc(ds_done, 1)
                if static(i):
                    return
                if n_above(i, s, NC):
                    pe.wait_ge(o_out, n - NC)
                for h in range(HEADS):
                    r, p = h % 2 * C, h // 2
                    last = nc.tensor.matmul(psAO[:, h % 2, 2 * DV + p * P:2 * DV + (p + 1) * P], KT[r:r + C, s, p * P:(p + 1) * P],
                                            QT[r:r + C, s, p * P:(p + 1) * P], start=True, stop=True)
                last.then_inc(at_done, 1)
                pe.wait_ge(at_out, n - NC + 1)
                for k, c in enumerate(order):
                    if k:
                        pe.wait_ge(sb_done, n + 1)
                        pe.sem_inc(passed, 1)
                    S = SB if k else SA
                    for h in range(HEADS):
                        r, p = h % 2 * C, h // 2
                        out = psAO[:, h % 2, p * DV:(p + 1) * DV]
                        if k == 0:
                            nc.tensor.matmul(out, AT[:, h], V[:, s, h * DV:(h + 1) * DV], start=h < 2, stop=False, skip_group_check=True)
                        last = nc.tensor.matmul(out[c * C:(c + 1) * C], QT[r:r + C, s, p * P + c * C:p * P + (c + 1) * C],
                                                S[r:r + C, p], start=False, stop=k == 1, skip_group_check=True)
                    last.then_inc(o_done if k else o_first, 1)
            staged(pe, pairs, early, front, back, apart=2)

        @block.scalar
        def _(act):
            act.wait_ge(set_up, 4)

            def early(i, s):
                n = i * 2 + s
                act.wait_ge(ab, n + 1)
                nc.scalar.activation(AB[:, :], AB[:, :], ACT.Exp).then_inc(ex, 1)
                act.wait_ge(ex, n + 1)
                act.wait_ge(one_set, 1)
                nc.scalar.activation(AB[:, :], AB[:, :], ACT.Ln, bias=one[:, 0:1]).then_inc(ln, 1)

            def front(i, s):
                n = i * 2 + s
                act.wait_ge(b_done, n + 3)
                act.wait_ge(sa_done, n + 1)
                act.wait_ge(scaled, n + 1)
                nc.scalar.activation(EB[:, s], psB[:, :], ACT.Exp)
                nc.scalar.activation(EN[:, s], psB[:, 0:QK], ACT.Exp, scale=-1.0).then_inc(eb_done, 1)

            def back(i, s):
                n = i * 2 + s
                if static(i):
                    return
                act.wait_ge(o_done, n + 3)
                act.wait_ge(stored[s], i * 16)
                nc.scalar.activation(O[:, s].rearrange("p (a b v) -> p b a v", a=2, b=2), psAO[:, :, 0:2 * DV].rearrange("p b (a v) -> p b a v", a=2),
                                     ACT.Copy).then_inc(o_out, 1)
            staged(act, pairs, early, front, back, apart=2)

        @block.vector
        def _(dve):
            dve.sem_inc(scaled, 2)
            dve.sem_inc(sa_done, 2)
            nc.vector.memset(one[:, :], 1.0).then_inc(one_set, 1)
            dve.wait_ge(const_in, NCONST)
            dve.wait_ge(set_up, 4)

            def early(i, s):
                n = i * 2 + s
                dve.wait_ge(z_done, n + 1)
                nc.vector.tensor_copy(ZT[0:2 * RANK, s], psU[0:2 * RANK, QK:QK + P]).then_inc(z_out, 1)
                dve.wait_ge(u_done, n + 1)
                nc.vector.tensor_scalar(NEG[:, :], psU[:, 0:QK], 0.0, None, ALU.min).then_inc(neg, 1)
                dve.wait_ge(neg, n + 1)
                nc.vector.scalar_tensor_tensor(AB[:, :], NEG[:, :], 2.0, psU[:, 0:QK], ALU.mult, ALU.subtract).then_inc(ab, 1)
                dve.wait_ge(ln, n + 1)
                dve.wait_ge(b_done, n + 1)
                nc.vector.tensor_tensor(LA[:, s], NEG[:, :], AB[:, :], ALU.subtract).then_inc(la_done, 1)

            def front(i, s):
                n = i * 2 + s
                dve.wait_ge(eb_done, n + 1)
                dve.wait_ge(qk_done, n + 1)
                if n_above(i, s, 1):
                    dve.wait_ge(ds_done, n - 1)
                dve.wait_ge(o_done, n + 1)
                nc.vector.scalar_tensor_tensor(QT[:, s], psQ[:, 0:QK], float(DK) ** -0.5, EB[:, s, 0:QK], ALU.mult, ALU.mult)
                nc.vector.tensor_tensor(KT[:, s], psQ[:, QK:2 * QK], EN[:, s], ALU.mult)
                nc.vector.tensor_tensor(KH[:, s], X[:, s, QK:2 * QK], EB[:, s, QK:2 * QK], ALU.mult).then_inc(scaled, 1)

            def back(i, s):
                n = i * 2 + s
                if not static(i):
                    dve.wait_ge(at_done, n - NC + 1)
                    dve.sem_inc(passed, 1)
                    for b in range(2):
                        at = AT[:, :].rearrange("p (a b) n -> p b a n", b=2)[:, b]
                        last = nc.vector.copy_predicated(at, MASK[:, :], psAO[:, b, 2 * DV:2 * DV + 2 * P].rearrange("p (a n) -> p a n", a=2))
                    last.then_inc(at_out, 1)
                dve.wait_ge(ds_done, n + 1)
                for k, c in enumerate(order):
                    old, new = (SB, SA) if k else (SA, SB)
                    if k:
                        dve.wait_ge(sb_done, n + 1)
                        if not static(i):
                            dve.wait_ge(o_first, n - NC + 1)
                    elif n_positive(i, s):
                        dve.wait_ge(sa_done, n + 2)
                        dve.wait_ge(o_done, n + 2)
                    for p in range(2):
                        for r in range(2):
                            q = slice(r * C, (r + 1) * C)
                            last = nc.vector.scalar_tensor_tensor(new[q, p], old[q, p], EB[q, s, p * P + edge[c]:p * P + edge[c] + 1],
                                                                  psS[q, c, (p * 2 + r) * DV:(p * 2 + r + 1) * DV], ALU.mult, ALU.add)
                    last.then_inc(sa_done if k else sb_done, 1)
            staged(dve, pairs, early, front, back, apart=2)

def gla_finish(nc, of_d, ob_d, proj_d, g, mix_d):
    pairs = NT // 2
    W = HEADS * DV
    with ExitStack() as ctx:
        m = Memory(nc, ctx, "gf")
        F = m.sbuf("f", [P, 2, W])
        B = m.sbuf("b", [P, 2, W])
        R = m.sbuf("r", [P, 2, W])
        S = m.sbuf("s", [P, 2, W])
        G = m.sbuf("g", [P, W])
        M = m.sbuf("m", [P, 2, W])
        junk = m.sbuf("junk", [P, W])
        stat = m.sbuf("stat", [P, 2, 3, HEADS])
        eps = m.sbuf("eps", [P, 1])
        const_in, eps_set = m.sem("const_in"), m.sem("eps_set")
        t_in = [m.sem(f"t_in{s}") for s in range(2)]
        summed = m.sem("summed")
        silu = m.sem("silu")
        squared = m.sem("squared")
        rooted = m.sem("rooted")
        gated = m.sem("gated")
        inverted = m.sem("inverted")
        done = m.sem("done")
        stored = [m.sem(f"stored{s}") for s in range(2)]
        block = ctx.enter_context(nc.Block())

        @block.sync
        def _(sp):
            for h in range(HEADS):
                sp.dma_start(G[:, h * DV:(h + 1) * DV], g.to_broadcast([P, DV])).then_inc(const_in, 16)
            sp.wait_ge(const_in, 16 * HEADS)
            for s in range(2):
                sp.sem_inc(stored[s], 16)

            def load(i, s):
                n = i * 2 + s
                sp.wait_ge(done, n + 1)
                sp.wait_ge(const_in, 16 * HEADS)
                sp.dma_start(F[:, s], rows(of_d, n)).then_inc(t_in[s], 16)
                sp.dma_start(B[:, s], rows(ob_d, n)).then_inc(t_in[s], 16)
                sp.dma_start(R[:, s], rows(proj_d[:, COL_R:COL_CQ], n + NC)).then_inc(t_in[s], 16)

            def store(i, s):
                n = i * 2 + s
                sp.wait_ge(done, n + 3)
                sp.wait_ge(const_in, 16 * HEADS)
                sp.dma_start(rows(mix_d[:, 0:W], n), M[:, s]).then_inc(stored[s], 16)
            staged(sp, pairs, load, nothing, store)
            for s in range(2):
                sp.wait_ge(stored[s], 16 * (pairs + 1))

        @block.scalar
        def _(act):
            act.wait_ge(eps_set, 1)

            def front(i, s):
                n = i * 2 + s
                act.wait_ge(summed, n + 1)
                for h in range(HEADS):
                    last = nc.scalar.activation(junk[:, h * DV:(h + 1) * DV], F[:, s, h * DV:(h + 1) * DV], ACT.Square,
                                                accum_out=stat[:, s, 0, h:h + 1])
                last.then_inc(squared, 1)
                act.wait_ge(squared, n + 1)
                nc.scalar.activation(stat[:, s, 1], stat[:, s, 0], ACT.Sqrt, bias=eps[:, 0:1], scale=1.0 / DV).then_inc(rooted, 1)
                nc.scalar.activation(S[:, s], R[:, s], ACT.Silu).then_inc(silu, 1)
            staged(act, pairs, nothing, front, nothing)

        @block.vector
        def _(dve):
            dve.sem_inc(done, 2)
            nc.vector.memset(eps[:, :], EPS).then_inc(eps_set, 1)
            dve.wait_ge(const_in, 16 * HEADS)

            def early(i, s):
                n = i * 2 + s
                dve.wait_ge(t_in[s], i * 48 + 48)
                nc.vector.tensor_tensor(F[:, s], F[:, s], B[:, s], ALU.add).then_inc(summed, 1)

            def front(i, s):
                n = i * 2 + s
                dve.wait_ge(silu, n + 1)
                nc.vector.tensor_tensor(S[:, s], S[:, s], G[:, :], ALU.mult).then_inc(gated, 1)
                nc.vector.reciprocal(stat[:, s, 2], stat[:, s, 1]).then_inc(inverted, 1)
                dve.wait_ge(gated, n + 1)
                dve.wait_ge(inverted, n + 1)
                dve.wait_ge(stored[s], i * 16 + 16)
                for h in range(HEADS):
                    q = slice(h * DV, (h + 1) * DV)
                    last = nc.vector.scalar_tensor_tensor(M[:, s, q], F[:, s, q], stat[:, s, 2, h:h + 1], S[:, s, q], ALU.mult, ALU.mult)
                last.then_inc(done, 1)
            staged(dve, pairs, early, front, nothing)


def fourier_channels(nc, hT_d, dft_d, alt_d, wa_d, wb_d, g_d):
    GR = 4
    NB = SEQ // BANK
    TB = BANK // P
    with ExitStack() as ctx:
        m = Memory(nc, ctx, "fc")
        H = m.sbuf("h", [P, 2, KD, BANK])
        AT = m.sbuf("at", [P, 2 * GR, BANK])
        AL = m.sbuf("al", [GR, BANK])
        DF = m.sbuf("df", [P, 2, 2, P])
        ALT = m.sbuf("alt", [P, KD, GR])
        WA = m.sbuf("wa", [P, GR, D])
        WB = m.sbuf("wb", [P, GR, D])
        WP = m.sbuf("wp", [P, GR, D])
        WM = m.sbuf("wm", [GR, D])
        sign = m.sbuf("sign", [P, 2])
        O = m.sbuf("o", [P, 2, 2, D])
        psA = m.psum("psA", [P, 2, BANK])
        psL = m.psum("psL", [P, BANK])
        psG = m.psum("psG", [P, 4, BANK])
        const_in, folded, set_up = m.sem("const_in"), m.sem("folded"), m.sem("set_up")
        h_in = [m.sem(f"h_in{s}") for s in range(2)]
        a_done = m.sem("a_done")
        a_out = m.sem("a_out")
        al_done, al_out = m.sem("al_done"), m.sem("al_out")
        g_done = m.sem("g_done")
        g_out = m.sem("g_out")
        stored = [m.sem(f"stored{s}") for s in range(2)]
        block = ctx.enter_context(nc.Block())

        @block.sync
        def _(sp):
            sp.dma_start(DF[:, :], dft_d).then_inc(const_in, 16)
            sp.dma_start(ALT[:, :], alt_d).then_inc(const_in, 16)
            sp.dma_start(WA[:, :], wa_d).then_inc(const_in, 16)
            sp.dma_start(WB[:, :], wb_d).then_inc(const_in, 16)
            sp.dma_start(WM[:, :], wb_d[0]).then_inc(const_in, 16)
            for s in range(2):
                sp.sem_inc(stored[s], 16)
            sp.wait_ge(const_in, 80)
            for s in range(2):
                sp.dma_start(H[:, s], hT_d[:, :, s * BANK:(s + 1) * BANK]).then_inc(h_in[s], 16)
            gv = g_d.rearrange("c (t p) n -> t p c n", p=P)
            for b in range(NB):
                for t in range(TB):
                    n = b * TB + t
                    sp.wait_ge(g_out, (n + 1) * 4)
                    sp.dma_start(gv[n], O[:, n % 2]).then_inc(stored[n % 2], 16)
                    if t == 0 and 1 <= b < NB - 1:
                        sp.dma_start(H[:, (b + 1) % 2], hT_d[:, :, (b + 1) * BANK:(b + 2) * BANK]).then_inc(h_in[(b + 1) % 2], 16)
            for s in range(2):
                sp.wait_ge(stored[s], 16 * (NT // 2 + 1))

        @block.tensor
        def _(pe):
            pe.wait_ge(const_in, 80)
            pe.wait_ge(folded, 2)
            for b in range(NB):
                s = b % 2
                pe.wait_ge(h_in[s], 16 * (b // 2 + 1))
                for q in range(2 * GR):
                    g, j = q // 2, q % 2
                    if b * 2 * GR + q >= 2:
                        pe.wait_ge(a_out, b * 2 * GR + q - 1)
                    for k in range(2):
                        last = nc.tensor.matmul(psA[:, q % 2], DF[:, k, j], H[:, s, 2 * g + k], start=k == 0, stop=k == 1)
                    last.then_inc(a_done, 1)
                if b:
                    pe.wait_ge(al_out, b)
                for k in range(KD):
                    last = nc.tensor.matmul(psL[0:GR, :], ALT[:, k], H[:, s, k], start=k == 0, stop=k == KD - 1)
                last.then_inc(al_done, 1)
                pe.wait_ge(a_out, (b + 1) * 2 * GR)
                pe.wait_ge(al_out, b + 1)
                for t in range(TB):
                    for c in range(2):
                        for h in range(2):
                            n = (b * TB + t) * 4 + c * 2 + h
                            if n >= 4:
                                pe.wait_ge(g_out, n - 3)
                            W = (WP, WA)[c]
                            for g in range(GR):
                                last = nc.tensor.matmul(psG[:, n % 4], AT[:, 2 * g + c, t * P:(t + 1) * P], W[:, g, h * BANK:(h + 1) * BANK],
                                                        start=g == 0, stop=c == 1 and g == GR - 1)
                            if c == 0:
                                last = nc.tensor.matmul(psG[:, n % 4], AL[:, t * P:(t + 1) * P], WM[:, h * BANK:(h + 1) * BANK],
                                                        start=False, stop=True)
                            last.then_inc(g_done, 1)

        @block.scalar
        def _(act):
            for b in range(NB):
                act.wait_ge(al_done, b + 1)
                nc.scalar.activation(AL[:, :], psL[0:GR, :], ACT.Copy).then_inc(al_out, 1)
                for t in range(TB):
                    i = b * TB + t
                    act.wait_ge(stored[i % 2], 16 * (i // 2 + 1))
                    for c in range(2):
                        for h in range(2):
                            n = i * 4 + c * 2 + h
                            act.wait_ge(g_done, n + 1)
                            nc.scalar.activation(O[:, i % 2, c, h * BANK:(h + 1) * BANK], psG[:, n % 4], ACT.Copy).then_inc(g_out, 1)

        @block.vector
        def _(dve):
            nc.vector.memset(sign[:, 0:1], 1.0).then_inc(set_up, 1)
            nc.vector.memset(sign[:, 1:2], -1.0).then_inc(set_up, 1)
            dve.wait_ge(set_up, 2)
            nc.vector.memset(sign[0:1, :], 0.0).then_inc(set_up, 1)
            dve.wait_ge(const_in, 80)
            dve.wait_ge(set_up, 3)
            nc.vector.scalar_tensor_tensor(WP[:, :], WB[:, :], sign[:, 0:1], WA[:, :], ALU.mult, ALU.add).then_inc(folded, 1)
            dve.wait_ge(folded, 1)
            nc.vector.scalar_tensor_tensor(WA[:, :], WB[:, :], sign[:, 1:2], WA[:, :], ALU.mult, ALU.add).then_inc(folded, 1)
            for b in range(NB):
                for q in range(2 * GR):
                    n = b * 2 * GR + q
                    dve.wait_ge(a_done, n + 1)
                    nc.vector.tensor_copy(AT[:, q], psA[:, q % 2]).then_inc(a_out, 1)


def fourier_tokens(nc, g_d, tw_d, y_d):
    J = 4
    TQ = NT // J
    with ExitStack() as ctx:
        m = Memory(nc, ctx, "ft")
        bufs = [m.sbuf(f"g{i}", [P, 2, J, TQ, BANK]) for i in range(2)]
        TW = m.sbuf("tw", [P, 2, TQ, 2, P])
        O = m.sbuf("o", [P, 2, BANK])
        psY = m.psum("psY", [P, 2, BANK])
        g_in = m.sem("g_in")
        v_step, p_step = m.sem("v_step"), m.sem("p_step")
        tw_in = [m.sem(f"tw_in{s}") for s in range(2)]
        y_done = m.sem("y_done")
        y_out = m.sem("y_out")
        half = m.sem("half")
        stored = [m.sem(f"stored{s}") for s in range(2)]
        block = ctx.enter_context(nc.Block())
        PER = J * TQ
        yv = y_d.rearrange("(k p r) n -> r k p n", p=P, r=J)
        twv = tw_d
        gv = g_d.rearrange("c (j t p) n -> p c j t n", p=P, t=TQ)

        def buffers(h):
            return (bufs[0], bufs[1]) if h == 0 else (bufs[1], bufs[0])

        def first(h, c, j):
            X, Y = buffers(h)
            return ((Y[:, c, j], X[:, c, j], X[:, c, j + 2], ALU.add),
                    (Y[:, c, j + 2], X[:, c, j], X[:, c, j + 2], ALU.subtract))

        def second(h):
            X, Y = buffers(h)
            even = [(X[:, c, r], Y[:, c, 0], Y[:, c, 1], op) for c in range(2) for r, op in ((0, ALU.add), (2, ALU.subtract))]
            odd = [(X[:, 0, 1], Y[:, 0, 2], Y[:, 1, 3], ALU.subtract), (X[:, 1, 1], Y[:, 1, 2], Y[:, 0, 3], ALU.add),
                   (X[:, 0, 3], Y[:, 0, 2], Y[:, 1, 3], ALU.add), (X[:, 1, 3], Y[:, 1, 2], Y[:, 0, 3], ALU.subtract)]
            return even, odd

        @block.sync
        def _(sp):
            for s in range(2):
                sp.sem_inc(stored[s], 16)
            for h in range(2):
                if h:
                    sp.wait_ge(v_step, 12)
                    sp.wait_ge(p_step, 4)
                for c in range(2):
                    for j in range(J):
                        sp.dma_start(buffers(h)[0][:, c, j], gv[:, c, j, :, h * BANK:(h + 1) * BANK]).then_inc(g_in, 16)
                with sp.Fori(0, J) as r:
                    for k in range(TQ):
                        s = k % 2
                        n = r * TQ + (h * PER + k)
                        sp.wait_ge(y_done, n + 1)
                        sp.wait_ge(g_in, 128 * (h + 1))
                        sp.dma_start(TW[:, s], twv[bass.ds(r, 1), k].rearrange("a p t c n -> p (a t) c n")).then_inc(tw_in[s], 16)
                        sp.wait_ge(y_out, n + 3)
                        sp.wait_ge(g_in, 128 * (h + 1))
                        sp.dma_start(yv[bass.ds(r, 1), k, :, h * BANK:(h + 1) * BANK].rearrange("a p n -> p (a n)"), O[:, s]).then_inc(stored[s], 16)
            for s in range(2):
                sp.wait_ge(stored[s], 16 * (PER + 1))

        @block.gpsimd
        def _(pool):
            for h in range(2):
                pool.wait_ge(g_in, 128 * (h + 1))
                if h:
                    pool.wait_ge(y_done, 2 + PER)
                for out, a, b, op in first(h, 1, 1):
                    nc.gpsimd.tensor_tensor(out, a, b, op).then_inc(p_step, 1)
                pool.wait_ge(v_step, h * 12 + 6)
                pool.wait_ge(p_step, h * 4 + 2)
                for out, a, b, op in second(h)[1][2:]:
                    nc.gpsimd.tensor_tensor(out, a, b, op).then_inc(p_step, 1)

        @block.vector
        def _(dve):
            for h in range(2):
                dve.wait_ge(g_in, 128 * (h + 1))
                if h:
                    dve.wait_ge(y_done, 2 + PER)
                for c, j in ((0, 0), (0, 1), (1, 0)):
                    for out, a, b, op in first(h, c, j):
                        nc.vector.tensor_tensor(out, a, b, op).then_inc(v_step, 1)
                dve.wait_ge(v_step, h * 12 + 6)
                dve.wait_ge(p_step, h * 4 + 2)
                even, odd = second(h)
                for out, a, b, op in even + odd[:2]:
                    nc.vector.tensor_tensor(out, a, b, op).then_inc(v_step, 1)

        @block.tensor
        def _(pe):
            pe.sem_inc(y_done, 2)
            for h in range(2):
                X = buffers(h)[0]
                pe.wait_ge(v_step, (h + 1) * 12)
                pe.wait_ge(p_step, (h + 1) * 4)
                with pe.Fori(0, J) as r:
                    for k in range(TQ):
                        s = k % 2
                        n = r * TQ + (h * PER + k)
                        pe.wait_ge(tw_in[s], (r * (TQ // 2) + (h * PER // 2 + k // 2 + 1)) * 16)
                        pe.wait_ge(y_out, n + 1)
                        for t in range(TQ):
                            for c in range(2):
                                last = nc.tensor.matmul(psY[:, s], TW[:, s, t, c], X[:, c, bass.ds(r, 1), t].rearrange("p a n -> p (a n)"),
                                                        start=t == 0 and c == 0, stop=t == TQ - 1 and c == 1)
                        last.then_inc(y_done, 1)

        @block.scalar
        def _(act):
            act.sem_inc(y_out, 2)
            with act.Fori(0, 2 * PER // 2) as i:
                for s in range(2):
                    n = i * 2 + s
                    act.wait_ge(y_done, n + 3)
                    act.wait_ge(stored[s], i * 16 + 16)
                    nc.scalar.activation(O[:, s], psY[:, s], ACT.Copy).then_inc(y_out, 1)


def router(nc, hT_d, w_router, iota_d, ident_d, gates_d):
    NE = w_router.shape[1]
    NB = SEQ // BANK
    with ExitStack() as ctx:
        m = Memory(nc, ctx, "rt")
        H = m.sbuf("h", [P, 2, KD, BANK])
        W = m.sbuf("w", [P, KD, NE])
        LT = m.sbuf("lt", [NE, SEQ])
        L = m.sbuf("l", [P, NT, NE])
        TOP = m.sbuf("top", [P, NT, 8])
        IX = m.sbuf("ix", [P, NT, 8], U32)
        IF = m.sbuf("if", [P, NT, 8])
        GG = m.sbuf("gg", [P, 4, NT])
        IO = m.sbuf("io", [P, NE])
        ON = m.sbuf("on", [P, NT, NE])
        O2 = m.sbuf("o2", [P, NT, NE])
        ident = m.sbuf("ident", [P, P])
        psL = m.psum("psL", [P, 2, BANK])
        psT = m.psum("psT", [P, BANK])
        const_in = m.sem("const_in")
        h_in = [m.sem(f"h_in{s}") for s in range(2)]
        l_done, l_out, t_done, chain, ex, stored = (m.sem(n) for n in ("l_done", "l_out", "t_done", "chain", "ex", "stored"))
        block = ctx.enter_context(nc.Block())

        @block.sync
        def _(sp):
            sp.dma_start(W[:, :], w_router.rearrange("(k p) e -> p k e", p=P)).then_inc(const_in, 16)
            sp.dma_start(ident[:, :], ident_d).then_inc(const_in, 16)
            sp.dma_start(IO[:, :], iota_d.to_broadcast([P, NE])).then_inc(const_in, 16)
            for b in range(NB):
                if b >= 2:
                    sp.wait_ge(l_done, b - 1)
                sp.dma_start(H[:, b % 2], hT_d[:, :, b * BANK:(b + 1) * BANK]).then_inc(h_in[b % 2], 16)
            sp.wait_ge(chain, 7)
            sp.dma_start(gates_d, ON[:, :]).then_inc(stored, 16)
            sp.wait_ge(stored, 16)

        @block.tensor
        def _(pe):
            pe.wait_ge(const_in, 48)
            for b in range(NB):
                pe.wait_ge(h_in[b % 2], 16 * (b // 2 + 1))
                if b >= 2:
                    pe.wait_ge(l_out, b - 1)
                for k in range(KD):
                    last = nc.tensor.matmul(psL[0:NE, b % 2], W[:, k], H[:, b % 2, k], start=k == 0, stop=k == KD - 1)
                last.then_inc(l_done, 1)
            pe.wait_ge(l_out, NB)
            for t in range(NT):
                last = nc.tensor.transpose(psT[:, t * NE:(t + 1) * NE], LT[:, t * P:(t + 1) * P], ident[0:NE, 0:NE])
            last.then_inc(t_done, 1)

        @block.scalar
        def _(act):
            act.wait_ge(chain, 3)
            nc.scalar.activation(GG[:, 1], GG[:, 0], ACT.Exp).then_inc(ex, 1)

        @block.vector
        def _(dve):
            for b in range(NB):
                dve.wait_ge(l_done, b + 1)
                nc.vector.tensor_copy(LT[:, b * BANK:(b + 1) * BANK], psL[0:NE, b % 2]).then_inc(l_out, 1)
            dve.wait_ge(t_done, 1)
            nc.vector.tensor_copy(L[:, :], psT[:, 0:NT * NE].rearrange("p (t e) -> p t e", t=NT)).then_inc(chain, 1)
            dve.wait_ge(chain, 1)
            for t in range(NT):
                last = nc.vector.max(TOP[:, t], L[:, t])
            last.then_inc(chain, 1)
            dve.wait_ge(chain, 2)
            for t in range(NT):
                last = nc.vector.max_index(IX[:, t], TOP[:, t], L[:, t])
            nc.vector.tensor_tensor(GG[:, 0], TOP[:, :, 1], TOP[:, :, 0], ALU.subtract).then_inc(chain, 1)
            dve.wait_ge(ex, 1)
            nc.vector.tensor_scalar(GG[:, 2], GG[:, 1], 1.0, None, ALU.add)
            nc.vector.tensor_copy(IF[:, :], IX[:, :]).then_inc(chain, 1)
            dve.wait_ge(chain, 4)
            nc.vector.reciprocal(GG[:, 2], GG[:, 2]).then_inc(chain, 1)
            dve.wait_ge(chain, 5)
            nc.vector.tensor_tensor(GG[:, 3], GG[:, 1], GG[:, 2], ALU.mult).then_inc(chain, 1)
            dve.wait_ge(const_in, 48)
            dve.wait_ge(chain, 6)
            for t in range(NT):
                nc.vector.tensor_scalar(ON[:, t], IO[:, :], IF[:, t, 0:1], GG[:, 2, t:t + 1], ALU.is_equal, ALU.mult)
                last = nc.vector.tensor_scalar(O2[:, t], IO[:, :], IF[:, t, 1:2], GG[:, 3, t:t + 1], ALU.is_equal, ALU.mult)
            last.then_inc(ex, 1)
            dve.wait_ge(ex, 2)
            nc.vector.tensor_tensor(ON[:, :], ON[:, :], O2[:, :], ALU.add).then_inc(chain, 1)


def build(nc, a, out):
    def scratch(name, shape):
        return nc.dram_tensor(name, shape, F32).ap()
    cols = scratch("cols", [2, 2, P, 2, 2, KD])
    gate = scratch("gate", [2, 2, D])
    proj = scratch("proj", [NA * P, D_IN])
    of, ob = scratch("of", [SEQ, HEADS * DV]), scratch("ob", [SEQ, HEADS * DV])
    mix = scratch("mix", [SEQ, D])
    y = [scratch(f"y{i}", [SEQ, D]) for i in range(4)]
    x = [a["x"]] + [scratch(f"x{i}", [SEQ, D]) for i in range(1, 4)] + [out]
    hT = [scratch(f"ht{i}", [P, KD, SEQ]) for i in range(3)]
    g = scratch("g", [2, SEQ, D])
    gates = scratch("gates", [P, NT, 8])
    ident = a["ident"]

    modulation(nc, a["cc"], a["w_mod"], a["b_mod"], a["g_mix_pre"], a["g_ffn_pre"], a["g_mix_post"], a["g_ffn_post"], ident, cols, gate)
    project(nc, "ip", a["xall"], NA, cols[0, 0, :, 0], cols[0, 0, :, 1], a["e_w_in"], D_IN, proj, ident)
    gla(nc, "gb", proj, a["e_w_gate_b"], a["e_b_gate_b"], a["cum_b"], a["rest_b"], a["mask_b"], ident, ob, True)
    gla(nc, "gf", proj, a["e_w_gate_f"], a["e_b_gate_f"], a["cum_f"], a["rest_f"], a["mask_f"], ident, of, False)
    gla_finish(nc, of, ob, proj, a["e_gla_norm"], mix)
    with ExitStack() as ctx:
        m = Memory(nc, ctx, "mla")
        ckvT, krT, ckv = m.sbuf("ckvT", [P, NA * P]), m.sbuf("krT", [ROPE, NA * P]), m.sbuf("ckv", [P, NA, P])
        cqT = m.sbuf("cqT", [P, 2, NA * P])
        mla_prepare(nc, proj, a["q_norm"], a["e_kv_norm"], a["rope_tok"], ident, ckvT, krT, ckv, cqT)
        mla_attend(nc, a["e_w_uq"], a["w_uq_swapped"], a["w_ukT"], a["e_w_ukv"], a["rope_feat"], ident, ckvT, krT, ckv, cqT, mix)
    project(nc, "op", mix, NT, None, None, a["e_w_o"], D, y[0], ident)
    residual(nc, "r0", y[0], x[0], x[1], gate[0, 0], cols[0, 1, :, 0], hT[0], ident)
    swiglu(nc, "fd", hT[0], a["e_w1"], a["e_w3"], a["e_w2"], None, y[1])
    residual(nc, "r1", y[1], x[1], x[2], gate[0, 1], cols[1, 0, :, 0], hT[1], ident)
    fourier_channels(nc, hT[1], a["dft"], a["alt"], a["w_fold_a"], a["w_fold_b"], g)
    fourier_tokens(nc, g, a["twiddle"], y[2])
    residual(nc, "r2", y[2], x[2], x[3], gate[1, 0], cols[1, 1, :, 0], hT[2], ident)
    router(nc, hT[2], a["o_w_router"], a["iota8"], ident, gates)
    swiglu(nc, "fe", hT[2], a["o_w1"], a["o_w3"], a["o_w2"], gates, y[3])
    residual(nc, "r3", y[3], x[3], x[4], gate[1, 1], None, None, ident)


def constants():
    f = np.float32
    c = {"ident": np.eye(P, dtype=f), "iota8": np.arange(8, dtype=f)[None]}
    half = ROPE // 2
    inv = 1.0 / (10000.0 ** (np.arange(0, half, 2, dtype=f) / f(half)))
    tok = np.arange(SEQ)
    ang = np.concatenate([(tok // GRID_W)[:, None].astype(f) * inv, (tok % GRID_W)[:, None].astype(f) * inv], -1).astype(f)
    cos, sin = np.cos(ang), np.sin(ang)
    q = half // 2
    C = np.concatenate([cos[:, :q], cos[:, :q], cos[:, q:], cos[:, q:]], 1).astype(f)
    S = np.concatenate([-sin[:, :q], sin[:, :q], -sin[:, q:], sin[:, q:]], 1).astype(f)
    c["rope_feat"] = np.ascontiguousarray(np.stack([C.T, S.T], 1))
    c["rope_tok"] = np.stack([np.concatenate([np.ones((CTX, ROPE), f), C]), np.concatenate([np.zeros((CTX, ROPE), f), S])], 1)
    j, i = np.arange(P)[:, None], np.arange(P)[None]
    same = j // 64 == i // 64
    for d, upto, after in (("f", j <= i, j > i), ("b", j >= i, j < i)):
        c[f"cum_{d}"] = (same & upto).astype(f) / f(16)
        c[f"rest_{d}"] = (same & after).astype(f) / f(16)
        c[f"mask_{d}"] = np.repeat((same & upto).astype(np.int32)[:, None], 2, 1)
    GW = D // 4
    norm = 1.0 / np.sqrt(float(SEQ * GW))
    n, m = np.arange(GW)[:, None], np.arange(P)[None]
    dft = np.stack([np.cos(2 * np.pi * (n * m % GW) / GW), np.sin(2 * np.pi * (n * m % GW) / GW)], 1) * norm
    dft[:, 1, 0] = 0.0
    c["dft"] = np.ascontiguousarray(dft.reshape(2, P, 2, P).transpose(1, 0, 2, 3)).astype(f)
    alt = np.zeros((P, KD, 4))
    for k in range(KD):
        alt[:, k, k // 2] = norm * (1 - 2 * (np.arange(P) % 2))
    c["alt"] = alt.astype(f)
    r, kk, nn = np.arange(4)[:, None, None], np.arange(SEQ // 4)[None, :, None], np.arange(SEQ // 4)[None, None]
    ang = 2 * np.pi * ((4 * kk + r) * nn % SEQ) / SEQ
    tw = np.stack([np.cos(ang), -np.sin(ang)])
    tw = tw.reshape(2, 4, 4, P, 4, P).transpose(1, 2, 5, 4, 0, 3)
    c["twiddle"] = np.ascontiguousarray(tw).astype(f)
    return c


def kernel(**inputs):
    import concourse.bacc as bacc
    from concourse.bass_utils import run_bass_kernel_spmd as run

    v = {k: np.asarray(t) for k, t in inputs.items()}
    a = {k: v[k] for k in ("w_mod", "b_mod", "g_mix_pre", "g_mix_post", "g_ffn_pre", "g_ffn_post")}
    for k in ("e_w_in", "e_w_gate_f", "e_w_gate_b", "e_w_uq", "e_w_ukv", "e_w_o", "o_w_router", "o_w1", "o_w3", "o_w2"):
        a[k] = v[k][0]
    for k in ("e_b_gate_f", "e_b_gate_b", "e_gla_norm", "e_kv_norm", "e_w1", "e_w3", "e_w2"):
        a[k] = v[k]
    a["x"] = v["x"][0]
    a["xall"] = np.concatenate([v["ctx"][0], v["x"][0]], 0)
    a["cc"] = np.stack([v["c"][0], v["c_ctx"]])
    a["q_norm"] = v["e_q_norm"].reshape(2, P).T
    swap = np.arange(ROPE).reshape(2, 2, ROPE // 4)[:, ::-1].reshape(-1)
    a["w_uq_swapped"] = v["e_w_uq"][0].reshape(QR, HEADS, NOPE + ROPE)[:, :, NOPE:][:, :, swap].reshape(QR, HEADS * ROPE)
    a["w_ukT"] = v["e_w_ukv"][0].reshape(KVR, HEADS, NOPE + DV)[:, :, :NOPE].transpose(2, 1, 0)
    wo = v["o_w_o"][0].reshape(4, D // 4, D)
    partner = np.concatenate([[P], 2 * P - np.arange(1, P)])
    a["w_fold_a"] = wo[:, :P].transpose(1, 0, 2)
    a["w_fold_b"] = wo[:, partner].transpose(1, 0, 2)
    a.update(constants())

    nc = bacc.Bacc("TRN2", target_bir_lowering=False, num_devices=1)
    arrays, aps = {}, {}
    for name, t in a.items():
        arrays[f"in_{name}"] = np.ascontiguousarray(t)
        aps[name] = nc.dram_tensor(f"in_{name}", t.shape, mybir.dt.from_np(t.dtype), kind="ExternalInput").ap()
    out = nc.dram_tensor("out", [SEQ, D], F32, kind="ExternalOutput").ap()
    build(nc, aps, out)
    r = run(nc, [arrays], core_ids=[0])
    return r.results[0]["out"].reshape(1, SEQ, D)
```

```python
from contextlib import ExitStack

import numpy as np

import concourse.bass as bass
from concourse import mybir

F32 = mybir.dt.float32
U32 = mybir.dt.uint32
I32 = mybir.dt.int32
ALU = mybir.AluOpType
ACT = mybir.ActivationFunctionType
AXX = mybir.AxisListType.X

P = 128
BANK = 512
D = 1024
KD = D // P
SEQ = 2048
CTX = 256
NT = SEQ // P
NC = CTX // P
NA = NT + NC
EPS = 1e-6

HEADS = 4
DK, DV = 64, 128
RANK = 16
QR, KVR, ROPE, NOPE = 256, 128, 64, 128
D_IN = 2016
COL_Q, COL_K, COL_V, COL_Z, COL_R, COL_CQ, COL_CKV, COL_KR = 0, 256, 512, 1024, 1056, 1568, 1824, 1952
GRID_W = 64


class Memory:

    def __init__(self, nc, ctx, name):
        self.nc, self.ctx, self.name = nc, ctx, name
        self.numbers = []
        ctx.callback(self.zero)

    def zero(self):
        while self.numbers:
            first = self.numbers.pop(0)
            end = first + 1
            while self.numbers and self.numbers[0] == end:
                end += 1
                self.numbers.pop(0)
            self.nc.all_engine_barrier(sems_to_clear=range(first, end))

    def sbuf(self, name, shape, dt=F32):
        return self.ctx.enter_context(self.nc.sbuf_tensor(f"{self.name}_{name}", shape, dt))

    def psum(self, name, shape, dt=F32):
        return self.ctx.enter_context(self.nc.psum_tensor(f"{self.name}_{name}", shape, dt))

    def sem(self, name):
        handle = self.ctx.enter_context(self.nc.semaphore(f"{self.name}_{name}"))
        self.numbers.append(handle.num)
        return handle

    def software_sem(self, name):
        return self.nc.alloc_semaphore(f"{self.name}_{name}")


def rows(ap, t):
    return ap.rearrange("(t p) n -> t p n", p=P)[bass.ds(t, 1)].rearrange("a p n -> p (a n)")


def modulation(nc, cc, w_mod, b_mod, g_mix_pre, g_ffn_pre, g_mix_post, g_ffn_post, ident_d, cols_d, gate_d):
    NB = 12
    with ExitStack() as ctx:
        m = Memory(nc, ctx, "mod")
        W = m.sbuf("w", [P, 3, KD, BANK])
        ident = m.sbuf("ident", [P, P])
        vec = m.sbuf("vec", [P, P])
        vecT = m.sbuf("vecT", [P, P])
        cin = m.sbuf("cin", [2 * KD, P])
        cT = m.sbuf("cT", [P, 2 * KD])
        ce = m.sbuf("ce", [P, 2 * KD])
        sil = m.sbuf("sil", [P, KD, 2])
        brow = m.sbuf("brow", [1, 2, 2, D])
        grow = m.sbuf("grow", [1, 2, 2, D])
        orow = m.sbuf("orow", [1, 2, D])
        ocol = m.sbuf("ocol", [P, 2, 2, 2, KD])
        psc = m.psum("psc", [P, 2, BANK])
        psr = m.psum("psr", [P, 2, 2, BANK])
        pst = m.psum("pst", [P, BANK])
        small_in, t_done, t_copied, c_exp, c_one, c_rec, sil_done = (
            m.sem(n) for n in ("small_in", "t_done", "t_copied", "c_exp", "c_one", "c_rec", "sil_done"))
        w_in = [m.sem(f"w_in{s}") for s in range(3)]
        w_used, half_read, stored, step = (m.sem(n) for n in ("w_used", "half_read", "stored", "step"))
        wv = w_mod.rearrange("l (k p) (b n) -> l b p k n", p=P, n=BANK)
        block = ctx.enter_context(nc.Block())

        def put(sp, u):
            sp.wait_ge(half_read, u + 1)
            if u:
                sp.wait_ge(stored, 32 * u)
            sp.dma_start(cols_d[u // 2, u % 2], ocol[:, u % 2]).then_inc(stored, 16)
            sp.dma_start(gate_d[u // 2, u % 2:u % 2 + 1], orow[:, u % 2]).then_inc(stored, 16)

        @block.sync
        def _(sp):
            sp.dma_start(ident[:, :], ident_d).then_inc(small_in, 16)
            sp.dma_start(vec[0:96, :], b_mod.rearrange("l (n p) -> (l n) p", p=P)).then_inc(small_in, 16)
            sp.dma_start(vec[96:112, :], g_mix_pre.rearrange("l (n p) -> (l n) p", p=P)).then_inc(small_in, 16)
            sp.dma_start(vec[112:128, :], g_ffn_pre.rearrange("l (n p) -> (l n) p", p=P)).then_inc(small_in, 16)
            sp.dma_start(cin[:, :], cc.rearrange("c (n p) -> (c n) p", p=P)).then_inc(small_in, 16)
            bv = b_mod.rearrange("(a l) (h s n) -> a l h s n", a=1, h=2, s=3)
            for l in range(2):
                sp.dma_start(brow[:, l], bv[:, l, :, 2]).then_inc(small_in, 16)
                sp.dma_start(grow[:, l, 0], g_mix_post[l:l + 1]).then_inc(small_in, 16)
                sp.dma_start(grow[:, l, 1], g_ffn_post[l:l + 1]).then_inc(small_in, 16)
            for l in range(2):
                for b in range(NB):
                    n = l * NB + b
                    if n >= 3:
                        sp.wait_ge(w_used, n - 2)
                    sp.dma_start(W[:, n % 3], wv[l, b]).then_inc(w_in[n % 3], 16)
                    if b % 6 == 5 and n > 6:
                        put(sp, l * 2 + b // 6 - 1)
            put(sp, 3)
            sp.wait_ge(stored, 4 * 32)

        @block.tensor
        def _(pe):
            pe.wait_ge(small_in, 16 * 11)
            nc.tensor.transpose(pst[:, 0:P], vec[:, :], ident[:, :])
            nc.tensor.transpose(pst[:, P:P + 16], cin[:, :], ident[0:16, 0:16]).then_inc(t_done, 1)
            pe.wait_ge(sil_done, 1)
            for l in range(2):
                for b in range(NB):
                    n, h, seg = l * NB + b, b // 6, b % 6 // 2
                    if b % 6 == 0 and l:
                        pe.wait_ge(half_read, (l - 1) * 2 + h + 1)
                    pe.wait_ge(w_in[n % 3], 16 * (n // 3 + 1))
                    if seg < 2:
                        for q in range(4):
                            at = (seg * KD + b % 2 * 4 + q) * 2
                            for k in range(KD):
                                last = nc.tensor.matmul(psc[:, h, at:at + 2], W[:, n % 3, k, q * P:(q + 1) * P],
                                                        sil[:, k], start=k == 0, stop=k == KD - 1)
                    else:
                        for k in range(KD):
                            last = nc.tensor.matmul(psr[0:2, h, b % 2], sil[:, k], W[:, n % 3, k],
                                                    start=k == 0, stop=k == KD - 1)
                    last.then_inc(w_used, 1)

        @block.scalar
        def _(act):
            act.wait_ge(t_copied, 1)
            nc.scalar.activation(ce[:, :], cT[:, :], ACT.Exp, scale=-1.0).then_inc(c_exp, 1)

        @block.vector
        def _(dve):
            dve.wait_ge(t_done, 1)
            nc.vector.tensor_copy(vecT[:, :], pst[:, 0:P])
            nc.vector.tensor_copy(cT[:, :], pst[:, P:P + 16]).then_inc(t_copied, 1)
            dve.wait_ge(c_exp, 1)
            nc.vector.tensor_scalar(ce[:, :], ce[:, :], 1.0, None, ALU.add).then_inc(c_one, 1)
            dve.wait_ge(c_one, 1)
            nc.vector.reciprocal(ce[:, :], ce[:, :]).then_inc(c_rec, 1)
            dve.wait_ge(c_rec, 1)
            nc.vector.tensor_tensor(sil[:, :, :].rearrange("p k c -> p c k"), cT[:, :].rearrange("p (c k) -> p c k", c=2),
                                    ce[:, :].rearrange("p (c k) -> p c k", c=2), ALU.mult).then_inc(sil_done, 1)
            for u in range(4):
                l, h = u // 2, u % 2
                dve.wait_ge(w_used, 6 * u + 6)
                if u >= 2:
                    dve.wait_ge(stored, 32 * (u - 1))
                pv = psc[:, h, 0:4 * KD].rearrange("p (s k c) -> p s k c", s=2, c=2)
                for c in range(2):
                    sh = vecT[:, l * 48 + h * 24:l * 48 + h * 24 + 8]
                    sc = vecT[:, l * 48 + h * 24 + 8:l * 48 + h * 24 + 16]
                    g = vecT[:, 96 + h * 16 + l * 8:96 + h * 16 + l * 8 + 8]
                    nc.vector.tensor_tensor(ocol[:, h, c, 0], pv[:, 0, :, c], sh, ALU.add)
                    nc.vector.tensor_tensor(ocol[:, h, c, 1], pv[:, 1, :, c], sc, ALU.add).then_inc(step, 1)
                    dve.wait_ge(step, 2 * u + c + 1)
                    nc.vector.scalar_tensor_tensor(ocol[:, h, c, 1], ocol[:, h, c, 1], 1.0, g, ALU.add, ALU.mult).then_inc(c_one, 1)
                ov = orow[:, h].rearrange("a (b n) -> a b n", b=2)
                bv = brow[:, l, h].rearrange("a (b n) -> a b n", b=2)
                gv = grow[:, l, h].rearrange("a (b n) -> a b n", b=2)
                nc.vector.tensor_tensor(ov, psr[0:1, h], bv, ALU.add).then_inc(c_one, 1)
                dve.wait_ge(c_one, 3 * u + 4)
                nc.vector.tensor_tensor(ov, ov, gv, ALU.mult).then_inc(half_read, 1)


def nothing(i, s):
    pass


def staged(eng, pairs, early, front, back, apart=1):
    def step(i):
        front(i, 0)
        early(i, 1)
        if not (isinstance(i, int) and i == 0):
            back(i - 1, 1)
        front(i, 1)
        if not (isinstance(i, int) and i == pairs - 1):
            early(i + 1, 0)
        back(i, 0)

    early(0, 0)
    for i in range(apart):
        step(i)
    with eng.Fori(apart, pairs - 1) as i:
        step(i)
    step(pairs - 1)
    back(pairs - 1, 1)


def project(nc, name, src, ntiles, cols_x, cols_c, w, width, dst, ident_d):
    norm = cols_x is not None
    nb = (width + BANK - 1) // BANK
    blocks = [(b * BANK, min(width, (b + 1) * BANK)) for b in range(nb)]
    pairs = ntiles // 2
    with ExitStack() as ctx:
        m = Memory(nc, ctx, name)
        W = m.sbuf("w", [P, KD, width])
        X = m.sbuf("x", [P, 2, D])
        XN = m.sbuf("xn", [P, 2, D]) if norm else X
        HT = m.sbuf("ht", [P, 2, KD, P])
        O = m.sbuf("o", [P, 2, width])
        ident = m.sbuf("ident", [P, P])
        mod = m.sbuf("mod", [P, 2, 2, KD])
        stat = m.sbuf("stat", [P, 2, 4])
        eps = m.sbuf("eps", [P, 1])
        psT = m.psum("psT", [P, 2, BANK])
        psO = m.psum("psO", [P, nb, BANK])
        w_loaded = m.sem("w_loaded")
        squared = m.sem("squared")
        rooted = m.sem("rooted")
        inverted = m.sem("inverted")
        xn_done = m.sem("xn_done")
        tr_done = m.sem("tr_done")
        ht_a, ht_v = m.sem("ht_a"), m.sem("ht_v")
        banks_done = m.sem("banks_done")
        banks_a, banks_v = m.sem("banks_a"), m.sem("banks_v")
        eps_set = m.sem("eps_set")
        ident_in = m.sem("ident_in")
        x_in = [m.sem(f"x_in{s}") for s in range(2)]
        o_free = [m.sem(f"o_free{s}") for s in range(2)]
        block = ctx.enter_context(nc.Block())
        consts = 16 * (2 if norm else 0)
        mine_a, mine_v = list(range(0, nb, 2)), list(range(1, nb, 2))
        x_free = xn_done if norm else tr_done

        @block.sync
        def _(sp):
            sp.dma_start(ident[:, :], ident_d).then_inc(ident_in, 16)
            if norm:
                sp.dma_start(mod[:, 0], cols_x).then_inc(w_loaded, 16)
                sp.dma_start(mod[:, 1], cols_c).then_inc(w_loaded, 16)
            wv = w.rearrange("(k p) n -> p k n", p=P)
            for k in range(0, KD, 2):
                sp.dma_start(W[:, k:k + 2], wv[:, k:k + 2]).then_inc(w_loaded, 16)

            for s in range(2):
                sp.sem_inc(o_free[s], 16)

            def load(i, s):
                sp.wait_ge(x_free, i * 2 + s + 1)
                sp.wait_ge(ident_in, 16)
                sp.dma_start(X[:, s], rows(src, i * 2 + s)).then_inc(x_in[s], 16)

            def store(i, s):
                n = i * 2 + s
                sp.wait_ge(banks_a, (n + 2) * len(mine_a))
                sp.wait_ge(banks_v, (n + 2) * len(mine_v))
                sp.wait_ge(ident_in, 16)
                sp.dma_start(rows(dst, i * 2 + s), O[:, s]).then_inc(o_free[s], 16)
            staged(sp, pairs, load, nothing, store)
            for s in range(2):
                sp.wait_ge(o_free[s], 16 * (pairs + 1))

        def banks_out(eng, i, s, mine, copied, copy):
            eng.wait_ge(o_free[s], i * 16 + 16)
            for b in mine:
                eng.wait_ge(banks_done, (i * 2 + s + 2) * nb + b + 1)
                a, z = blocks[b]
                copy(O[:, s, a:z], psO[:, b, 0:z - a]).then_inc(copied, 1)

        @block.scalar
        def _(act):
            act.sem_inc(banks_a, len(mine_a))
            act.wait_ge(w_loaded, consts + 64)
            if norm:
                act.wait_ge(eps_set, 1)

            def early(i, s):
                n = i * 2 + s
                if norm:
                    act.wait_ge(x_in[s], i * 16 + 16)
                    act.wait_ge(tr_done, n + 1)
                    nc.scalar.activation(XN[:, s], X[:, s], ACT.Square, accum_out=stat[:, s, 0:1]).then_inc(squared, 1)
                    act.wait_ge(squared, n + 1)
                    nc.scalar.activation(stat[:, s, 1:2], stat[:, s, 0:1], ACT.Sqrt, bias=eps[:, 0:1],
                                         scale=1.0 / D).then_inc(rooted, 1)

            def front(i, s):
                n = i * 2 + s
                act.wait_ge(tr_done, n + 3)
                act.wait_ge(banks_done, (n + 1) * nb)
                if norm:
                    c = 1 if isinstance(i, int) and i == 0 else 0
                    for k in range(4, 8):
                        last = nc.scalar.activation(HT[:, s, k], psT[:, 1, (k - 4) * P:(k - 3) * P], ACT.Identity,
                                                    bias=mod[:, c, 0, k:k + 1], scale=mod[:, c, 1, k:k + 1])
                else:
                    last = nc.scalar.activation(HT[:, s, 4:8], psT[:, 1].rearrange("p (k n) -> p k n", k=4), ACT.Copy)
                last.then_inc(ht_a, 1)

            def back(i, s):
                banks_out(act, i, s, mine_a, banks_a,
                          lambda out, ps: nc.scalar.activation(out, ps, ACT.Copy))
            staged(act, pairs, early, front, back)

        @block.vector
        def _(dve):
            dve.sem_inc(banks_v, len(mine_v))
            dve.sem_inc(xn_done, 2)
            nc.vector.memset(eps[:, :], EPS).then_inc(eps_set, 1)
            dve.wait_ge(w_loaded, consts + 64)

            def early(i, s):
                n = i * 2 + s
                if norm:
                    dve.wait_ge(rooted, n + 1)
                    nc.vector.reciprocal(stat[:, s, 2:3], stat[:, s, 1:2]).then_inc(inverted, 1)
                    dve.wait_ge(inverted, n + 1)
                    nc.vector.tensor_scalar(XN[:, s], X[:, s], stat[:, s, 2:3], None, ALU.mult).then_inc(xn_done, 1)

            def front(i, s):
                n = i * 2 + s
                dve.wait_ge(tr_done, n + 3)
                dve.wait_ge(banks_done, (n + 1) * nb)
                if norm:
                    c = 1 if isinstance(i, int) and i == 0 else 0
                    for k in range(4):
                        last = nc.vector.tensor_scalar(HT[:, s, k], psT[:, 0, k * P:(k + 1) * P], mod[:, c, 1, k:k + 1],
                                                       mod[:, c, 0, k:k + 1], ALU.mult, ALU.add)
                else:
                    last = nc.vector.tensor_copy(HT[:, s, 0:4], psT[:, 0].rearrange("p (k n) -> p k n", k=4))
                last.then_inc(ht_v, 1)

            def back(i, s):
                banks_out(dve, i, s, mine_v, banks_v, nc.vector.tensor_copy)
            staged(dve, pairs, early, front, back)

        @block.tensor
        def _(pe):
            pe.sem_inc(banks_done, 2 * nb)
            pe.sem_inc(tr_done, 2)
            pe.wait_ge(w_loaded, consts + 64)
            pe.wait_ge(ident_in, 16)

            def front(i, s):
                n = i * 2 + s
                if norm:
                    pe.wait_ge(xn_done, n + 3)
                else:
                    pe.wait_ge(x_in[s], i * 16 + 16)
                if not isinstance(i, int) or n > 0:
                    pe.wait_ge(ht_a, n)
                    pe.wait_ge(ht_v, n)
                for k in range(KD):
                    last = nc.tensor.transpose(psT[:, k // 4, k % 4 * P:(k % 4 + 1) * P], XN[:, s, k * P:(k + 1) * P],
                                               ident[:, :])
                last.then_inc(tr_done, 1)

            def back(i, s):
                n = i * 2 + s
                pe.wait_ge(ht_a, n + 1)
                pe.wait_ge(ht_v, n + 1)
                for b, (a, z) in enumerate(blocks):
                    mine, copied = (mine_a, banks_a) if b in mine_a else (mine_v, banks_v)
                    pe.wait_ge(copied, n * len(mine) + mine.index(b) + 1)
                    for k in range(KD):
                        last = nc.tensor.matmul(psO[:, b, 0:z - a], HT[:, s, k], W[:, k, a:z], start=k == 0, stop=k == KD - 1)
                    last.then_inc(banks_done, 1)
            staged(pe, pairs, nothing, front, back)


def residual(nc, name, y, x, dst, gate, cols, hT_d, ident_d, xn_d=None):
    pairs = NT // 2
    with ExitStack() as ctx:
        m = Memory(nc, ctx, name)
        Y = m.sbuf("y", [P, 2, D])
        X = m.sbuf("x", [P, 2, D])
        T = m.sbuf("t", [P, 2, D])
        XO = m.sbuf("xo", [P, 2, D])
        XN = m.sbuf("xn", [P, 2, D])
        junk = m.sbuf("junk", [P, D])
        HT = m.sbuf("ht", [P, 2, KD, P])
        G = m.sbuf("g", [P, D])
        ident = m.sbuf("ident", [P, P])
        mod = m.sbuf("mod", [P, 2, KD])
        stat = m.sbuf("stat", [P, 2, 8])
        eps = m.sbuf("eps", [P, 1])
        psT = m.psum("psT", [P, 2, 2, BANK])
        const_in = m.sem("const_in")
        ident_in = m.sem("ident_in")
        eps_set = m.sem("eps_set")
        passed = m.sem("passed")
        yx_in = [m.software_sem(f"yx_in{s}") for s in range(2)]
        yroot = m.sem("yroot")
        xroot = m.sem("xroot")
        sq_y, sq_x = m.sem("sq_y"), m.sem("sq_x")
        inv, inv_x = m.sem("inv"), m.sem("inv_x")
        scaled = m.sem("scaled")
        summed = m.sem("summed")
        normed = m.sem("normed")
        tr_done = m.sem("tr_done")
        ht_a, ht_v = m.sem("ht_a"), m.sem("ht_v")
        x_out = [m.sem(f"x_out{s}") for s in range(2)]
        h_out = [m.sem(f"h_out{s}") for s in range(2)]
        n_out = [m.sem(f"n_out{s}") for s in range(2)]
        block = ctx.enter_context(nc.Block())
        nconst = 16 * (2 if cols is not None else 1)

        @block.sync
        def _(sp):
            sp.dma_start(ident[:, :], ident_d).then_inc(ident_in, 16)
            sp.dma_start(G[:, :], gate.rearrange("(a n) -> a n", a=1).to_broadcast([P, D])).then_inc(const_in, 16)
            if cols is not None:
                sp.dma_start(mod[:, :], cols).then_inc(const_in, 16)
            for s in range(2):
                sp.sem_inc(x_out[s], 16)
                sp.sem_inc(n_out[s], 16)
                sp.sem_inc(h_out[s], 16)

            def store_x(i, s):
                n = i * 2 + s
                sp.wait_ge(summed, n + 3)
                sp.wait_ge(ident_in, 16)
                sp.dma_start(rows(dst, n), XO[:, s]).then_inc(x_out[s], 16)

            def store_h(i, s):
                n = i * 2 + s
                if cols is None:
                    return
                sp.wait_ge(ht_a, n + 3)
                sp.wait_ge(ht_v, n + 3)
                sp.wait_ge(ident_in, 16)
                sp.dma_start(hT_d[:, :, bass.ds(n * P, P)], HT[:, s]).then_inc(h_out[s], 16)
                if xn_d is not None:
                    sp.dma_start(rows(xn_d, n), XN[:, s]).then_inc(n_out[s], 16)
            staged(sp, pairs, nothing, store_x, store_h)
            if xn_d is not None:
                for s in range(2):
                    sp.wait_ge(n_out[s], 16 * (pairs + 1))
            for s in range(2):
                sp.wait_ge(x_out[s], 16 * (pairs + 1))
                sp.wait_ge(h_out[s], 16 * (pairs + 1) if cols is not None else 16)

        @block.gpsimd
        def _(pool):
            def load(i, s):
                n = i * 2 + s
                pool.wait_ge(summed, n + 1)
                pool.sem_inc(passed, 1)
                pool.dma_start(Y[:, s], rows(y, n)).then_inc(yx_in[s], 16)
                pool.dma_start(X[:, s], rows(x, n)).then_inc(yx_in[s], 16)
            staged(pool, pairs, nothing, load, nothing)

        @block.scalar
        def _(act):
            act.sem_inc(ht_a, 2)
            act.wait_ge(eps_set, 1)
            act.wait_ge(const_in, nconst)

            def early(i, s):
                n = i * 2 + s
                act.wait_ge(yx_in[s], i * 32 + 32)
                nc.scalar.activation(junk[:, :], Y[:, s], ACT.Square, accum_out=stat[:, s, 0:1]).then_inc(sq_y, 1)
                act.wait_ge(sq_y, n + 1)
                nc.scalar.activation(stat[:, s, 1:2], stat[:, s, 0:1], ACT.Sqrt, bias=eps[:, 0:1], scale=1.0 / D).then_inc(yroot, 1)

            def front(i, s):
                n = i * 2 + s
                if cols is None:
                    return
                act.wait_ge(summed, n + 3)
                nc.scalar.activation(junk[:, :], XO[:, s], ACT.Square, accum_out=stat[:, s, 4:5]).then_inc(sq_x, 1)
                act.wait_ge(sq_x, n + 1)
                nc.scalar.activation(stat[:, s, 5:6], stat[:, s, 4:5], ACT.Sqrt, bias=eps[:, 0:1], scale=1.0 / D).then_inc(xroot, 1)

            def back(i, s):
                n = i * 2 + s
                if cols is None:
                    return
                act.wait_ge(tr_done, n + 3)
                act.wait_ge(h_out[s], i * 16 + 16)
                for k in range(4, 8):
                    last = nc.scalar.activation(HT[:, s, k], psT[:, s, 1, (k - 4) * P:(k - 3) * P], ACT.Identity,
                                                bias=mod[:, 0, k:k + 1], scale=mod[:, 1, k:k + 1])
                last.then_inc(ht_a, 1)
            staged(act, pairs, early, front, back)

        @block.vector
        def _(dve):
            dve.sem_inc(summed, 2)
            dve.sem_inc(ht_v, 2)
            nc.vector.memset(eps[:, :], EPS).then_inc(eps_set, 1)
            dve.wait_ge(const_in, nconst)

            def early(i, s):
                n = i * 2 + s
                dve.wait_ge(yroot, n + 1)
                nc.vector.reciprocal(stat[:, s, 2:3], stat[:, s, 1:2]).then_inc(inv, 1)
                dve.wait_ge(inv, n + 1)
                nc.vector.scalar_tensor_tensor(T[:, s], Y[:, s], stat[:, s, 2:3], G[:, :], ALU.mult, ALU.mult).then_inc(scaled, 1)
                dve.wait_ge(scaled, n + 1)
                dve.wait_ge(x_out[s], i * 16 + 16)
                if cols is not None:
                    dve.wait_ge(tr_done, n + 1)
                nc.vector.tensor_tensor(XO[:, s], X[:, s], T[:, s], ALU.add).then_inc(summed, 1)

            def front(i, s):
                n = i * 2 + s
                if cols is None:
                    return
                dve.wait_ge(xroot, n + 1)
                nc.vector.reciprocal(stat[:, s, 6:7], stat[:, s, 5:6]).then_inc(inv_x, 1)
                dve.wait_ge(inv_x, n + 1)
                dve.wait_ge(tr_done, n + 1)
                if xn_d is not None:
                    dve.wait_ge(n_out[s], i * 16 + 16)
                nc.vector.tensor_scalar(XN[:, s], XO[:, s], stat[:, s, 6:7], None, ALU.mult).then_inc(normed, 1)

            def back(i, s):
                n = i * 2 + s
                if cols is None:
                    return
                dve.wait_ge(tr_done, n + 3)
                dve.wait_ge(h_out[s], i * 16 + 16)
                for k in range(4):
                    last = nc.vector.tensor_scalar(HT[:, s, k], psT[:, s, 0, k * P:(k + 1) * P], mod[:, 1, k:k + 1],
                                                   mod[:, 0, k:k + 1], ALU.mult, ALU.add)
                last.then_inc(ht_v, 1)
            staged(dve, pairs, early, front, back)

        @block.tensor
        def _(pe):
            pe.sem_inc(tr_done, 2)
            pe.wait_ge(ident_in, 16)

            def front(i, s):
                n = i * 2 + s
                if cols is None:
                    return
                pe.wait_ge(normed, n + 1)
                pe.wait_ge(ht_a, n + 1)
                pe.wait_ge(ht_v, n + 1)
                for k in range(KD):
                    last = nc.tensor.transpose(psT[:, s, k // 4, k % 4 * P:(k % 4 + 1) * P], XN[:, s, k * P:(k + 1) * P],
                                               ident[:, :])
                last.then_inc(tr_done, 1)
            staged(pe, pairs, nothing, front, nothing)


def swiglu(nc, name, hT_d, w1, w3, w2, gates_d, y_d, clear=()):
    E, _, F = w1.shape
    FC = F // P
    NB = SEQ // BANK
    TB = BANK // P
    with ExitStack() as ctx:
        m = Memory(nc, ctx, name)
        HT = m.sbuf("ht", [P, KD, SEQ])
        YA = m.sbuf("ya", [P, NT, D])
        W1 = m.sbuf("w1", [P, 2, KD, P])
        W3 = m.sbuf("w3", [P, 2, KD, P])
        W2 = m.sbuf("w2", [P, 2, D])
        S = m.sbuf("s", [P, 2, BANK])
        A = m.sbuf("a", [P, 2, BANK])
        GT = m.sbuf("gt", [P, NT, E])
        psU = m.psum("psU", [P, 2, BANK])
        psG = m.psum("psG", [P, 2, BANK])
        psY = m.psum("psY", [P, 4, BANK])
        h_in = m.sem("h_in")
        w_in = [m.sem(f"w_in{s}") for s in range(2)]
        h_ready = m.sem("h_ready")
        ug_done = m.sem("ug_done")
        silu_done = m.sem("silu_done")
        a_done = m.sem("a_done")
        y_done = m.sem("y_done")
        y_added = m.sem("y_added")
        zeroed = m.sem("zeroed")
        ZERO = m.sbuf("zero", [P, D])
        zero_set, cleared = m.sem("zero_set"), m.software_sem("cleared")
        y_out = m.sem("y_out")
        block = ctx.enter_context(nc.Block())
        per = NB * TB * 2
        npairs = FC // 2

        @block.sync
        def _(sp):
            for k in range(KD):
                sp.dma_start(HT[:, k], hT_d[:, k]).then_inc(h_in, 16)
            if gates_d is not None:
                sp.dma_start(GT[:, :], gates_d).then_inc(h_in, 16)
            w1v = w1.rearrange("e (k p) (f n) -> e f p k n", p=P, n=P)
            w3v = w3.rearrange("e (k p) (f n) -> e f p k n", p=P, n=P)
            w2v = w2.rearrange("e (f p) n -> e f p n", p=P)
            with sp.Fori(0, E) as e:
                with sp.Fori(0, npairs) as i:
                    for s in range(2):
                        c = (e * npairs + i) * 2 + s
                        sp.wait_ge(y_done, c * per + per)
                        sp.wait_ge(a_done, 2)
                        f = i * 2 + s
                        sp.dma_start(W1[:, s], w1v[bass.ds(e, 1), bass.ds(f, 1)].rearrange("a b p k n -> p (a b k) n")).then_inc(w_in[s], 16)
                        sp.dma_start(W3[:, s], w3v[bass.ds(e, 1), bass.ds(f, 1)].rearrange("a b p k n -> p (a b k) n")).then_inc(w_in[s], 16)
                        sp.dma_start(W2[:, s], w2v[bass.ds(e, 1), bass.ds(f, 1)].rearrange("a b p n -> p (a b n)")).then_inc(w_in[s], 16)
            sp.wait_ge(y_added, 4 + E * FC * per)
            for t in range(0, NT, 4):
                sp.dma_start(y_d.rearrange("(t p) n -> p t n", p=P)[:, t:t + 4], YA[:, t:t + 4]).then_inc(y_out, 16)
            sp.wait_ge(y_out, 16 * (NT // 4))

        @block.gpsimd
        def _(pool):
            if not clear:
                return
            pool.memset(ZERO[:, :], 0.0).then_inc(zero_set, 1)
            pool.wait_ge(zero_set, 1)
            n = clear[0].shape[0] // P
            with pool.Fori(0, n) as t:
                for c in clear:
                    pool.dma_start(rows(c, t), ZERO[:, :]).then_inc(cleared, 16)
            pool.wait_ge(cleared, 16 * n * len(clear))

        @block.tensor
        def _(pe):
            pe.sem_inc(y_done, 2 * per)
            pe.wait_ge(h_in, 16 * (KD + (1 if gates_d is not None else 0)))

            def up(c, ws, s, b):
                n = c * NB + b
                if b == 0:
                    pe.wait_ge(w_in[s], ws * 48 + 48)
                pe.wait_ge(a_done, n + 1)
                for ps, W in ((psU, W1), (psG, W3)):
                    for k in range(KD):
                        last = nc.tensor.matmul(ps[:, b % 2], W[:, s, k], HT[:, k, b * BANK:(b + 1) * BANK],
                                                start=k == 0, stop=k == KD - 1)
                last.then_inc(ug_done, 1)

            def down(c, s, b):
                n = c * NB + b
                pe.wait_ge(a_done, n + 3)
                for t in range(TB):
                    for h in range(2):
                        j = t * 2 + h
                        pe.wait_ge(y_added, c * per + b * TB * 2 + j + 1)
                        nc.tensor.matmul(psY[:, j % 4], A[:, b % 2, t * P:(t + 1) * P], W2[:, s, h * BANK:(h + 1) * BANK],
                                         start=True, stop=True).then_inc(y_done, 1)
            with pe.Fori(0, E) as e:
                with pe.Fori(0, npairs) as i:
                    for s in range(2):
                        ws = e * npairs + i
                        c = ws * 2 + s
                        for b in range(NB + 1):
                            if b < NB:
                                up(c, ws, s, b)
                            if b:
                                down(c, s, b - 1)

        @block.scalar
        def _(act):
            act.sem_inc(silu_done, 2)
            with act.Fori(0, E * npairs) as i:
                for s in range(2):
                    for b in range(NB):
                        n = (i * 2 + s) * NB + b
                        act.wait_ge(ug_done, n + 1)
                        act.wait_ge(a_done, n + 1)
                        nc.scalar.activation(S[:, b % 2], psU[:, b % 2], ACT.Silu).then_inc(silu_done, 1)

        @block.vector
        def _(dve):
            dve.sem_inc(a_done, 2)
            dve.sem_inc(y_added, 4)
            nc.vector.memset(YA[:, :], 0.0).then_inc(zeroed, 1)
            dve.wait_ge(h_in, 16 * (KD + (1 if gates_d is not None else 0)))
            dve.wait_ge(zeroed, 1)

            def hidden(c, b):
                n = c * NB + b
                dve.wait_ge(silu_done, n + 3)
                dve.wait_ge(y_done, c * per + (2 + 0) * per + (b - 1) * TB * 2)
                nc.vector.tensor_tensor(A[:, b % 2], S[:, b % 2], psG[:, b % 2], ALU.mult).then_inc(a_done, 1)

            def add(e, c, b):
                for t in range(TB):
                    for h in range(2):
                        j = t * 2 + h
                        dve.wait_ge(y_done, (c + 2) * per + b * TB * 2 + j + 1)
                        out = YA[:, b * TB + t, h * BANK:(h + 1) * BANK]
                        if gates_d is None:
                            nc.vector.tensor_tensor(out, psY[:, j % 4], out, ALU.add).then_inc(y_added, 1)
                        else:
                            nc.vector.scalar_tensor_tensor(out, psY[:, j % 4], GT[:, b * TB + t, bass.ds(e, 1)], out,
                                                           ALU.mult, ALU.add).then_inc(y_added, 1)
            with dve.Fori(0, E) as e:
                with dve.Fori(0, npairs) as i:
                    for s in range(2):
                        c = (e * npairs + i) * 2 + s
                        for b in range(NB + 1):
                            if b < NB:
                                hidden(c, b)
                            if b:
                                add(e, c, b - 1)


def mla_prepare(nc, proj_d, q_norm, kv_norm, rope_tok, ident_d, ckvT, krT, ckv, cqT):
    W = D_IN - COL_CQ
    KV, KR = COL_CKV - COL_CQ, COL_KR - COL_CQ
    pairs = NA // 2
    with ExitStack() as ctx:
        m = Memory(nc, ctx, "mp")
        X = m.sbuf("x", [P, 2, W])
        N = m.sbuf("n", [P, 2, QR])
        R = m.sbuf("r", [P, 2, 2, ROPE])
        RT = m.sbuf("rt", [P, 2, 2, ROPE])
        junk = m.sbuf("junk", [P, QR])
        junk2 = m.sbuf("junk2", [P, KVR])
        K = m.sbuf("k", [P, 2, KVR])
        G = m.sbuf("g", [P, KVR])
        qn = m.sbuf("qn", [P, 2])
        ident = m.sbuf("ident", [P, P])
        stat = m.sbuf("stat", [P, 2, 8])
        eps = m.sbuf("eps", [P, 1])
        psT = m.psum("psT", [P, 2, BANK])
        psK = m.psum("psK", [P, 2, BANK])
        const_in, eps_set = m.sem("const_in"), m.sem("eps_set")
        x_in = [m.sem(f"x_in{s}") for s in range(2)]
        squared, rooted, inverted = m.sem("squared"), m.sem("rooted"), m.sem("inverted")
        parts = m.sem("parts")
        ready = m.sem("ready")
        tr_done = m.sem("tr_done")
        out_a, out_v = m.sem("out_a"), m.sem("out_v")
        block = ctx.enter_context(nc.Block())

        @block.sync
        def _(sp):
            sp.dma_start(ident[:, :], ident_d).then_inc(const_in, 16)
            sp.dma_start(G[:, :], kv_norm.to_broadcast([P, KVR])).then_inc(const_in, 16)
            sp.dma_start(qn[:, :], q_norm).then_inc(const_in, 16)
            sp.wait_ge(const_in, 48)

            def load(i, s):
                n = i * 2 + s
                sp.wait_ge(ready, n + 1)
                sp.wait_ge(const_in, 48)
                sp.dma_start(X[:, s], rows(proj_d[:, COL_CQ:D_IN], n)).then_inc(x_in[s], 16)
                sp.dma_start(RT[:, s], rope_tok.rearrange("(t p) a n -> t p a n", p=P)[bass.ds(n, 1)].rearrange("t p a n -> p (t a) n")).then_inc(x_in[s], 16)
            staged(sp, pairs, load, nothing, nothing)

        @block.scalar
        def _(act):
            act.sem_inc(out_a, 2)
            act.wait_ge(const_in, 48)
            act.wait_ge(eps_set, 1)

            def early(i, s):
                n = i * 2 + s
                act.wait_ge(x_in[s], i * 32 + 32)
                nc.scalar.activation(junk[:, 0:QR], X[:, s, 0:QR], ACT.Square, accum_out=stat[:, s, 0:1]).then_inc(squared, 1)
                nc.scalar.activation(junk2[:, :], X[:, s, KV:KV + KVR], ACT.Square, accum_out=stat[:, s, 1:2]).then_inc(squared, 1)
                act.wait_ge(squared, n * 2 + 2)
                nc.scalar.activation(stat[:, s, 2:3], stat[:, s, 0:1], ACT.Sqrt, bias=eps[:, 0:1], scale=1.0 / QR)
                nc.scalar.activation(stat[:, s, 3:4], stat[:, s, 1:2], ACT.Sqrt, bias=eps[:, 0:1], scale=1.0 / KVR).then_inc(rooted, 1)

            def front(i, s):
                n = i * 2 + s
                act.wait_ge(tr_done, n + 3)
                for k in range(2):
                    last = nc.scalar.activation(cqT[:, k, bass.ds(n * P, P)], psT[:, s, k * P:(k + 1) * P], ACT.Copy,
                                                scale=qn[:, k:k + 1])
                last.then_inc(out_a, 1)
            staged(act, pairs, early, front, nothing)

        @block.vector
        def _(dve):
            dve.sem_inc(ready, 2)
            dve.sem_inc(out_v, 2)
            nc.vector.memset(eps[:, :], EPS).then_inc(eps_set, 1)
            dve.wait_ge(const_in, 48)

            def early(i, s):
                n = i * 2 + s
                dve.wait_ge(rooted, n + 1)
                nc.vector.reciprocal(stat[:, s, 4:6], stat[:, s, 2:4]).then_inc(inverted, 1)
                dve.wait_ge(inverted, n + 1)
                dve.wait_ge(tr_done, n + 1)
                nc.vector.tensor_scalar(N[:, s], X[:, s, 0:QR], stat[:, s, 4:5], None, ALU.mult)
                nc.vector.scalar_tensor_tensor(K[:, s], X[:, s, KV:KV + KVR], stat[:, s, 5:6], G[:, :],
                                               ALU.mult, ALU.mult)
                kr = X[:, s, KR:KR + ROPE].rearrange("p (a u n) -> p a u n", a=2, u=2)
                sn = RT[:, s, 1].rearrange("p (a u n) -> p a u n", a=2, u=2)
                r1 = R[:, s, 1].rearrange("p (a u n) -> p a u n", a=2, u=2)
                nc.vector.tensor_tensor(R[:, s, 0], X[:, s, KR:KR + ROPE], RT[:, s, 0], ALU.mult)
                nc.vector.tensor_tensor(r1[:, :, 0], kr[:, :, 1], sn[:, :, 0], ALU.mult).then_inc(parts, 1)
                nc.vector.tensor_tensor(r1[:, :, 1], kr[:, :, 0], sn[:, :, 1], ALU.mult).then_inc(parts, 1)
                dve.wait_ge(parts, n * 2 + 2)
                nc.vector.tensor_tensor(R[:, s, 0], R[:, s, 0], R[:, s, 1], ALU.add).then_inc(ready, 1)

            def front(i, s):
                n = i * 2 + s
                dve.wait_ge(tr_done, n + 3)
                nc.vector.tensor_copy(ckvT[:, bass.ds(n * P, P)], psK[:, s, 0:P])
                nc.vector.tensor_copy(ckv[:, bass.ds(n, 1)].rearrange("p a n -> p (a n)"), K[:, s])
                nc.vector.tensor_copy(krT[:, bass.ds(n * P, P)], psK[0:ROPE, s, P:2 * P]).then_inc(out_v, 1)
            staged(dve, pairs, early, front, nothing)

        @block.tensor
        def _(pe):
            pe.sem_inc(tr_done, 2)
            pe.wait_ge(const_in, 48)

            def front(i, s):
                n = i * 2 + s
                pe.wait_ge(ready, n + 3)
                pe.wait_ge(out_a, n + 1)
                pe.wait_ge(out_v, n + 1)
                for k in range(2):
                    nc.tensor.transpose(psT[:, s, k * P:(k + 1) * P], N[:, s, k * P:(k + 1) * P], ident[:, :])
                nc.tensor.transpose(psK[:, s, 0:P], K[:, s], ident[:, :])
                nc.tensor.transpose(psK[0:ROPE, s, P:2 * P], R[:, s, 0], ident[:, :]).then_inc(tr_done, 1)
            staged(pe, pairs, nothing, front, nothing)


def mla_attend(nc, w_uq, w_uq_swapped, w_ukT, w_ukv, rope_feat, ident_d, ckvT, krT, ckv, cqT, mix_d):
    KT = NA
    KEYS = KT * P
    chunks = [(c * BANK, min(KEYS, (c + 1) * BANK)) for c in range((KEYS + BANK - 1) // BANK)]
    groups = [(g, min(KT, g + 4)) for g in range(0, KT, 4)]
    NCH, NG = len(chunks), len(groups)
    SCALE = float(NOPE + ROPE) ** -0.5
    HW = NOPE + ROPE
    with ExitStack() as ctx:
        m = Memory(nc, ctx, "ma")
        WUQ = m.sbuf("wuq", [P, 2, HEADS * HW])
        WUS = m.sbuf("wus", [P, 2, HEADS * ROPE])
        WKT = m.sbuf("wkt", [P, HEADS, KVR])
        WV = m.sbuf("wv", [P, HEADS, DV])
        RF = m.sbuf("rf", [ROPE, 2, SEQ])
        ident = m.sbuf("ident", [P, P])
        QN = m.sbuf("qn", [P, HEADS, P])
        QP = m.sbuf("qp", [P, HEADS, P])
        QR_ = m.sbuf("qr", [ROPE, HEADS, P])
        QT = m.sbuf("qt", [ROPE, HEADS, P])
        PM = m.sbuf("pm", [P, 2, KEYS])
        PT = m.sbuf("pt", [P, KT, P])
        OL = m.sbuf("ol", [P, P])
        MX = m.sbuf("mx", [P, HEADS * DV])
        stat = m.sbuf("stat", [P, 2, 2, 8])
        top = m.sbuf("top", [P, 2, 4])
        psS = m.psum("psS", [P, NCH, BANK])
        psT = m.psum("psT", [P, 2, BANK])
        psO = m.psum("psO", [P, BANK])
        const_in = m.sem("const_in")
        q_done = m.sem("q_done")
        qn_out = m.sem("qn_out")
        qr_part = m.sem("qr_part")
        qr_out = m.sem("qr_out")
        qp_done = m.sem("qp_done")
        qp_out = m.sem("qp_out")
        s_done = m.sem("s_done")
        c_max = m.sem("c_max")
        h_max = m.sem("h_max")
        neg_max = m.sem("neg_max")
        exp_done = m.sem("exp_done")
        sums = m.sem("sums")
        inv_done = m.sem("inv_done")
        t_done = m.sem("t_done")
        t_out = m.sem("t_out")
        pv_done = m.sem("pv_done")
        ol_out = m.sem("ol_out")
        av_done = m.sem("av_done")
        av_out = m.sem("av_out")
        m_out = m.sem("m_out")
        block = ctx.enter_context(nc.Block())
        NCONST = 6 * 16

        def heads(eng, tile_start, score, weigh):
            def tile(t, before):
                tile_start(t)
                for h in range(HEADS):
                    score(t, h)
                    if h:
                        weigh(t, h - 1)
                    elif before is not None:
                        weigh(before, HEADS - 1)
            tile(0, None)
            with eng.Fori(1, NT) as t:
                tile(t, t - 1)
            weigh(NT - 1, HEADS - 1)

        @block.sync
        def _(sp):
            sp.dma_start(WUQ[:, :], w_uq.rearrange("(k p) n -> p k n", p=P)).then_inc(const_in, 16)
            sp.dma_start(WUS[:, :], w_uq_swapped.rearrange("(k p) n -> p k n", p=P)).then_inc(const_in, 16)
            sp.dma_start(WKT[:, :], w_ukT).then_inc(const_in, 16)
            sp.dma_start(WV[:, :], w_ukv.rearrange("c (h n) -> c h n", h=HEADS)[:, :, NOPE:NOPE + DV]).then_inc(const_in, 16)
            sp.dma_start(RF[:, :], rope_feat).then_inc(const_in, 16)
            sp.dma_start(ident[:, :], ident_d).then_inc(const_in, 16)
            sp.wait_ge(const_in, NCONST)
            with sp.Fori(0, NT) as t:
                sp.wait_ge(av_out, t * HEADS + HEADS)
                sp.wait_ge(const_in, NCONST)
                sp.dma_start(rows(mix_d[:, HEADS * DV:2 * HEADS * DV], t), MX[:, :]).then_inc(m_out, 16)
            sp.wait_ge(m_out, 16 * NT)

        @block.tensor
        def _(pe):
            pe.wait_ge(const_in, NCONST)

            def start(t):
                if not isinstance(t, int):
                    pe.wait_ge(exp_done, t * HEADS * NCH)
                tok = bass.ds((t + NC) * P, P)
                for h in range(HEADS):
                    for k in range(2):
                        nc.tensor.matmul(psS[:, 0, h * P:(h + 1) * P], WUQ[:, k, h * HW:h * HW + NOPE], cqT[:, k, tok],
                                         start=k == 0, stop=k == 1)
                for h in range(HEADS):
                    for k in range(2):
                        nc.tensor.matmul(psS[0:ROPE, 1, h * P:(h + 1) * P], WUQ[:, k, h * HW + NOPE:(h + 1) * HW], cqT[:, k, tok],
                                         start=k == 0, stop=k == 1)
                for h in range(HEADS):
                    for k in range(2):
                        last = nc.tensor.matmul(psS[0:ROPE, 2, h * P:(h + 1) * P], WUS[:, k, h * ROPE:(h + 1) * ROPE], cqT[:, k, tok],
                                                start=k == 0, stop=k == 1)
                last.then_inc(q_done, 1)
                pe.wait_ge(qn_out, t + 1)
                for h in range(HEADS):
                    last = nc.tensor.matmul(psS[:, 3, h * P:(h + 1) * P], WKT[:, h], QN[:, h], start=True, stop=True)
                last.then_inc(qp_done, 1)
                pe.wait_ge(qp_out, t + 1)
                pe.wait_ge(qr_out, t + 1)

            def score(t, h):
                g = t * HEADS + h
                for c, (a, z) in enumerate(chunks):
                    if h or not isinstance(t, int):
                        pe.wait_ge(exp_done, (g - 1) * NCH + c + 1)
                    nc.tensor.matmul(psS[:, c, 0:z - a], QP[:, h], ckvT[:, a:z], start=True, stop=False)
                    nc.tensor.matmul(psS[:, c, 0:z - a], QR_[:, h], krT[:, a:z], start=False, stop=True).then_inc(s_done, 1)

            def weigh(t, h):
                g = t * HEADS + h
                s = h % 2
                pe.wait_ge(exp_done, (g + 1) * NCH)
                for j in range(NG + 1):
                    if j < NG:
                        a, z = groups[j]
                        if j >= 2 or h or not isinstance(t, int):
                            pe.wait_ge(t_out, g * NG + j - 1)
                        for q in range(a, z):
                            last = nc.tensor.transpose(psT[:, (j + h) % 2, (q - a) * P:(q - a + 1) * P], PM[:, s, q * P:(q + 1) * P], ident[:, :])
                        last.then_inc(t_done, 1)
                    if j:
                        a, z = groups[j - 1]
                        pe.wait_ge(t_out, g * NG + j)
                        if j == 1 and (h or not isinstance(t, int)):
                            pe.wait_ge(av_out, g)
                        for q in range(a, z):
                            last = nc.tensor.matmul(psO[:, 0:P], ckv[:, q], PT[:, q], start=q == 0, stop=q == KT - 1)
                last.then_inc(pv_done, 1)
                pe.wait_ge(ol_out, g + 1)
                nc.tensor.matmul(psO[:, P:2 * P], OL[:, :], WV[:, h], start=True, stop=True).then_inc(av_done, 1)
            heads(pe, start, score, weigh)

        @block.scalar
        def _(act):
            act.wait_ge(const_in, NCONST)

            def start(t):
                act.wait_ge(q_done, t + 1)
                nc.scalar.activation(QN[:, :], psS[:, 0].rearrange("p (h n) -> p h n", h=HEADS), ACT.Copy).then_inc(qn_out, 1)
                act.wait_ge(qp_done, t + 1)
                nc.scalar.activation(QP[:, :], psS[:, 3].rearrange("p (h n) -> p h n", h=HEADS), ACT.Copy).then_inc(qp_out, 1)

            def score(t, h):
                g = t * HEADS + h
                s = h % 2
                act.wait_ge(neg_max, g + 1)
                for c, (a, z) in enumerate(chunks):
                    if c == 0 and (h >= 2 or not isinstance(t, int)):
                        act.wait_ge(pv_done, g - 1)
                    nc.scalar.activation(PM[:, s, a:z], psS[:, c, 0:z - a], ACT.Exp, bias=top[:, s, 1:2], scale=SCALE,
                                         accum_out=stat[:, s, 1, c:c + 1]).then_inc(exp_done, 1)

            def weigh(t, h):
                g = t * HEADS + h
                s = h % 2
                act.wait_ge(pv_done, g + 1)
                nc.scalar.activation(OL[:, :], psO[:, 0:P], ACT.Copy).then_inc(ol_out, 1)
                act.wait_ge(inv_done, g + 1)
                act.wait_ge(av_done, g + 1)
                if h == 0 and not isinstance(t, int):
                    act.wait_ge(m_out, t * 16)
                nc.scalar.activation(MX[:, h * DV:(h + 1) * DV], psO[:, P:2 * P], ACT.Copy, scale=top[:, s, 3:4]).then_inc(av_out, 1)
            heads(act, start, score, weigh)

        @block.vector
        def _(dve):
            dve.wait_ge(const_in, NCONST)

            def start(t):
                dve.wait_ge(q_done, t + 1)
                cos = RF[:, 0, bass.ds(t * P, P)]
                sin = RF[:, 1, bass.ds(t * P, P)]
                for h in range(HEADS):
                    nc.vector.tensor_tensor(QR_[:, h], psS[0:ROPE, 1, h * P:(h + 1) * P], cos, ALU.mult)
                    last = nc.vector.tensor_tensor(QT[:, h], psS[0:ROPE, 2, h * P:(h + 1) * P], sin, ALU.mult)
                last.then_inc(qr_part, 1)
                dve.wait_ge(qr_part, t + 1)
                nc.vector.tensor_tensor(QR_[:, :], QR_[:, :], QT[:, :], ALU.add).then_inc(qr_out, 1)

            def score(t, h):
                g = t * HEADS + h
                s = h % 2
                for c, (a, z) in enumerate(chunks):
                    dve.wait_ge(s_done, g * NCH + c + 1)
                    last = nc.vector.reduce_max(stat[:, s, 0, c:c + 1], psS[:, c, 0:z - a], AXX)
                last.then_inc(c_max, 1)
                dve.wait_ge(c_max, g + 1)
                nc.vector.reduce_max(top[:, s, 0:1], stat[:, s, 0, 0:NCH], AXX).then_inc(h_max, 1)
                dve.wait_ge(h_max, g + 1)
                nc.vector.tensor_scalar(top[:, s, 1:2], top[:, s, 0:1], -SCALE, None, ALU.mult).then_inc(neg_max, 1)

            def weigh(t, h):
                g = t * HEADS + h
                s = h % 2
                for j, (a, z) in enumerate(groups):
                    dve.wait_ge(t_done, g * NG + j + 1)
                    if j == 0 and (h or not isinstance(t, int)):
                        dve.wait_ge(pv_done, g)
                    nc.vector.tensor_copy(PT[:, a:z], psT[:, (j + h) % 2, 0:(z - a) * P].rearrange("p (k n) -> p k n", n=P)).then_inc(t_out, 1)
                    if j == 0:
                        dve.wait_ge(exp_done, (g + 1) * NCH)
                        nc.vector.reduce_sum(top[:, s, 2:3], stat[:, s, 1, 0:NCH], AXX).then_inc(sums, 1)
                        dve.wait_ge(sums, g + 1)
                        nc.vector.reciprocal(top[:, s, 3:4], top[:, s, 2:3]).then_inc(inv_done, 1)
            heads(dve, start, score, weigh)


def gla(nc, name, proj_d, w_gate, b_gate, cum_d, rest_d, mask_d, ident_d, o_d, backward):
    C = P // 2
    order = (1, 0) if backward else (0, 1)
    edge = [0, C] if backward else [C - 1, P - 1]
    QK = HEADS * DK
    pairs = NA // 2

    def place(n):
        if not backward:
            return n
        if isinstance(n, int):
            return NC - 1 - n if n < NC else NA - 1 - n + NC
        return (n * -1) + (NA - 1 + NC)

    def n_positive(i, s):
        return n_above(i, s, 0)

    def n_above(i, s, k):
        return not (isinstance(i, int) and i * 2 + s <= k)

    def static(i):
        return isinstance(i, int) and i == 0

    with ExitStack() as ctx:
        m = Memory(nc, ctx, name)
        X = m.sbuf("x", [P, 2, 2 * QK])
        Z = m.sbuf("z", [P, 2, 2 * RANK])
        V = m.sbuf("v", [P, 2, HEADS * DV])
        ZT = m.sbuf("zt", [2 * RANK + 1, 2, P])
        WG = m.sbuf("wg", [2 * RANK + 1, QK])
        NEG = m.sbuf("neg", [P, QK])
        AB = m.sbuf("ab", [P, QK])
        LA = m.sbuf("la", [P, 2, QK])
        EB = m.sbuf("eb", [P, 2, 2 * QK])
        EN = m.sbuf("en", [P, 2, QK])
        QT = m.sbuf("qt", [P, 2, QK])
        KT = m.sbuf("kt", [P, 2, QK])
        KH = m.sbuf("kh", [P, 2, QK])
        AT = m.sbuf("at", [P, HEADS, P])
        SA = m.sbuf("sa", [P, 2, DV])
        SB = m.sbuf("sb", [P, 2, DV])
        O = m.sbuf("o", [P, 2, HEADS * DV])
        CUM = m.sbuf("cum", [P, P])
        REST = m.sbuf("rest", [P, P])
        MASK = m.sbuf("mask", [P, 2, P], I32)
        ident = m.sbuf("ident", [P, P])
        one = m.sbuf("one", [P, 1])
        psU = m.psum("psU", [P, BANK])
        psB = m.psum("psB", [P, BANK])
        psQ = m.psum("psQ", [P, BANK])
        psAO = m.psum("psAO", [P, 2, BANK])
        psS = m.psum("psS", [P, 2, BANK])
        const_in, set_up, one_set = m.sem("const_in"), m.sem("set_up"), m.sem("one_set")
        x_in = [m.sem(f"x_in{s}") for s in range(2)]
        v_in = [m.sem(f"v_in{s}") for s in range(2)]
        passed = m.sem("passed")
        z_done = m.sem("z_done")
        z_out = m.sem("z_out")
        u_done = m.sem("u_done")
        neg = m.sem("neg")
        ab = m.sem("ab")
        ex = m.sem("ex")
        ln = m.sem("ln")
        la_done = m.sem("la_done")
        b_done = m.sem("b_done")
        qk_done = m.sem("qk_done")
        eb_done = m.sem("eb_done")
        scaled = m.sem("scaled")
        ds_done = m.sem("ds_done")
        at_done = m.sem("at_done")
        at_out = m.sem("at_out")
        o_first = m.sem("o_first")
        o_done = m.sem("o_done")
        sb_done = m.sem("sb_done")
        sa_done = m.sem("sa_done")
        o_out = m.sem("o_out")
        stored = [m.sem(f"stored{s}") for s in range(2)]
        block = ctx.enter_context(nc.Block())
        NCONST = 16 * 6

        @block.sync
        def _(sp):
            sp.dma_start(ident[:, :], ident_d).then_inc(const_in, 16)
            sp.dma_start(CUM[:, :], cum_d).then_inc(const_in, 16)
            sp.dma_start(REST[:, :], rest_d).then_inc(const_in, 16)
            sp.dma_start(MASK[:, :], mask_d).then_inc(const_in, 16)
            for s in range(2):
                sp.sem_inc(stored[s], 16)
            sp.wait_ge(set_up, 4)
            a = RANK if backward else 0
            sp.dma_start(WG[a:a + RANK, :], w_gate).then_inc(const_in, 16)
            sp.dma_start(WG[2 * RANK:2 * RANK + 1, :], b_gate).then_inc(const_in, 16)
            sp.wait_ge(const_in, NCONST)

            def load_x(i, s):
                n = i * 2 + s
                t = place(n)
                sp.wait_ge(scaled, n + 1)
                sp.wait_ge(const_in, NCONST)
                sp.dma_start(X[:, s], rows(proj_d[:, COL_Q:COL_V], t)).then_inc(x_in[s], 16)
                sp.dma_start(Z[:, s], rows(proj_d[:, COL_Z:COL_R], t)).then_inc(x_in[s], 16)

            def load_v(i, s):
                n = i * 2 + s
                t = place(n)
                if isinstance(i, int) and i == 1:
                    sp.wait_ge(ds_done, n - 1)
                sp.wait_ge(o_done, n + 1)
                sp.wait_ge(const_in, NCONST)
                sp.dma_start(V[:, s], rows(proj_d[:, COL_V:COL_Z], t)).then_inc(v_in[s], 16)

            def store(i, s):
                n = i * 2 + s
                if static(i):
                    return
                t = place(n)
                sp.wait_ge(o_out, n - NC + 1)
                sp.wait_ge(const_in, NCONST)
                sp.dma_start(rows(o_d, t + (-NC)), O[:, s]).then_inc(stored[s], 16)
            staged(sp, pairs, load_x, load_v, store, apart=2)
            for s in range(2):
                sp.wait_ge(stored[s], 16 * pairs)

        @block.gpsimd
        def _(pool):
            pool.memset(WG[:, :], 0.0).then_inc(set_up, 1)
            pool.wait_ge(set_up, 1)
            pool.memset(AT[:, :], 0.0).then_inc(set_up, 1)
            pool.wait_ge(set_up, 2)
            pool.memset(SA[:, :], 0.0).then_inc(set_up, 1)
            pool.wait_ge(set_up, 3)
            pool.memset(ZT[2 * RANK:2 * RANK + 1, :], 1.0).then_inc(set_up, 1)

        @block.tensor
        def _(pe):
            pe.sem_inc(b_done, 2)
            pe.sem_inc(o_done, 2 + NC)
            pe.wait_ge(const_in, NCONST)
            pe.wait_ge(set_up, 4)

            def early(i, s):
                n = i * 2 + s
                pe.wait_ge(x_in[s], i * 32 + 32)
                if n_positive(i, s):
                    pe.wait_ge(ab, n)
                    pe.wait_ge(neg, n)
                nc.tensor.transpose(psU[0:2 * RANK, QK:QK + P], Z[:, s], ident[:, :]).then_inc(z_done, 1)
                pe.wait_ge(z_out, n + 1)
                nc.tensor.matmul(psU[:, 0:QK], ZT[:, s], WG[:, :], start=True, stop=True).then_inc(u_done, 1)

            def front(i, s):
                n = i * 2 + s
                pe.wait_ge(la_done, n + 1)
                if n_positive(i, s):
                    pe.wait_ge(eb_done, n)
                for p in range(2):
                    nc.tensor.matmul(psB[:, p * P:(p + 1) * P], LA[:, s, p * P:(p + 1) * P], CUM[:, :], start=True, stop=True)
                nc.tensor.matmul(psB[:, QK:2 * QK], REST[:, :], LA[:, s], start=True, stop=True).then_inc(b_done, 1)
                if n_positive(i, s):
                    pe.wait_ge(scaled, n + 2)
                for p in range(4):
                    last = nc.tensor.transpose(psQ[:, p * P:(p + 1) * P], X[:, s, p * P:(p + 1) * P], ident[:, :])
                last.then_inc(qk_done, 1)

            def back(i, s):
                n = i * 2 + s
                pe.wait_ge(scaled, n + 3)
                pe.wait_ge(v_in[s], i * 16 + 16)
                if n_positive(i, s):
                    pe.wait_ge(sa_done, n + 2)
                for c in range(2):
                    for p in range(2):
                        last = nc.tensor.matmul(psS[:, c, p * 2 * DV:(p + 1) * 2 * DV], KH[c * C:(c + 1) * C, s, p * P:(p + 1) * P],
                                                V[c * C:(c + 1) * C, s, p * 2 * DV:(p + 1) * 2 * DV], start=True, stop=True)
                last.then_inc(ds_done, 1)
                if static(i):
                    return
                if n_above(i, s, NC):
                    pe.wait_ge(o_out, n - NC)
                for h in range(HEADS):
                    r, p = h % 2 * C, h // 2
                    last = nc.tensor.matmul(psAO[:, h % 2, 2 * DV + p * P:2 * DV + (p + 1) * P], KT[r:r + C, s, p * P:(p + 1) * P],
                                            QT[r:r + C, s, p * P:(p + 1) * P], start=True, stop=True)
                last.then_inc(at_done, 1)
                pe.wait_ge(at_out, n - NC + 1)
                for k, c in enumerate(order):
                    if k:
                        pe.wait_ge(sb_done, n + 1)
                        pe.sem_inc(passed, 1)
                    S = SB if k else SA
                    for h in range(HEADS):
                        r, p = h % 2 * C, h // 2
                        out = psAO[:, h % 2, p * DV:(p + 1) * DV]
                        if k == 0:
                            nc.tensor.matmul(out, AT[:, h], V[:, s, h * DV:(h + 1) * DV], start=h < 2, stop=False, skip_group_check=True)
                        last = nc.tensor.matmul(out[c * C:(c + 1) * C], QT[r:r + C, s, p * P + c * C:p * P + (c + 1) * C],
                                                S[r:r + C, p], start=False, stop=k == 1, skip_group_check=True)
                    last.then_inc(o_done if k else o_first, 1)
            staged(pe, pairs, early, front, back, apart=2)

        @block.scalar
        def _(act):
            act.wait_ge(set_up, 4)

            def early(i, s):
                n = i * 2 + s
                act.wait_ge(ab, n + 1)
                nc.scalar.activation(AB[:, :], AB[:, :], ACT.Exp).then_inc(ex, 1)
                act.wait_ge(ex, n + 1)
                act.wait_ge(one_set, 1)
                nc.scalar.activation(AB[:, :], AB[:, :], ACT.Ln, bias=one[:, 0:1]).then_inc(ln, 1)

            def front(i, s):
                n = i * 2 + s
                act.wait_ge(b_done, n + 3)
                act.wait_ge(sa_done, n + 1)
                act.wait_ge(scaled, n + 1)
                nc.scalar.activation(EB[:, s], psB[:, :], ACT.Exp)
                nc.scalar.activation(EN[:, s], psB[:, 0:QK], ACT.Exp, scale=-1.0).then_inc(eb_done, 1)

            def back(i, s):
                n = i * 2 + s
                if static(i):
                    return
                act.wait_ge(o_done, n + 3)
                act.wait_ge(stored[s], i * 16)
                nc.scalar.activation(O[:, s].rearrange("p (a b v) -> p b a v", a=2, b=2), psAO[:, :, 0:2 * DV].rearrange("p b (a v) -> p b a v", a=2),
                                     ACT.Copy).then_inc(o_out, 1)
            staged(act, pairs, early, front, back, apart=2)

        @block.vector
        def _(dve):
            dve.sem_inc(scaled, 2)
            dve.sem_inc(sa_done, 2)
            nc.vector.memset(one[:, :], 1.0).then_inc(one_set, 1)
            dve.wait_ge(const_in, NCONST)
            dve.wait_ge(set_up, 4)

            def early(i, s):
                n = i * 2 + s
                dve.wait_ge(z_done, n + 1)
                nc.vector.tensor_copy(ZT[0:2 * RANK, s], psU[0:2 * RANK, QK:QK + P]).then_inc(z_out, 1)
                dve.wait_ge(u_done, n + 1)
                nc.vector.tensor_scalar(NEG[:, :], psU[:, 0:QK], 0.0, None, ALU.min).then_inc(neg, 1)
                dve.wait_ge(neg, n + 1)
                nc.vector.scalar_tensor_tensor(AB[:, :], NEG[:, :], 2.0, psU[:, 0:QK], ALU.mult, ALU.subtract).then_inc(ab, 1)
                dve.wait_ge(ln, n + 1)
                dve.wait_ge(b_done, n + 1)
                nc.vector.tensor_tensor(LA[:, s], NEG[:, :], AB[:, :], ALU.subtract).then_inc(la_done, 1)

            def front(i, s):
                n = i * 2 + s
                dve.wait_ge(eb_done, n + 1)
                dve.wait_ge(qk_done, n + 1)
                if n_above(i, s, 1):
                    dve.wait_ge(ds_done, n - 1)
                dve.wait_ge(o_done, n + 1)
                nc.vector.scalar_tensor_tensor(QT[:, s], psQ[:, 0:QK], float(DK) ** -0.5, EB[:, s, 0:QK], ALU.mult, ALU.mult)
                nc.vector.tensor_tensor(KT[:, s], psQ[:, QK:2 * QK], EN[:, s], ALU.mult)
                nc.vector.tensor_tensor(KH[:, s], X[:, s, QK:2 * QK], EB[:, s, QK:2 * QK], ALU.mult).then_inc(scaled, 1)

            def back(i, s):
                n = i * 2 + s
                if not static(i):
                    dve.wait_ge(at_done, n - NC + 1)
                    dve.sem_inc(passed, 1)
                    for b in range(2):
                        at = AT[:, :].rearrange("p (a b) n -> p b a n", b=2)[:, b]
                        last = nc.vector.copy_predicated(at, MASK[:, :], psAO[:, b, 2 * DV:2 * DV + 2 * P].rearrange("p (a n) -> p a n", a=2))
                    last.then_inc(at_out, 1)
                dve.wait_ge(ds_done, n + 1)
                for k, c in enumerate(order):
                    old, new = (SB, SA) if k else (SA, SB)
                    if k:
                        dve.wait_ge(sb_done, n + 1)
                        if not static(i):
                            dve.wait_ge(o_first, n - NC + 1)
                    elif n_positive(i, s):
                        dve.wait_ge(sa_done, n + 2)
                        dve.wait_ge(o_done, n + 2)
                    for p in range(2):
                        for r in range(2):
                            q = slice(r * C, (r + 1) * C)
                            last = nc.vector.scalar_tensor_tensor(new[q, p], old[q, p], EB[q, s, p * P + edge[c]:p * P + edge[c] + 1],
                                                                  psS[q, c, (p * 2 + r) * DV:(p * 2 + r + 1) * DV], ALU.mult, ALU.add)
                    last.then_inc(sa_done if k else sb_done, 1)
            staged(dve, pairs, early, front, back, apart=2)

def gla_finish(nc, of_d, ob_d, proj_d, g, mix_d):
    pairs = NT // 2
    W = HEADS * DV
    with ExitStack() as ctx:
        m = Memory(nc, ctx, "gf")
        F = m.sbuf("f", [P, 2, W])
        B = m.sbuf("b", [P, 2, W])
        R = m.sbuf("r", [P, 2, W])
        S = m.sbuf("s", [P, 2, W])
        G = m.sbuf("g", [P, W])
        M = m.sbuf("m", [P, 2, W])
        junk = m.sbuf("junk", [P, W])
        stat = m.sbuf("stat", [P, 2, 3, HEADS])
        eps = m.sbuf("eps", [P, 1])
        const_in, eps_set = m.sem("const_in"), m.sem("eps_set")
        t_in = [m.sem(f"t_in{s}") for s in range(2)]
        summed = m.sem("summed")
        silu = m.sem("silu")
        squared = m.sem("squared")
        rooted = m.sem("rooted")
        gated = m.sem("gated")
        inverted = m.sem("inverted")
        done = m.sem("done")
        stored = [m.sem(f"stored{s}") for s in range(2)]
        block = ctx.enter_context(nc.Block())

        @block.sync
        def _(sp):
            for h in range(HEADS):
                sp.dma_start(G[:, h * DV:(h + 1) * DV], g.to_broadcast([P, DV])).then_inc(const_in, 16)
            sp.wait_ge(const_in, 16 * HEADS)
            for s in range(2):
                sp.sem_inc(stored[s], 16)

            def load(i, s):
                n = i * 2 + s
                sp.wait_ge(done, n + 1)
                sp.wait_ge(const_in, 16 * HEADS)
                sp.dma_start(F[:, s], rows(of_d, n)).then_inc(t_in[s], 16)
                sp.dma_start(B[:, s], rows(ob_d, n)).then_inc(t_in[s], 16)
                sp.dma_start(R[:, s], rows(proj_d[:, COL_R:COL_CQ], n + NC)).then_inc(t_in[s], 16)

            def store(i, s):
                n = i * 2 + s
                sp.wait_ge(done, n + 3)
                sp.wait_ge(const_in, 16 * HEADS)
                sp.dma_start(rows(mix_d[:, 0:W], n), M[:, s]).then_inc(stored[s], 16)
            staged(sp, pairs, load, nothing, store)
            for s in range(2):
                sp.wait_ge(stored[s], 16 * (pairs + 1))

        @block.scalar
        def _(act):
            act.wait_ge(eps_set, 1)

            def front(i, s):
                n = i * 2 + s
                act.wait_ge(summed, n + 1)
                for h in range(HEADS):
                    last = nc.scalar.activation(junk[:, h * DV:(h + 1) * DV], F[:, s, h * DV:(h + 1) * DV], ACT.Square,
                                                accum_out=stat[:, s, 0, h:h + 1])
                last.then_inc(squared, 1)
                act.wait_ge(squared, n + 1)
                nc.scalar.activation(stat[:, s, 1], stat[:, s, 0], ACT.Sqrt, bias=eps[:, 0:1], scale=1.0 / DV).then_inc(rooted, 1)
                nc.scalar.activation(S[:, s], R[:, s], ACT.Silu).then_inc(silu, 1)
            staged(act, pairs, nothing, front, nothing)

        @block.vector
        def _(dve):
            dve.sem_inc(done, 2)
            nc.vector.memset(eps[:, :], EPS).then_inc(eps_set, 1)
            dve.wait_ge(const_in, 16 * HEADS)

            def early(i, s):
                n = i * 2 + s
                dve.wait_ge(t_in[s], i * 48 + 48)
                nc.vector.tensor_tensor(F[:, s], F[:, s], B[:, s], ALU.add).then_inc(summed, 1)

            def front(i, s):
                n = i * 2 + s
                dve.wait_ge(silu, n + 1)
                nc.vector.tensor_tensor(S[:, s], S[:, s], G[:, :], ALU.mult).then_inc(gated, 1)
                nc.vector.reciprocal(stat[:, s, 2], stat[:, s, 1]).then_inc(inverted, 1)
                dve.wait_ge(gated, n + 1)
                dve.wait_ge(inverted, n + 1)
                dve.wait_ge(stored[s], i * 16 + 16)
                for h in range(HEADS):
                    q = slice(h * DV, (h + 1) * DV)
                    last = nc.vector.scalar_tensor_tensor(M[:, s, q], F[:, s, q], stat[:, s, 2, h:h + 1], S[:, s, q], ALU.mult, ALU.mult)
                last.then_inc(done, 1)
            staged(dve, pairs, early, front, nothing)


def fourier_channels(nc, hT_d, dft_d, alt_d, wa_d, wb_d, g_d):
    GR = 4
    NB = SEQ // BANK
    TB = BANK // P
    with ExitStack() as ctx:
        m = Memory(nc, ctx, "fc")
        H = m.sbuf("h", [P, 2, KD, BANK])
        AT = m.sbuf("at", [P, 2 * GR, BANK])
        AL = m.sbuf("al", [GR, BANK])
        DF = m.sbuf("df", [P, 2, 2, P])
        ALT = m.sbuf("alt", [P, KD, GR])
        WA = m.sbuf("wa", [P, GR, D])
        WB = m.sbuf("wb", [P, GR, D])
        WP = m.sbuf("wp", [P, GR, D])
        WM = m.sbuf("wm", [GR, D])
        sign = m.sbuf("sign", [P, 2])
        O = m.sbuf("o", [P, 2, 2, D])
        psA = m.psum("psA", [P, 2, BANK])
        psL = m.psum("psL", [P, BANK])
        psG = m.psum("psG", [P, 4, BANK])
        const_in, folded, set_up = m.sem("const_in"), m.sem("folded"), m.sem("set_up")
        h_in = [m.sem(f"h_in{s}") for s in range(2)]
        a_done = m.sem("a_done")
        a_out = m.sem("a_out")
        al_done, al_out = m.sem("al_done"), m.sem("al_out")
        g_done = m.sem("g_done")
        g_out = m.sem("g_out")
        stored = [m.sem(f"stored{s}") for s in range(2)]
        block = ctx.enter_context(nc.Block())

        @block.sync
        def _(sp):
            sp.dma_start(DF[:, :], dft_d).then_inc(const_in, 16)
            sp.dma_start(ALT[:, :], alt_d).then_inc(const_in, 16)
            sp.dma_start(WA[:, :], wa_d).then_inc(const_in, 16)
            sp.dma_start(WB[:, :], wb_d).then_inc(const_in, 16)
            sp.dma_start(WM[:, :], wb_d[0]).then_inc(const_in, 16)
            for s in range(2):
                sp.sem_inc(stored[s], 16)
            sp.wait_ge(const_in, 80)
            for s in range(2):
                sp.dma_start(H[:, s], hT_d[:, :, s * BANK:(s + 1) * BANK]).then_inc(h_in[s], 16)
            gv = g_d.rearrange("c (t p) n -> t p c n", p=P)
            for b in range(NB):
                for t in range(TB):
                    n = b * TB + t
                    sp.wait_ge(g_out, (n + 1) * 4)
                    sp.dma_start(gv[n], O[:, n % 2]).then_inc(stored[n % 2], 16)
                    if t == 0 and 1 <= b < NB - 1:
                        sp.dma_start(H[:, (b + 1) % 2], hT_d[:, :, (b + 1) * BANK:(b + 2) * BANK]).then_inc(h_in[(b + 1) % 2], 16)
            for s in range(2):
                sp.wait_ge(stored[s], 16 * (NT // 2 + 1))

        @block.tensor
        def _(pe):
            pe.wait_ge(const_in, 80)
            pe.wait_ge(folded, 2)
            for b in range(NB):
                s = b % 2
                pe.wait_ge(h_in[s], 16 * (b // 2 + 1))
                for q in range(2 * GR):
                    g, j = q // 2, q % 2
                    if b * 2 * GR + q >= 2:
                        pe.wait_ge(a_out, b * 2 * GR + q - 1)
                    for k in range(2):
                        last = nc.tensor.matmul(psA[:, q % 2], DF[:, k, j], H[:, s, 2 * g + k], start=k == 0, stop=k == 1)
                    last.then_inc(a_done, 1)
                if b:
                    pe.wait_ge(al_out, b)
                for k in range(KD):
                    last = nc.tensor.matmul(psL[0:GR, :], ALT[:, k], H[:, s, k], start=k == 0, stop=k == KD - 1)
                last.then_inc(al_done, 1)
                pe.wait_ge(a_out, (b + 1) * 2 * GR)
                pe.wait_ge(al_out, b + 1)
                for t in range(TB):
                    for c in range(2):
                        for h in range(2):
                            n = (b * TB + t) * 4 + c * 2 + h
                            if n >= 4:
                                pe.wait_ge(g_out, n - 3)
                            W = (WP, WA)[c]
                            for g in range(GR):
                                last = nc.tensor.matmul(psG[:, n % 4], AT[:, 2 * g + c, t * P:(t + 1) * P], W[:, g, h * BANK:(h + 1) * BANK],
                                                        start=g == 0, stop=c == 1 and g == GR - 1)
                            if c == 0:
                                last = nc.tensor.matmul(psG[:, n % 4], AL[:, t * P:(t + 1) * P], WM[:, h * BANK:(h + 1) * BANK],
                                                        start=False, stop=True)
                            last.then_inc(g_done, 1)

        @block.scalar
        def _(act):
            for b in range(NB):
                act.wait_ge(al_done, b + 1)
                nc.scalar.activation(AL[:, :], psL[0:GR, :], ACT.Copy).then_inc(al_out, 1)
                for t in range(TB):
                    i = b * TB + t
                    act.wait_ge(stored[i % 2], 16 * (i // 2 + 1))
                    for c in range(2):
                        for h in range(2):
                            n = i * 4 + c * 2 + h
                            act.wait_ge(g_done, n + 1)
                            nc.scalar.activation(O[:, i % 2, c, h * BANK:(h + 1) * BANK], psG[:, n % 4], ACT.Copy).then_inc(g_out, 1)

        @block.vector
        def _(dve):
            nc.vector.memset(sign[:, 0:1], 1.0).then_inc(set_up, 1)
            nc.vector.memset(sign[:, 1:2], -1.0).then_inc(set_up, 1)
            dve.wait_ge(set_up, 2)
            nc.vector.memset(sign[0:1, :], 0.0).then_inc(set_up, 1)
            dve.wait_ge(const_in, 80)
            dve.wait_ge(set_up, 3)
            nc.vector.scalar_tensor_tensor(WP[:, :], WB[:, :], sign[:, 0:1], WA[:, :], ALU.mult, ALU.add).then_inc(folded, 1)
            dve.wait_ge(folded, 1)
            nc.vector.scalar_tensor_tensor(WA[:, :], WB[:, :], sign[:, 1:2], WA[:, :], ALU.mult, ALU.add).then_inc(folded, 1)
            for b in range(NB):
                for q in range(2 * GR):
                    n = b * 2 * GR + q
                    dve.wait_ge(a_done, n + 1)
                    nc.vector.tensor_copy(AT[:, q], psA[:, q % 2]).then_inc(a_out, 1)


def fourier_tokens(nc, g_d, tw_d, y_d):
    J = 4
    TQ = NT // J
    with ExitStack() as ctx:
        m = Memory(nc, ctx, "ft")
        bufs = [m.sbuf(f"g{i}", [P, 2, J, TQ, BANK]) for i in range(2)]
        TW = m.sbuf("tw", [P, 2, TQ, 2, P])
        O = m.sbuf("o", [P, 2, BANK])
        psY = m.psum("psY", [P, 2, BANK])
        g_in = m.sem("g_in")
        v_step, p_step = m.sem("v_step"), m.sem("p_step")
        tw_in = [m.sem(f"tw_in{s}") for s in range(2)]
        y_done = m.sem("y_done")
        y_out = m.sem("y_out")
        half = m.sem("half")
        stored = [m.sem(f"stored{s}") for s in range(2)]
        block = ctx.enter_context(nc.Block())
        PER = J * TQ
        yv = y_d.rearrange("(k p r) n -> r k p n", p=P, r=J)
        twv = tw_d
        gv = g_d.rearrange("c (j t p) n -> p c j t n", p=P, t=TQ)

        def buffers(h):
            return (bufs[0], bufs[1]) if h == 0 else (bufs[1], bufs[0])

        def first(h, c, j):
            X, Y = buffers(h)
            return ((Y[:, c, j], X[:, c, j], X[:, c, j + 2], ALU.add),
                    (Y[:, c, j + 2], X[:, c, j], X[:, c, j + 2], ALU.subtract))

        def second(h):
            X, Y = buffers(h)
            even = [(X[:, c, r], Y[:, c, 0], Y[:, c, 1], op) for c in range(2) for r, op in ((0, ALU.add), (2, ALU.subtract))]
            odd = [(X[:, 0, 1], Y[:, 0, 2], Y[:, 1, 3], ALU.subtract), (X[:, 1, 1], Y[:, 1, 2], Y[:, 0, 3], ALU.add),
                   (X[:, 0, 3], Y[:, 0, 2], Y[:, 1, 3], ALU.add), (X[:, 1, 3], Y[:, 1, 2], Y[:, 0, 3], ALU.subtract)]
            return even, odd

        @block.sync
        def _(sp):
            for s in range(2):
                sp.sem_inc(stored[s], 16)
            for h in range(2):
                if h:
                    sp.wait_ge(v_step, 12)
                    sp.wait_ge(p_step, 4)
                for c in range(2):
                    for j in range(J):
                        sp.dma_start(buffers(h)[0][:, c, j], gv[:, c, j, :, h * BANK:(h + 1) * BANK]).then_inc(g_in, 16)
                with sp.Fori(0, J) as r:
                    for k in range(TQ):
                        s = k % 2
                        n = r * TQ + (h * PER + k)
                        sp.wait_ge(y_done, n + 1)
                        sp.wait_ge(g_in, 128 * (h + 1))
                        sp.dma_start(TW[:, s], twv[bass.ds(r, 1), k].rearrange("a p t c n -> p (a t) c n")).then_inc(tw_in[s], 16)
                        sp.wait_ge(y_out, n + 3)
                        sp.wait_ge(g_in, 128 * (h + 1))
                        sp.dma_start(yv[bass.ds(r, 1), k, :, h * BANK:(h + 1) * BANK].rearrange("a p n -> p (a n)"), O[:, s]).then_inc(stored[s], 16)
            for s in range(2):
                sp.wait_ge(stored[s], 16 * (PER + 1))

        @block.gpsimd
        def _(pool):
            for h in range(2):
                pool.wait_ge(g_in, 128 * (h + 1))
                if h:
                    pool.wait_ge(y_done, 2 + PER)
                for out, a, b, op in first(h, 1, 1):
                    nc.gpsimd.tensor_tensor(out, a, b, op).then_inc(p_step, 1)
                pool.wait_ge(v_step, h * 12 + 6)
                pool.wait_ge(p_step, h * 4 + 2)
                for out, a, b, op in second(h)[1][2:]:
                    nc.gpsimd.tensor_tensor(out, a, b, op).then_inc(p_step, 1)

        @block.vector
        def _(dve):
            for h in range(2):
                dve.wait_ge(g_in, 128 * (h + 1))
                if h:
                    dve.wait_ge(y_done, 2 + PER)
                for c, j in ((0, 0), (0, 1), (1, 0)):
                    for out, a, b, op in first(h, c, j):
                        nc.vector.tensor_tensor(out, a, b, op).then_inc(v_step, 1)
                dve.wait_ge(v_step, h * 12 + 6)
                dve.wait_ge(p_step, h * 4 + 2)
                even, odd = second(h)
                for out, a, b, op in even + odd[:2]:
                    nc.vector.tensor_tensor(out, a, b, op).then_inc(v_step, 1)

        @block.tensor
        def _(pe):
            pe.sem_inc(y_done, 2)
            for h in range(2):
                X = buffers(h)[0]
                pe.wait_ge(v_step, (h + 1) * 12)
                pe.wait_ge(p_step, (h + 1) * 4)
                with pe.Fori(0, J) as r:
                    for k in range(TQ):
                        s = k % 2
                        n = r * TQ + (h * PER + k)
                        pe.wait_ge(tw_in[s], (r * (TQ // 2) + (h * PER // 2 + k // 2 + 1)) * 16)
                        pe.wait_ge(y_out, n + 1)
                        for t in range(TQ):
                            for c in range(2):
                                last = nc.tensor.matmul(psY[:, s], TW[:, s, t, c], X[:, c, bass.ds(r, 1), t].rearrange("p a n -> p (a n)"),
                                                        start=t == 0 and c == 0, stop=t == TQ - 1 and c == 1)
                        last.then_inc(y_done, 1)

        @block.scalar
        def _(act):
            act.sem_inc(y_out, 2)
            with act.Fori(0, 2 * PER // 2) as i:
                for s in range(2):
                    n = i * 2 + s
                    act.wait_ge(y_done, n + 3)
                    act.wait_ge(stored[s], i * 16 + 16)
                    nc.scalar.activation(O[:, s], psY[:, s], ACT.Copy).then_inc(y_out, 1)


def router(nc, hT_d, w_router, iota_d, ident_d, gates_d, picks_d):
    NE = w_router.shape[1]
    NB = SEQ // BANK
    with ExitStack() as ctx:
        m = Memory(nc, ctx, "rt")
        H = m.sbuf("h", [P, 2, KD, BANK])
        W = m.sbuf("w", [P, KD, NE])
        LT = m.sbuf("lt", [NE, SEQ])
        L = m.sbuf("l", [P, NT, NE])
        TOP = m.sbuf("top", [P, NT, 8])
        IX = m.sbuf("ix", [P, NT, 8], U32)
        IF = m.sbuf("if", [P, NT, 8])
        GG = m.sbuf("gg", [P, 4, NT])
        IO = m.sbuf("io", [P, NE])
        PK = m.sbuf("pk", [P, 2, NT])
        ON = m.sbuf("on", [P, NT, NE])
        O2 = m.sbuf("o2", [P, NT, NE])
        ident = m.sbuf("ident", [P, P])
        psL = m.psum("psL", [P, 2, BANK])
        psT = m.psum("psT", [P, BANK])
        const_in = m.sem("const_in")
        h_in = [m.sem(f"h_in{s}") for s in range(2)]
        l_done, l_out, t_done, chain, ex, stored = (m.sem(n) for n in ("l_done", "l_out", "t_done", "chain", "ex", "stored"))
        block = ctx.enter_context(nc.Block())

        @block.sync
        def _(sp):
            sp.dma_start(W[:, :], w_router.rearrange("(k p) e -> p k e", p=P)).then_inc(const_in, 16)
            sp.dma_start(ident[:, :], ident_d).then_inc(const_in, 16)
            sp.dma_start(IO[:, :], iota_d.to_broadcast([P, NE])).then_inc(const_in, 16)
            for b in range(NB):
                if b >= 2:
                    sp.wait_ge(l_done, b - 1)
                sp.dma_start(H[:, b % 2], hT_d[:, :, b * BANK:(b + 1) * BANK]).then_inc(h_in[b % 2], 16)
            sp.wait_ge(chain, 7)
            sp.dma_start(gates_d, ON[:, :]).then_inc(stored, 16)
            sp.dma_start(picks_d, PK[:, :]).then_inc(stored, 16)
            sp.wait_ge(stored, 32)

        @block.tensor
        def _(pe):
            pe.wait_ge(const_in, 48)
            for b in range(NB):
                pe.wait_ge(h_in[b % 2], 16 * (b // 2 + 1))
                if b >= 2:
                    pe.wait_ge(l_out, b - 1)
                for k in range(KD):
                    last = nc.tensor.matmul(psL[0:NE, b % 2], W[:, k], H[:, b % 2, k], start=k == 0, stop=k == KD - 1)
                last.then_inc(l_done, 1)
            pe.wait_ge(l_out, NB)
            for t in range(NT):
                last = nc.tensor.transpose(psT[:, t * NE:(t + 1) * NE], LT[:, t * P:(t + 1) * P], ident[0:NE, 0:NE])
            last.then_inc(t_done, 1)

        @block.scalar
        def _(act):
            act.wait_ge(chain, 3)
            nc.scalar.activation(GG[:, 1], GG[:, 0], ACT.Exp).then_inc(ex, 1)

        @block.vector
        def _(dve):
            for b in range(NB):
                dve.wait_ge(l_done, b + 1)
                nc.vector.tensor_copy(LT[:, b * BANK:(b + 1) * BANK], psL[0:NE, b % 2]).then_inc(l_out, 1)
            dve.wait_ge(t_done, 1)
            nc.vector.tensor_copy(L[:, :], psT[:, 0:NT * NE].rearrange("p (t e) -> p t e", t=NT)).then_inc(chain, 1)
            dve.wait_ge(chain, 1)
            for t in range(NT):
                last = nc.vector.max(TOP[:, t], L[:, t])
            last.then_inc(chain, 1)
            dve.wait_ge(chain, 2)
            for t in range(NT):
                last = nc.vector.max_index(IX[:, t], TOP[:, t], L[:, t])
            nc.vector.tensor_tensor(GG[:, 0], TOP[:, :, 1], TOP[:, :, 0], ALU.subtract).then_inc(chain, 1)
            dve.wait_ge(ex, 1)
            nc.vector.tensor_scalar(GG[:, 2], GG[:, 1], 1.0, None, ALU.add)
            for q in range(2):
                nc.vector.tensor_copy(PK[:, q], IX[:, :, q])
            nc.vector.tensor_copy(IF[:, :], IX[:, :]).then_inc(chain, 1)
            dve.wait_ge(chain, 4)
            nc.vector.reciprocal(GG[:, 2], GG[:, 2]).then_inc(chain, 1)
            dve.wait_ge(chain, 5)
            nc.vector.tensor_tensor(GG[:, 3], GG[:, 1], GG[:, 2], ALU.mult).then_inc(chain, 1)
            dve.wait_ge(const_in, 48)
            dve.wait_ge(chain, 6)
            for t in range(NT):
                nc.vector.tensor_scalar(ON[:, t], IO[:, :], IF[:, t, 0:1], GG[:, 2, t:t + 1], ALU.is_equal, ALU.mult)
                last = nc.vector.tensor_scalar(O2[:, t], IO[:, :], IF[:, t, 1:2], GG[:, 3, t:t + 1], ALU.is_equal, ALU.mult)
            last.then_inc(ex, 1)
            dve.wait_ge(ex, 2)
            nc.vector.tensor_tensor(ON[:, :], ON[:, :], O2[:, :], ALU.add).then_inc(chain, 1)


NE = 8
MAXB = 44


def positions(nc, gates_d, picks_d, tri_d, ones_d, POS, GK, counts_d):
    with ExitStack() as ctx:
        m = Memory(nc, ctx, "po")
        GA = m.sbuf("ga", [P, NT, NE])
        PK = m.sbuf("pk", [P, 2, NT])
        ON = m.sbuf("on", [P, 2, NT, NE])
        M = m.sbuf("m", [P, NT, NE])
        TMP = m.sbuf("tmp", [P, NT, NE])
        EX = m.sbuf("ex", [P, NT, NE])
        RK = m.sbuf("rk", [P, NT, NE])
        IO = m.sbuf("io", [P, NE])
        N = m.sbuf("n", [P, NE])
        NI = m.sbuf("ni", [P, NE], I32)
        NB = m.sbuf("nb", [P, NE])
        B0 = m.sbuf("b0", [P, NE])
        CI = m.sbuf("ci", [P, 2, NE], I32)
        PF = m.sbuf("pf", [P, 2, NT])
        TRI = m.sbuf("tri", [P, P])
        ONE = m.sbuf("one", [P, P])
        psR = m.psum("psR", [P, BANK])
        psC = m.psum("psC", [P, BANK])
        const_in, step, prefix, stored = m.sem("const_in"), m.sem("step"), m.sem("prefix"), m.sem("stored")
        masks, block_out = m.sem("masks"), m.sem("block_out")
        block = ctx.enter_context(nc.Block())

        @block.sync
        def _(sp):
            sp.dma_start(GA[:, :], gates_d).then_inc(const_in, 16)
            sp.dma_start(PK[:, :], picks_d).then_inc(const_in, 16)
            sp.dma_start(TRI[:, :], tri_d).then_inc(const_in, 16)
            sp.dma_start(ONE[:, :], ones_d).then_inc(const_in, 16)
            sp.wait_ge(block_out, 1)
            sp.dma_start(counts_d, CI[0:1, :]).then_inc(stored, 16)
            sp.wait_ge(stored, 16)

        @block.tensor
        def _(pe):
            pe.wait_ge(const_in, 64)
            pe.wait_ge(masks, 1)
            mv = M[:, :].rearrange("p t e -> p (t e)")
            nc.tensor.matmul(psR[:, 0:NT * NE], TRI[:, :], mv, start=True, stop=True)
            nc.tensor.matmul(psC[:, 0:NT * NE], ONE[:, :], mv, start=True, stop=True).then_inc(prefix, 1)

        @block.vector
        def _(dve):
            n = [0]

            def then(ins):
                ins.then_inc(step, 1)
                n[0] += 1
                dve.wait_ge(step, n[0])
            dve.wait_ge(const_in, 64)
            for e in range(NE):
                for k in range(2):
                    last = nc.vector.tensor_scalar(ON[:, k, :, e], PK[:, k], float(e), None, ALU.is_equal)
            then(last)
            nc.vector.tensor_tensor(M[:, :], ON[:, 0], ON[:, 1], ALU.add).then_inc(masks, 1)
            for k in range(2):
                then(nc.vector.tensor_tensor(TMP[:, :], ON[:, k], GA[:, :], ALU.mult))
                then(nc.vector.reduce_sum(GK[:, k], TMP[:, :], AXX))
            dve.wait_ge(prefix, 1)
            pc = psC[:, 0:NT * NE].rearrange("p (t e) -> p t e", t=NT)
            then(nc.vector.memset(EX[:, 0], 0.0))
            for t in range(1, NT):
                then(nc.vector.tensor_tensor(EX[:, t], pc[:, t - 1], EX[:, t - 1], ALU.add))
            then(nc.vector.tensor_tensor(N[:, :], pc[:, NT - 1], EX[:, NT - 1], ALU.add))
            then(nc.vector.tensor_tensor(RK[:, :], psR[:, 0:NT * NE].rearrange("p (t e) -> p t e", t=NT), EX[:, :], ALU.add))
            then(nc.vector.tensor_scalar(NI[:, :], N[:, :], float(P - 1), None, ALU.add))
            then(nc.vector.tensor_scalar(NI[:, :], NI[:, :], 7, None, ALU.logical_shift_right))
            then(nc.vector.tensor_scalar(NB[:, :], NI[:, :], 2.0, None, ALU.max))
            then(nc.vector.memset(B0[:, 0:1], 0.0))
            for e in range(1, NE):
                then(nc.vector.tensor_tensor(B0[:, e:e + 1], B0[:, e - 1:e], NB[:, e - 1:e], ALU.add))
            nc.vector.tensor_copy(CI[:, 0], NB[:, :])
            then(nc.vector.tensor_copy(CI[:, 1], B0[:, :]))
            then(nc.vector.tensor_scalar(B0[:, :], B0[:, :], float(P), None, ALU.mult))
            for t in range(NT):
                last = nc.vector.tensor_tensor(RK[:, t], RK[:, t], B0[:, :], ALU.add)
            then(last)
            for k in range(2):
                then(nc.vector.tensor_tensor(TMP[:, :], ON[:, k], RK[:, :], ALU.mult))
                then(nc.vector.reduce_sum(PF[:, k], TMP[:, :], AXX))
            nc.vector.tensor_copy(POS[:, :], PF[:, :]).then_inc(block_out, 1)


def spread(nc, xn_d, POS, xs_d):
    with ExitStack() as ctx:
        m = Memory(nc, ctx, "sp")
        DEPTH = 4
        X = m.sbuf("x", [P, DEPTH, D])
        x_in = [m.sem(f"x_in{s}") for s in range(DEPTH)]
        out = [m.software_sem(f"out{s}") for s in range(DEPTH)]
        block = ctx.enter_context(nc.Block())

        @block.sync
        def _(sp):
            for t in range(NT):
                if t >= DEPTH:
                    sp.wait_ge(out[t % DEPTH], 32 * (t // DEPTH))
                sp.dma_start(X[:, t % DEPTH], rows(xn_d, t)).then_inc(x_in[t % DEPTH], 16)

        @block.gpsimd
        def _(pool):
            for t in range(NT):
                s = t % DEPTH
                pool.wait_ge(x_in[s], 16 * (t // DEPTH + 1))
                for k in range(2):
                    pool.indirect_dma_start(out=xs_d, out_offset=bass.IndirectOffsetOnAxis(ap=POS[:, k, t:t + 1], axis=0),
                                            in_=X[:, s], in_offset=None).then_inc(out[s], 16)
            for s in range(DEPTH):
                pool.wait_ge(out[s], 32 * (NT // DEPTH))


def combine(nc, ys_d, POS, GK, y_d):
    pairs = NT // 2
    with ExitStack() as ctx:
        m = Memory(nc, ctx, "cb")
        Y = m.sbuf("y", [P, 2, 2, D])
        O = m.sbuf("o", [P, 2, D])
        T = m.sbuf("t", [P, 2, D])
        y_in = [m.software_sem(f"y_in{s}") for s in range(2)]
        first, done = m.sem("first"), m.sem("done")
        stored = [m.sem(f"stored{s}") for s in range(2)]
        block = ctx.enter_context(nc.Block())

        @block.gpsimd
        def _(pool):
            for t in range(NT):
                if t >= 2:
                    pool.wait_ge(done, t - 1)
                for k in range(2):
                    pool.indirect_dma_start(out=Y[:, t % 2, k], out_offset=None, in_=ys_d,
                                            in_offset=bass.IndirectOffsetOnAxis(ap=POS[:, k, t:t + 1], axis=0)).then_inc(y_in[t % 2], 16)

        @block.vector
        def _(dve):
            for t in range(NT):
                s = t % 2
                dve.wait_ge(y_in[s], 32 * (t // 2 + 1))
                nc.vector.tensor_scalar(T[:, s], Y[:, s, 0], GK[:, 0, t:t + 1], None, ALU.mult).then_inc(first, 1)
                dve.wait_ge(first, t + 1)
                if t >= 2:
                    dve.wait_ge(stored[s], 16 * (t // 2))
                nc.vector.scalar_tensor_tensor(O[:, s], Y[:, s, 1], GK[:, 1, t:t + 1], T[:, s], ALU.mult, ALU.add).then_inc(done, 1)

        @block.sync
        def _(sp):
            for t in range(NT):
                sp.wait_ge(done, t + 1)
                sp.dma_start(rows(y_d, t), O[:, t % 2]).then_inc(stored[t % 2], 16)
            for s in range(2):
                sp.wait_ge(stored[s], 16 * pairs)


def transpose_rows(nc, xs_d, cols, xT_d, ident_d):
    pairs = MAXB // 2
    with ExitStack() as ctx:
        m = Memory(nc, ctx, "tr")
        X = m.sbuf("x", [P, 2, D])
        HT = m.sbuf("ht", [P, 2, KD, P])
        mod = m.sbuf("mod", [P, 2, KD])
        ident = m.sbuf("ident", [P, P])
        psT = m.psum("psT", [P, 2, 2, BANK])
        const_in = m.sem("const_in")
        x_in = [m.sem(f"x_in{s}") for s in range(2)]
        tr_done = m.sem("tr_done")
        ht_a, ht_v = m.sem("ht_a"), m.sem("ht_v")
        h_out = [m.sem(f"h_out{s}") for s in range(2)]
        block = ctx.enter_context(nc.Block())

        @block.sync
        def _(sp):
            sp.dma_start(ident[:, :], ident_d).then_inc(const_in, 16)
            sp.dma_start(mod[:, :], cols).then_inc(const_in, 16)
            sp.wait_ge(const_in, 32)
            for s in range(2):
                sp.sem_inc(h_out[s], 16)

            def load(i, s):
                sp.wait_ge(tr_done, i * 2 + s + 1)
                sp.wait_ge(const_in, 32)
                sp.dma_start(X[:, s], rows(xs_d, i * 2 + s)).then_inc(x_in[s], 16)

            def store(i, s):
                n = i * 2 + s
                sp.wait_ge(ht_a, n + 3)
                sp.wait_ge(ht_v, n + 3)
                sp.wait_ge(const_in, 32)
                sp.dma_start(xT_d[:, :, bass.ds(n * P, P)], HT[:, s]).then_inc(h_out[s], 16)
            staged(sp, pairs, load, nothing, store)
            for s in range(2):
                sp.wait_ge(h_out[s], 16 * (pairs + 1))

        @block.tensor
        def _(pe):
            pe.sem_inc(tr_done, 2)
            pe.wait_ge(const_in, 32)

            def front(i, s):
                n = i * 2 + s
                pe.wait_ge(x_in[s], i * 16 + 16)
                pe.wait_ge(ht_a, n + 1)
                pe.wait_ge(ht_v, n + 1)
                for k in range(KD):
                    last = nc.tensor.transpose(psT[:, s, k // 4, k % 4 * P:(k % 4 + 1) * P], X[:, s, k * P:(k + 1) * P], ident[:, :])
                last.then_inc(tr_done, 1)
            staged(pe, pairs, nothing, front, nothing)

        @block.scalar
        def _(act):
            act.sem_inc(ht_a, 2)
            act.wait_ge(const_in, 32)

            def front(i, s):
                act.wait_ge(tr_done, i * 2 + s + 3)
                act.wait_ge(h_out[s], i * 16 + 16)
                for k in range(4, 8):
                    last = nc.scalar.activation(HT[:, s, k], psT[:, s, 1, (k - 4) * P:(k - 3) * P], ACT.Identity,
                                                bias=mod[:, 0, k:k + 1], scale=mod[:, 1, k:k + 1])
                last.then_inc(ht_a, 1)
            staged(act, pairs, nothing, front, nothing)

        @block.vector
        def _(dve):
            dve.sem_inc(ht_v, 2)
            dve.wait_ge(const_in, 32)

            def front(i, s):
                dve.wait_ge(tr_done, i * 2 + s + 3)
                dve.wait_ge(h_out[s], i * 16 + 16)
                for k in range(4):
                    last = nc.vector.tensor_scalar(HT[:, s, k], psT[:, s, 0, k * P:(k + 1) * P], mod[:, 1, k:k + 1],
                                                   mod[:, 0, k:k + 1], ALU.mult, ALU.add)
                last.then_inc(ht_v, 1)
            staged(dve, pairs, nothing, front, nothing)


def experts(nc, xT_d, w1, w3, w2, counts_d, ys_d):
    F = w1.shape[2]
    HU = 2
    FC = F // (HU * P)
    HB = NT
    with ExitStack() as ctx:
        m = Memory(nc, ctx, "ex")
        XT = m.sbuf("xt", [P, KD, HB * P])
        YA = m.sbuf("ya", [P, HB, D])
        W1 = m.sbuf("w1", [P, 2, KD, HU * P])
        W3 = m.sbuf("w3", [P, 2, KD, HU * P])
        W2 = m.sbuf("w2", [P, 2, HU, D])
        S = m.sbuf("s", [P, HU, P])
        A = m.sbuf("a", [P, HU, P])
        CT = m.sbuf("ct", [1, 2, NE], I32)
        psH = m.psum("psH", [P, HU, BANK])
        psY = m.psum("psY", [P, 2, BANK])
        counts_in = m.sem("counts_in")
        passed_sp, passed_pool = m.sem("passed_sp"), m.sem("passed_pool")
        w_in = [m.sem(f"w_in{s}") for s in range(2)]
        w_used = m.sem("w_used")
        x_in = m.software_sem("x_in")
        x_ready = m.sem("x_ready")
        x_used = m.sem("x_used")
        up_done = m.sem("up_done")
        s_done = m.sem("s_done")
        a_done = m.sem("a_done")
        y_done = m.sem("y_done")
        y_added = m.sem("y_added")
        stored = m.software_sem("stored")
        y_free = m.sem("y_free")
        block = ctx.enter_context(nc.Block())

        def expert(eng, e):
            nb = eng.value_load(CT[0:1, 0, bass.ds(e, 1)], min_val=2, max_val=HB)
            b0 = eng.value_load(CT[0:1, 1, bass.ds(e, 1)], min_val=0, max_val=MAXB - 2)
            return nb, b0

        def place(row):
            return (row % HB).with_bounds(min_val=0, max_val=HB - 1)

        @block.sync
        def _(sp):
            sp.dma_start(CT[:, :], counts_d).then_inc(counts_in, 16)
            w1v = w1.rearrange("e (k p) (f n) -> e f p k n", p=P, n=HU * P)
            w3v = w3.rearrange("e (k p) (f n) -> e f p k n", p=P, n=HU * P)
            w2v = w2.rearrange("e (f h p) n -> e f p h n", p=P, h=HU)
            with sp.Fori(0, NE) as e:
                with sp.Fori(0, FC // 2) as i:
                    for s in range(2):
                        f = i * 2 + s
                        sp.wait_ge(w_used, e * FC + f + 1)
                        sp.sem_inc(passed_sp, 1)
                        sp.dma_start(W1[:, s], w1v[bass.ds(e, 1), bass.ds(f, 1)].rearrange("a b p k n -> p (a b k) n")).then_inc(w_in[s], 16)
                        sp.dma_start(W3[:, s], w3v[bass.ds(e, 1), bass.ds(f, 1)].rearrange("a b p k n -> p (a b k) n")).then_inc(w_in[s], 16)
                        sp.dma_start(W2[:, s], w2v[bass.ds(e, 1), bass.ds(f, 1)].rearrange("a b p h n -> p (a b h) n")).then_inc(w_in[s], 16)

        @block.gpsimd
        def _(pool):
            pool.sem_inc(y_free, 1)
            pool.wait_ge(counts_in, 16)

            def load(e):
                nb, b0 = expert(pool, e)
                with pool.Fori(0, nb) as j:
                    row = (b0 + j).with_bounds(max_val=MAXB - 1)
                    pool.wait_ge(x_used, row + 1)
                    pool.sem_inc(passed_pool, 1)
                    pool.dma_start(XT[:, :, bass.ds(place(row) * P, P)], xT_d[:, :, bass.ds(row * P, P)]).then_inc(x_in, 16)
                pool.wait_ge(x_in, (b0 + nb) * 16)
                pool.sem_inc(x_ready, 1)

            def store(e):
                nb, b0 = expert(pool, e)
                pool.wait_ge(y_added, (b0 + nb) * (FC * 2) + 4)
                pool.sem_inc(passed_pool, 1)
                with pool.Fori(0, nb) as j:
                    row = (b0 + j).with_bounds(max_val=MAXB - 1)
                    pool.dma_start(rows(ys_d, row), YA[:, bass.ds(j, 1)].rearrange("p a n -> p (a n)")).then_inc(stored, 16)
                pool.wait_ge(stored, (b0 + nb) * 16)
                pool.sem_inc(y_free, 1)
            load(0)
            with pool.Fori(1, NE) as e:
                load(e)
                store(e - 1)
            store(NE - 1)

        def nb_last(eng):
            return eng.value_load(CT[0:1, 0, NE - 1:NE], min_val=2, max_val=HB)

        @block.tensor
        def _(pe):
            pe.sem_inc(w_used, 2)
            pe.sem_inc(y_done, 2)
            pe.sem_inc(x_used, HB)
            pe.wait_ge(counts_in, 16)

            def up(b0, s, h, j, n):
                at = pe.snap(place((b0 + j).with_bounds(max_val=MAXB - 1)) * P)
                pe.wait_ge(a_done, n * HU + h + 1)
                for q, W in enumerate((W1, W3)):
                    for k in range(KD):
                        last = nc.tensor.matmul(psH[:, h, q * P:(q + 1) * P], W[:, s, k, h * P:(h + 1) * P], XT[:, k, bass.ds(at, P)],
                                                start=k == 0, stop=k == KD - 1)
                last.then_inc(up_done, 1)

            def down(s, n, final=False):
                pe.wait_ge(a_done, n * HU + HU + 2)
                for c in range(2):
                    pe.wait_ge(y_added, n * 2 + c + 3)
                    for h in range(HU):
                        last = nc.tensor.matmul(psY[:, c], A[:, h], W2[:, s, h, c * BANK:(c + 1) * BANK], start=h == 0, stop=h == HU - 1)
                        if final and c == 0 and h == 0:
                            last.then_inc(x_used, 1)
                    last.then_inc(y_done, 1)

            with pe.Fori(0, NE) as e:
                nb, b0 = expert(pe, e)
                pe.wait_ge(x_ready, e + 1)

                def chunk(s, lo, first, final):
                    up(b0, s, 0, 0, lo)
                    if not first:
                        down(1 - s, lo - 1)
                        nc.tensor.drain().then_inc(w_used, 1)
                    up(b0, s, 1, 0, lo)
                    with pe.Fori(1, nb) as j:
                        up(b0, s, 0, j, lo + j)
                        down(s, lo + j - 1, final)
                        up(b0, s, 1, j, lo + j)

                def chunk_in(s, lo, first, count, final=False):
                    pe.wait_ge(w_in[s], count * 48)
                    chunk(s, lo, first, final)
                chunk_in(0, b0 * FC, True, e * (FC // 2) + 1)
                chunk_in(1, b0 * FC + nb, False, e * (FC // 2) + 1)
                with pe.Fori(1, FC // 2 - 1) as i:
                    lo = pe.snap(b0 * FC + nb * (i * 2), min_val=0, max_val=MAXB * FC)
                    chunk_in(0, lo, False, e * (FC // 2) + i + 1)
                    chunk_in(1, lo + nb, False, e * (FC // 2) + i + 1)
                lo = pe.snap(b0 * FC + nb * (FC - 2), min_val=0, max_val=MAXB * FC)
                chunk_in(0, lo, False, (e + 1) * (FC // 2))
                chunk_in(1, lo + nb, False, (e + 1) * (FC // 2), True)
                down(1, (b0 + nb) * FC - 1, True)
                nc.tensor.drain().then_inc(w_used, 1)

        @block.scalar
        def _(act):
            act.wait_ge(counts_in, 16)
            total = (act.value_load(CT[0:1, 1, NE - 1:NE], min_val=0, max_val=MAXB - 2) + nb_last(act)) * FC
            with act.Fori(0, total) as n:
                for h in range(HU):
                    act.wait_ge(up_done, n * HU + h + 1)
                    act.wait_ge(a_done, n * HU + h + 1)
                    nc.scalar.activation(S[:, h], psH[:, h, 0:P], ACT.Silu).then_inc(s_done, 1)

        @block.vector
        def _(dve):
            dve.sem_inc(a_done, 2)
            dve.sem_inc(y_added, 4)
            dve.wait_ge(counts_in, 16)

            def hidden0(h, n):
                dve.wait_ge(s_done, n * HU + h + 1)
                nc.vector.tensor_tensor(A[:, h], S[:, h], psH[:, h, P:2 * P], ALU.mult).then_inc(a_done, 1)

            def add(j, n, first):
                out = YA[:, bass.ds(j, 1)].rearrange("p a n -> p (a n)")
                for c in range(2):
                    dve.wait_ge(y_done, n * 2 + c + 3)
                    o = out[:, c * BANK:(c + 1) * BANK]
                    if first:
                        nc.vector.tensor_copy(o, psY[:, c]).then_inc(y_added, 1)
                    else:
                        nc.vector.tensor_tensor(o, psY[:, c], o, ALU.add).then_inc(y_added, 1)

            with dve.Fori(0, NE) as e:
                nb, b0 = expert(dve, e)

                def chunk(s, lo, first, second=False):
                    if first:
                        hidden0(0, lo)
                    else:
                        hidden_after(0, lo)
                        add(nb - 1, lo - 1, second)
                    hidden0(1, lo)
                    with dve.Fori(1, nb) as j:
                        hidden_after(0, lo + j)
                        add(j - 1, lo + j - 1, first)
                        hidden0(1, lo + j)

                def hidden_after(h, n):
                    dve.wait_ge(y_done, n * 2 + 2)
                    hidden0(h, n)
                dve.wait_ge(y_free, e + 1)
                chunk(0, b0 * FC, True)
                chunk(1, b0 * FC + nb, False, True)
                with dve.Fori(1, FC // 2) as i:
                    lo = dve.snap(b0 * FC + nb * (i * 2), min_val=0, max_val=MAXB * FC)
                    chunk(0, lo, False)
                    chunk(1, lo + nb, False)
                add(nb - 1, (b0 + nb) * FC - 1, False)


def build(nc, a, out):
    def scratch(name, shape):
        return nc.dram_tensor(name, shape, F32).ap()
    cols = scratch("cols", [2, 2, P, 2, 2, KD])
    gate = scratch("gate", [2, 2, D])
    proj = scratch("proj", [NA * P, D_IN])
    of, ob = scratch("of", [SEQ, HEADS * DV]), scratch("ob", [SEQ, HEADS * DV])
    mix = scratch("mix", [SEQ, D])
    y = [scratch(f"y{i}", [SEQ, D]) for i in range(4)]
    x = [a["x"]] + [scratch(f"x{i}", [SEQ, D]) for i in range(1, 4)] + [out]
    hT = [scratch(f"ht{i}", [P, KD, SEQ]) for i in range(3)]
    g = scratch("g", [2, SEQ, D])
    gates, picks = scratch("gates", [P, NT, NE]), scratch("picks", [P, 2, NT])
    xn, xs, ys = scratch("xn", [SEQ, D]), scratch("xs", [MAXB * P, D]), scratch("ys", [MAXB * P, D])
    xsT = scratch("xst", [P, KD, MAXB * P])
    counts = nc.dram_tensor("counts", [1, 2, NE], I32).ap()
    ident = a["ident"]

    modulation(nc, a["cc"], a["w_mod"], a["b_mod"], a["g_mix_pre"], a["g_ffn_pre"], a["g_mix_post"], a["g_ffn_post"], ident, cols, gate)
    project(nc, "ip", a["xall"], NA, cols[0, 0, :, 0], cols[0, 0, :, 1], a["e_w_in"], D_IN, proj, ident)
    gla(nc, "gb", proj, a["e_w_gate_b"], a["e_b_gate_b"], a["cum_b"], a["rest_b"], a["mask_b"], ident, ob, True)
    gla(nc, "gf", proj, a["e_w_gate_f"], a["e_b_gate_f"], a["cum_f"], a["rest_f"], a["mask_f"], ident, of, False)
    gla_finish(nc, of, ob, proj, a["e_gla_norm"], mix)
    with ExitStack() as ctx:
        m = Memory(nc, ctx, "mla")
        ckvT, krT, ckv = m.sbuf("ckvT", [P, NA * P]), m.sbuf("krT", [ROPE, NA * P]), m.sbuf("ckv", [P, NA, P])
        cqT = m.sbuf("cqT", [P, 2, NA * P])
        mla_prepare(nc, proj, a["q_norm"], a["e_kv_norm"], a["rope_tok"], ident, ckvT, krT, ckv, cqT)
        mla_attend(nc, a["e_w_uq"], a["w_uq_swapped"], a["w_ukT"], a["e_w_ukv"], a["rope_feat"], ident, ckvT, krT, ckv, cqT, mix)
    project(nc, "op", mix, NT, None, None, a["e_w_o"], D, y[0], ident)
    residual(nc, "r0", y[0], x[0], x[1], gate[0, 0], cols[0, 1, :, 0], hT[0], ident)
    swiglu(nc, "fd", hT[0], a["e_w1"], a["e_w3"], a["e_w2"], None, y[1], clear=(xs, ys))
    residual(nc, "r1", y[1], x[1], x[2], gate[0, 1], cols[1, 0, :, 0], hT[1], ident)
    fourier_channels(nc, hT[1], a["dft"], a["alt"], a["w_fold_a"], a["w_fold_b"], g)
    fourier_tokens(nc, g, a["twiddle"], y[2])
    residual(nc, "r2", y[2], x[2], x[3], gate[1, 0], cols[1, 1, :, 0], hT[2], ident, xn_d=xn)
    router(nc, hT[2], a["o_w_router"], a["iota8"], ident, gates, picks)
    with ExitStack() as ctx:
        m = Memory(nc, ctx, "moe")
        POS, GK = m.sbuf("pos", [P, 2, NT], U32), m.sbuf("gk", [P, 2, NT])
        positions(nc, gates, picks, a["tri"], a["ones"], POS, GK, counts)
        spread(nc, xn, POS, xs)
        transpose_rows(nc, xs, cols[1, 1, :, 0], xsT, ident)
        experts(nc, xsT, a["o_w1"], a["o_w3"], a["o_w2"], counts, ys)
        combine(nc, ys, POS, GK, y[3])
    residual(nc, "r3", y[3], x[3], x[4], gate[1, 1], None, None, ident)


def constants():
    f = np.float32
    c = {"ident": np.eye(P, dtype=f), "iota8": np.arange(8, dtype=f)[None], "ones": np.ones((P, P), f),
         "tri": np.triu(np.ones((P, P), f), 1)}
    half = ROPE // 2
    inv = 1.0 / (10000.0 ** (np.arange(0, half, 2, dtype=f) / f(half)))
    tok = np.arange(SEQ)
    ang = np.concatenate([(tok // GRID_W)[:, None].astype(f) * inv, (tok % GRID_W)[:, None].astype(f) * inv], -1).astype(f)
    cos, sin = np.cos(ang), np.sin(ang)
    q = half // 2
    C = np.concatenate([cos[:, :q], cos[:, :q], cos[:, q:], cos[:, q:]], 1).astype(f)
    S = np.concatenate([-sin[:, :q], sin[:, :q], -sin[:, q:], sin[:, q:]], 1).astype(f)
    c["rope_feat"] = np.ascontiguousarray(np.stack([C.T, S.T], 1))
    c["rope_tok"] = np.stack([np.concatenate([np.ones((CTX, ROPE), f), C]), np.concatenate([np.zeros((CTX, ROPE), f), S])], 1)
    j, i = np.arange(P)[:, None], np.arange(P)[None]
    same = j // 64 == i // 64
    for d, upto, after in (("f", j <= i, j > i), ("b", j >= i, j < i)):
        c[f"cum_{d}"] = (same & upto).astype(f) / f(16)
        c[f"rest_{d}"] = (same & after).astype(f) / f(16)
        c[f"mask_{d}"] = np.repeat((same & upto).astype(np.int32)[:, None], 2, 1)
    GW = D // 4
    norm = 1.0 / np.sqrt(float(SEQ * GW))
    n, m = np.arange(GW)[:, None], np.arange(P)[None]
    dft = np.stack([np.cos(2 * np.pi * (n * m % GW) / GW), np.sin(2 * np.pi * (n * m % GW) / GW)], 1) * norm
    dft[:, 1, 0] = 0.0
    c["dft"] = np.ascontiguousarray(dft.reshape(2, P, 2, P).transpose(1, 0, 2, 3)).astype(f)
    alt = np.zeros((P, KD, 4))
    for k in range(KD):
        alt[:, k, k // 2] = norm * (1 - 2 * (np.arange(P) % 2))
    c["alt"] = alt.astype(f)
    r, kk, nn = np.arange(4)[:, None, None], np.arange(SEQ // 4)[None, :, None], np.arange(SEQ // 4)[None, None]
    ang = 2 * np.pi * ((4 * kk + r) * nn % SEQ) / SEQ
    tw = np.stack([np.cos(ang), -np.sin(ang)])
    tw = tw.reshape(2, 4, 4, P, 4, P).transpose(1, 2, 5, 4, 0, 3)
    c["twiddle"] = np.ascontiguousarray(tw).astype(f)
    return c


def kernel(**inputs):
    import concourse.bacc as bacc
    from concourse.bass_utils import run_bass_kernel_spmd as run

    v = {k: np.asarray(t) for k, t in inputs.items()}
    a = {k: v[k] for k in ("w_mod", "b_mod", "g_mix_pre", "g_mix_post", "g_ffn_pre", "g_ffn_post")}
    for k in ("e_w_in", "e_w_gate_f", "e_w_gate_b", "e_w_uq", "e_w_ukv", "e_w_o", "o_w_router", "o_w1", "o_w3", "o_w2"):
        a[k] = v[k][0]
    for k in ("e_b_gate_f", "e_b_gate_b", "e_gla_norm", "e_kv_norm", "e_w1", "e_w3", "e_w2"):
        a[k] = v[k]
    a["x"] = v["x"][0]
    a["xall"] = np.concatenate([v["ctx"][0], v["x"][0]], 0)
    a["cc"] = np.stack([v["c"][0], v["c_ctx"]])
    a["q_norm"] = v["e_q_norm"].reshape(2, P).T
    swap = np.arange(ROPE).reshape(2, 2, ROPE // 4)[:, ::-1].reshape(-1)
    a["w_uq_swapped"] = v["e_w_uq"][0].reshape(QR, HEADS, NOPE + ROPE)[:, :, NOPE:][:, :, swap].reshape(QR, HEADS * ROPE)
    a["w_ukT"] = v["e_w_ukv"][0].reshape(KVR, HEADS, NOPE + DV)[:, :, :NOPE].transpose(2, 1, 0)
    wo = v["o_w_o"][0].reshape(4, D // 4, D)
    partner = np.concatenate([[P], 2 * P - np.arange(1, P)])
    a["w_fold_a"] = wo[:, :P].transpose(1, 0, 2)
    a["w_fold_b"] = wo[:, partner].transpose(1, 0, 2)
    a.update(constants())

    nc = bacc.Bacc("TRN2", target_bir_lowering=False, num_devices=1)
    arrays, aps = {}, {}
    for name, t in a.items():
        arrays[f"in_{name}"] = np.ascontiguousarray(t)
        aps[name] = nc.dram_tensor(f"in_{name}", t.shape, mybir.dt.from_np(t.dtype), kind="ExternalInput").ap()
    out = nc.dram_tensor("out", [SEQ, D], F32, kind="ExternalOutput").ap()
    build(nc, aps, out)
    r = run(nc, [arrays], core_ids=[0])
    return r.results[0]["out"].reshape(1, SEQ, D)
```
